# Optimizing a Trainium2 kernel written in Bass

```python
import math
import jax, jax.numpy as jnp
from jax import lax
import numpy as np
import jax
import jax.numpy as jnp

D_MODEL = 1024
BATCH = 1
SEQ = 512
DEPTH = 2

CHUNK = 64
Q_BLOCK = 128
HEAD_DIM = 64
N_HEADS_DIFF = 4
DIFF_V_DIM = 2 * HEAD_DIM
N_HEADS_SB = 8
N_HEADS_FOX = 8
W_DIFF = N_HEADS_DIFF * DIFF_V_DIM
W_SB = N_HEADS_SB * HEAD_DIM
W_FOX = N_HEADS_FOX * HEAD_DIM
D_MIX = W_DIFF + W_SB + W_FOX
ROT_DIM = HEAD_DIM // 4
ROPE_THETA = 500000.0
NORM_EPS = 1e-6
IN_SPLITS = [W_DIFF, W_DIFF, W_DIFF, W_DIFF,
             W_SB, W_SB, W_SB, W_SB,
             W_FOX, W_FOX, W_FOX, W_FOX,
             N_HEADS_FOX]
D_IN = sum(IN_SPLITS)


def rms_norm(x, gain):
    xf = x.astype(jnp.float32)
    y = xf * lax.rsqrt(jnp.mean(xf * xf, axis=-1, keepdims=True) + NORM_EPS)
    return (y * gain.astype(jnp.float32)).astype(x.dtype)

def rope_tables(seq):
    pos = jnp.arange(seq, dtype=jnp.float32)
    inv_freq = ROPE_THETA ** (-jnp.arange(0, ROT_DIM, 2, dtype=jnp.float32) / ROT_DIM)
    ang = pos[:, None] * inv_freq[None, :]
    return jnp.cos(ang), jnp.sin(ang)

def apply_partial_rope(t, cos, sin):
    rot, rest = t[..., :ROT_DIM], t[..., ROT_DIM:]
    r1, r2 = rot[..., :ROT_DIM // 2], rot[..., ROT_DIM // 2:]
    rot = jnp.concatenate([r1 * cos - r2 * sin, r2 * cos + r1 * sin], axis=-1).astype(t.dtype)
    return jnp.concatenate([rot, rest], axis=-1)

def diff_attention(q, k, v, lam, lambda_init, sub_gain):
    seq = q.shape[3]
    scale = q.shape[-1] ** -0.5
    chunk_id = jnp.arange(seq) // CHUNK
    outs = []
    for i in range(seq // Q_BLOCK):
        q0, q1 = i * Q_BLOCK, (i + 1) * Q_BLOCK
        s = jnp.einsum('bhcqd,bhckd->bhcqk', q[:, :, :, q0:q1], k[:, :, :, :q1]).astype(jnp.float32) * scale
        allowed = chunk_id[:q1][None, :] <= chunk_id[q0:q1][:, None]
        p = jax.nn.softmax(jnp.where(allowed, s, -jnp.inf), axis=-1)
        w = p[:, :, 0] - lam * p[:, :, 1]
        outs.append(jnp.einsum('bhqk,bhkd->bhqd', w, v[:, :, :q1].astype(jnp.float32)))
    o = jnp.concatenate(outs, axis=2)
    return rms_norm(o, sub_gain) * (1.0 - lambda_init)

def stick_breaking_attention(q, k, v):
    seq = q.shape[2]
    scale = q.shape[-1] ** -0.5
    pos = jnp.arange(seq)
    outs = []
    for i in range(seq // Q_BLOCK):
        q0, q1 = i * Q_BLOCK, (i + 1) * Q_BLOCK
        z = jnp.einsum('bhqd,bhkd->bhqk', q[:, :, q0:q1], k[:, :, :q1]).astype(jnp.float32) * scale
        strict = pos[:q1][None, :] < pos[q0:q1][:, None]
        log_keep = jnp.where(strict, jax.nn.log_sigmoid(-z), 0.0)
        log_rest = lax.cumsum(log_keep, axis=3, reverse=True) - log_keep
        a = jnp.where(strict, jnp.exp(jax.nn.log_sigmoid(z) + log_rest), 0.0)
        outs.append(jnp.einsum('bhqk,bhkd->bhqd', a, v[:, :, :q1].astype(jnp.float32)))
    return jnp.concatenate(outs, axis=2)

def forgetting_attention(q, k, v, cum_log_f):
    seq = q.shape[2]
    scale = q.shape[-1] ** -0.5
    pos = jnp.arange(seq)
    outs = []
    for i in range(seq // Q_BLOCK):
        q0, q1 = i * Q_BLOCK, (i + 1) * Q_BLOCK
        logits = jnp.einsum('bhqd,bhkd->bhqk', q[:, :, q0:q1], k[:, :, :q1]).astype(jnp.float32) * scale
        logits = logits + cum_log_f[:, :, q0:q1, None] - cum_log_f[:, :, None, :q1]
        causal = pos[:q1][None, :] <= pos[q0:q1][:, None]
        p = jax.nn.softmax(jnp.where(causal, logits, -jnp.inf), axis=-1)
        outs.append(jnp.einsum('bhqk,bhkd->bhqd', p, v[:, :, :q1].astype(jnp.float32)))
    return jnp.concatenate(outs, axis=2)

def hybrid_layer(x, w_in, f_bias, lam_vec, subln, w_out, g_pre, g_post, layer_idx, cos, sin):
    b, s, _ = x.shape
    dt = x.dtype
    h = rms_norm(x, g_pre)
    p = h @ w_in
    split_at = np.cumsum(IN_SPLITS)[:-1].tolist()
    qa, ka, va, ga, qs, ks, vs, gs, qf, kf, vf, gf, ff = jnp.split(p, split_at, axis=-1)

    def heads(t, n, d):
        return t.reshape(b, s, n, d).transpose(0, 2, 1, 3)

    def merge(t):
        return t.transpose(0, 2, 1, 3).reshape(b, s, -1).astype(dt)

    qa = apply_partial_rope(qa.reshape(b, s, N_HEADS_DIFF, 2, HEAD_DIM).transpose(0, 2, 3, 1, 4), cos, sin)
    ka = apply_partial_rope(ka.reshape(b, s, N_HEADS_DIFF, 2, HEAD_DIM).transpose(0, 2, 3, 1, 4), cos, sin)
    lambda_init = 0.8 - 0.6 * math.exp(-0.3 * layer_idx)
    lv = lam_vec.astype(jnp.float32)
    lam = jnp.exp(jnp.sum(lv[0] * lv[1])) - jnp.exp(jnp.sum(lv[2] * lv[3])) + lambda_init
    ya = merge(diff_attention(qa, ka, heads(va, N_HEADS_DIFF, DIFF_V_DIM), lam, lambda_init, subln))
    ya = ya * jax.nn.silu(ga)

    yb = merge(stick_breaking_attention(heads(qs, N_HEADS_SB, HEAD_DIM), heads(ks, N_HEADS_SB, HEAD_DIM),
                                        heads(vs, N_HEADS_SB, HEAD_DIM)))
    yb = yb * jax.nn.silu(gs)

    log_f = jax.nn.log_sigmoid((ff + f_bias).astype(jnp.float32)).transpose(0, 2, 1)
    cum_log_f = jnp.cumsum(log_f, axis=-1)
    yc = merge(forgetting_attention(heads(qf, N_HEADS_FOX, HEAD_DIM), heads(kf, N_HEADS_FOX, HEAD_DIM),
                                    heads(vf, N_HEADS_FOX, HEAD_DIM), cum_log_f))
    yc = yc * jax.nn.silu(gf)

    y = jnp.concatenate([ya, yb, yc], axis=-1) @ w_out
    return x + rms_norm(y, g_post)

def first_inputs(seed: int = 0) -> dict:
    key = jax.random.key(seed)
    ks = jax.random.split(key, 8)
    x = jax.random.normal(ks[0], (BATCH, SEQ, D_MODEL), jnp.float32)
    w_in = jax.random.normal(ks[1], (DEPTH, D_MODEL, D_IN), jnp.float32) * D_MODEL ** -0.5
    forget_bias = jax.random.uniform(ks[2], (DEPTH, N_HEADS_FOX), jnp.float32, minval=1.0, maxval=4.0)
    diff_lambda = 0.1 * jax.random.normal(ks[3], (DEPTH, 4, HEAD_DIM), jnp.float32)
    diff_subln = 1.0 + 0.02 * jax.random.normal(ks[4], (DEPTH, DIFF_V_DIM), jnp.float32)
    w_out = jax.random.normal(ks[5], (DEPTH, D_MIX, D_MODEL), jnp.float32) * D_MIX ** -0.5
    pre_norm = 1.0 + 0.02 * jax.random.normal(ks[6], (DEPTH, D_MODEL), jnp.float32)
    post_norm = 1.0 + 0.02 * jax.random.normal(ks[7], (DEPTH, D_MODEL), jnp.float32)
    return {"x": x, "w_in": w_in, "forget_bias": forget_bias, "diff_lambda": diff_lambda,
            "diff_subln": diff_subln, "w_out": w_out, "pre_norm": pre_norm, "post_norm": post_norm}

def first_block(x, w_in, forget_bias, diff_lambda, diff_subln, w_out, pre_norm, post_norm):
    cos, sin = rope_tables(x.shape[1])
    for l in range(DEPTH):
        x = hybrid_layer(x, w_in[l], forget_bias[l], diff_lambda[l], diff_subln[l], w_out[l],
                         pre_norm[l], post_norm[l], l, cos, sin)
    return x


GRID_W = 64
CTX_LEN = 256
N_MIXERS = 4
EPS = 1e-6
NEG_INF = -1e30
F32 = jnp.float32

HY_ORDER = 2
HY_SHORT = 3
HY_EMB = 33
HY_FFN = 64
HY_FAST_DECAY = 0.3
HY_SLOW_DECAY = 1.5
HY_TARGET = 1e-2
HY_SHIFT = 0.05

SW_HQ = 16
SW_HKV = 4
SW_REP = SW_HQ // SW_HKV
SW_HD = 64
SW_WINDOW = 128
SW_BLOCK = SW_WINDOW
ROPE_BASE = 10000.0

GD_H = 8
GD_DK = 128
GD_DV = 128
GD_QK = GD_H * GD_DK
GD_V = GD_H * GD_DV
GD_CONV = 3
GD_CHUNK = 64

HG_DK = 128
HG_H = D_MODEL // HG_DK
HG_DV = D_MODEL // HG_H
HG_CHUNK = 64

N_EXPERTS = 16
EXPERT_FF = 1024
EC_CAPACITY = 2


def rms_norm_2(x, w):
    xf = x.astype(F32)
    y = xf * lax.rsqrt(jnp.mean(xf * xf, axis=-1, keepdims=True) + EPS)
    return (y * w.astype(F32)).astype(x.dtype)

def l2_normalize(x):
    xf = x.astype(F32)
    return xf * lax.rsqrt(jnp.sum(xf * xf, axis=-1, keepdims=True) + EPS)

def orient(t, direction):
    return jnp.flip(t, axis=1) if direction == 1 else t

def centred_depthwise_conv(x, w, b=None):
    K, C = w.shape
    y = lax.conv_general_dilated(x, w[:, None, :].astype(x.dtype), window_strides=(1,),
                                 padding=[(K // 2, K // 2)],
                                 dimension_numbers=('NWC', 'WIO', 'NWC'), feature_group_count=C)
    return y if b is None else y + b

def hyena_positional_features(L):
    t = jnp.linspace(0.0, 1.0, L, dtype=F32)[:, None]
    bands = (HY_EMB - 1) // 2
    w = 2.0 * math.pi * jnp.arange(L, dtype=F32)[:, None] / L
    f = jnp.linspace(1e-4, bands - 1, bands, dtype=F32)[None, :]
    z = jnp.concatenate([t, jnp.cos(f * w), -jnp.sin(f * w)], axis=-1)
    return t, z

def hyena_filters(L, w1, b1, w2, b2, w3, freq):
    t, z = hyena_positional_features(L)
    h = jnp.sin(freq[0].astype(F32) * (z @ w1.astype(F32) + b1.astype(F32)))
    h = jnp.sin(freq[1].astype(F32) * (h @ w2.astype(F32) + b2.astype(F32)))
    h = (h @ w3.astype(F32)).reshape(L, HY_ORDER, 2, D_MODEL)
    max_decay = math.log(HY_TARGET) / HY_FAST_DECAY
    min_decay = math.log(HY_TARGET) / HY_SLOW_DECAY
    deltas = jnp.abs(jnp.linspace(min_decay, max_decay, D_MODEL, dtype=F32))
    window = jnp.exp(-t * deltas) + HY_SHIFT
    return h * window[:, None, None, :]

def two_sided_fft_conv(u, h_fwd, h_bwd, bias):
    L = u.shape[1]
    kern = jnp.concatenate([h_fwd, jnp.zeros((1, h_fwd.shape[1]), F32), h_bwd[:0:-1]], axis=0)
    uf = u.astype(F32)
    spec = jnp.fft.rfft(uf, n=2 * L, axis=1) * jnp.fft.rfft(kern, n=2 * L, axis=0)[None]
    y = jnp.fft.irfft(spec, n=2 * L, axis=1)[:, :L]
    return (y + uf * bias.astype(F32)).astype(u.dtype)

def hyena_mixer(h, w_in, b_in, short_w, short_b, w1, b1, w2, b2, w3, freq, filt_bias, w_out, b_out):
    L = h.shape[1]
    u = centred_depthwise_conv(h @ w_in + b_in, short_w, short_b)
    v, x1, x2 = jnp.split(u, 3, axis=-1)
    filt = hyena_filters(L, w1, b1, w2, b2, w3, freq)
    z = x1 * two_sided_fft_conv(v, filt[:, 0, 0], filt[:, 0, 1], filt_bias[0])
    z = x2 * two_sided_fft_conv(z, filt[:, 1, 0], filt[:, 1, 1], filt_bias[1])
    return z @ w_out + b_out

def axial_rope_tables(L):
    rows = L // GRID_W
    row = jnp.repeat(jnp.arange(rows, dtype=F32), GRID_W)
    col = jnp.tile(jnp.arange(GRID_W, dtype=F32), rows)
    nf = SW_HD // 4
    inv = ROPE_BASE ** (-jnp.arange(nf, dtype=F32) / nf)
    ang = jnp.concatenate([row[:, None] * inv, col[:, None] * inv], axis=-1)
    return jnp.cos(ang), jnp.sin(ang)

def apply_rope(x, cos, sin):
    shape = (1, cos.shape[0]) + (1,) * (x.ndim - 3) + (cos.shape[1],)
    cos = cos.reshape(shape).astype(x.dtype)
    sin = sin.reshape(shape).astype(x.dtype)
    x1, x2 = jnp.split(x, 2, axis=-1)
    return jnp.concatenate([x1 * cos - x2 * sin, x2 * cos + x1 * sin], axis=-1)

def sink_softmax(s, sink):
    sk = jnp.broadcast_to(sink.astype(F32).reshape(SW_HKV, SW_REP, 1, 1), s.shape[:-1] + (1,))
    return jax.nn.softmax(jnp.concatenate([s, sk], axis=-1), axis=-1)[..., :-1]

def swa_mixer(h_ctx, h_lat, w_in, sink, w_out, with_ctx_out):
    B, L, _ = h_lat.shape
    scale = SW_HD ** -0.5

    def project(h):
        n = h.shape[1]
        u = h @ w_in
        q = u[..., :SW_HQ * SW_HD].reshape(B, n, SW_HKV, SW_REP, SW_HD)
        k = u[..., SW_HQ * SW_HD:(SW_HQ + SW_HKV) * SW_HD].reshape(B, n, SW_HKV, SW_HD)
        v = u[..., (SW_HQ + SW_HKV) * SW_HD:].reshape(B, n, SW_HKV, SW_HD)
        return q, k, v

    q_c, k_c, v_c = project(h_ctx)
    q_l, k_l, v_l = project(h_lat)
    cos, sin = axial_rope_tables(L)
    q_l = apply_rope(q_l, cos, sin)
    k_l = apply_rope(k_l, cos, sin)
    n_ctx = k_c.shape[1]
    nb = L // SW_BLOCK

    def band(t):
        tp = jnp.pad(t, ((0, 0), (SW_BLOCK, SW_BLOCK), (0, 0), (0, 0)))
        tp = tp.reshape(B, nb + 2, SW_BLOCK, SW_HKV, SW_HD)
        return jnp.concatenate([tp[:, :-2], tp[:, 1:-1], tp[:, 2:]], axis=2).swapaxes(0, 1)

    blk = jnp.arange(nb)[:, None, None]
    qpos = blk * SW_BLOCK + jnp.arange(SW_BLOCK)[None, :, None]
    kpos = (blk - 1) * SW_BLOCK + jnp.arange(3 * SW_BLOCK)[None, None, :]
    band_mask = (jnp.abs(qpos - kpos) <= SW_WINDOW) & (kpos >= 0) & (kpos < L)
    q_blocks = q_l.reshape(B, nb, SW_BLOCK, SW_HKV, SW_REP, SW_HD).swapaxes(0, 1)

    def block_attention(xs):
        q_b, k_b, v_b, m_b = xs
        s_ctx = jnp.einsum('bqgrd,bkgd->bgrqk', q_b, k_c).astype(F32) * scale
        s_loc = jnp.einsum('bqgrd,bkgd->bgrqk', q_b, k_b).astype(F32) * scale
        s_loc = jnp.where(m_b, s_loc, NEG_INF)
        p = sink_softmax(jnp.concatenate([s_ctx, s_loc], axis=-1), sink).astype(v_b.dtype)
        return (jnp.einsum('bgrqk,bkgd->bqgrd', p[..., :n_ctx], v_c)
                + jnp.einsum('bgrqk,bkgd->bqgrd', p[..., n_ctx:], v_b))

    o_l = lax.map(block_attention, (q_blocks, band(k_l), band(v_l), band_mask))
    y_lat = o_l.swapaxes(0, 1).reshape(B, L, SW_HQ * SW_HD) @ w_out
    y_ctx = None
    if with_ctx_out:
        s = jnp.einsum('bqgrd,bkgd->bgrqk', q_c, k_c).astype(F32) * scale
        p = sink_softmax(s, sink).astype(v_c.dtype)
        y_ctx = jnp.einsum('bgrqk,bkgd->bqgrd', p, v_c).reshape(B, n_ctx, SW_HQ * SW_HD) @ w_out
    return y_ctx, y_lat

def to_chunks(t, size):
    B, L, H = t.shape[:3]
    t = t.reshape((B, L // size, size, H) + t.shape[3:])
    return jnp.moveaxis(t, (1, 3), (0, 2))

def from_chunks(t):
    t = jnp.moveaxis(t, (0, 2), (1, 3))
    return t.reshape((t.shape[0], t.shape[1] * t.shape[2]) + t.shape[3:])

def chunk_gated_delta(q, k, v, g, beta, S0):
    dv = v.shape[-1]
    C = GD_CHUNK
    qc, kc, vc = to_chunks(q, C), to_chunks(k, C), to_chunks(v, C)
    gc, bc = to_chunks(g, C), to_chunks(beta, C)
    G = jnp.cumsum(gc, axis=-1)
    incl = jnp.tril(jnp.ones((C, C), bool))
    strict = jnp.tril(jnp.ones((C, C), bool), -1)
    decay = jnp.exp(jnp.where(incl, G[..., :, None] - G[..., None, :], -jnp.inf))
    kb = kc * bc[..., None]
    A = jnp.where(strict, jnp.einsum('nbhid,nbhjd->nbhij', kb, kc) * decay, 0.0)
    rhs = jnp.concatenate([vc * bc[..., None], kb * jnp.exp(G)[..., None]], axis=-1)
    uw = lax.linalg.triangular_solve(jnp.eye(C, dtype=F32) + A, rhs, left_side=True, lower=True,
                                     unit_diagonal=True)
    u, w = uw[..., :dv], uw[..., dv:]

    def step(S, xs):
        q_i, k_i, u_i, w_i, G_i, dec_i = xs
        v_new = u_i - jnp.einsum('bhck,bhkv->bhcv', w_i, S)
        attn = jnp.einsum('bhik,bhjk->bhij', q_i, k_i) * dec_i
        o = (jnp.einsum('bhck,bhkv->bhcv', q_i * jnp.exp(G_i)[..., None], S)
             + jnp.einsum('bhij,bhjv->bhiv', attn, v_new))
        g_last = G_i[..., -1:]
        S = (S * jnp.exp(g_last)[..., None]
             + jnp.einsum('bhck,bhcv->bhkv', k_i * jnp.exp(g_last - G_i)[..., None], v_new))
        return S, o

    S, o = lax.scan(step, S0, (qc, kc, u, w, G, decay))
    return from_chunks(o), S

def chunk_gla(q, k, v, logf, S0):
    C = HG_CHUNK
    qc, kc, vc, gc = to_chunks(q, C), to_chunks(k, C), to_chunks(v, C), to_chunks(logf, C)
    G = jnp.cumsum(gc, axis=-2)
    incl = jnp.tril(jnp.ones((C, C), bool))[:, :, None]

    def step(S, xs):
        q_i, k_i, v_i, G_i = xs
        dec = jnp.exp(jnp.where(incl, G_i[:, :, :, None, :] - G_i[:, :, None, :, :], -jnp.inf))
        attn = jnp.einsum('bhtk,bhtsk->bhts', q_i, dec * k_i[:, :, None, :, :])
        o = (jnp.einsum('bhtk,bhkv->bhtv', q_i * jnp.exp(G_i), S)
             + jnp.einsum('bhts,bhsv->bhtv', attn, v_i))
        g_last = G_i[:, :, -1:, :]
        S = (S * jnp.exp(g_last[:, :, 0, :])[..., None]
             + jnp.einsum('bhsk,bhsv->bhkv', k_i * jnp.exp(g_last - G_i), v_i))
        return S, o

    S, o = lax.scan(step, S0, (qc, kc, vc, G))
    return from_chunks(o), S

def gdn_mixer(h_ctx, h_lat, w_in, conv_w, a_log, dt_bias, norm_w, w_out, with_ctx_out):
    n_qkv = 2 * GD_QK + GD_V

    def project(h):
        B, n, _ = h.shape
        u = h @ w_in
        qkv = jax.nn.silu(centred_depthwise_conv(u[..., :n_qkv], conv_w))
        q = l2_normalize(qkv[..., :GD_QK].reshape(B, n, GD_H, GD_DK)) * GD_DK ** -0.5
        k = l2_normalize(qkv[..., GD_QK:2 * GD_QK].reshape(B, n, GD_H, GD_DK))
        v = qkv[..., 2 * GD_QK:].astype(F32).reshape(B, n, GD_H, GD_DV)
        z = u[..., n_qkv:n_qkv + GD_V]
        ba = u[..., n_qkv + GD_V:].astype(F32).reshape(B, n, 2, 2, GD_H)
        beta = jax.nn.sigmoid(ba[:, :, 0])
        g = -jnp.exp(a_log.astype(F32)) * jax.nn.softplus(ba[:, :, 1] + dt_bias.astype(F32))
        return q, k, v, z, beta, g

    qc, kc, vc, zc, bc, gc = project(h_ctx)
    ql, kl, vl, zl, bl, gl = project(h_lat)
    S0 = jnp.zeros((h_lat.shape[0], GD_H, GD_DK, GD_DV), F32)
    o_c = 0.0
    o_l = 0.0
    for d in range(2):
        oc_d, S_c = chunk_gated_delta(orient(qc, d), orient(kc, d), orient(vc, d),
                                      orient(gc[:, :, d], d), orient(bc[:, :, d], d), S0)
        ol_d, _ = chunk_gated_delta(orient(ql, d), orient(kl, d), orient(vl, d),
                                    orient(gl[:, :, d], d), orient(bl[:, :, d], d), S_c)
        o_c = o_c + orient(oc_d, d)
        o_l = o_l + orient(ol_d, d)

    def readout(o, z):
        B, n = o.shape[:2]
        y = rms_norm_2(o, norm_w) * jax.nn.silu(z.astype(F32)).reshape(B, n, GD_H, GD_DV)
        return y.reshape(B, n, GD_V).astype(z.dtype) @ w_out

    y_ctx = readout(o_c, zc) if with_ctx_out else None
    return y_ctx, readout(o_l, zl)

def hgrn2_mixer(h_ctx, h_lat, w_in, lb, norm_w, w_out, with_ctx_out):
    lbh = lb.reshape(HG_H, HG_DK)

    def project(h):
        B, n, _ = h.shape
        q, f_fw, f_bw, i, g = jnp.split(h @ w_in, 5, axis=-1)
        q = jax.nn.silu(q).astype(F32).reshape(B, n, HG_H, HG_DK)
        f = jnp.stack([f_fw, f_bw], axis=2).astype(F32).reshape(B, n, 2, HG_H, HG_DK)
        logf = jnp.log(lbh + (1.0 - lbh) * jax.nn.sigmoid(f))
        k = (1.0 - lbh) * jax.nn.sigmoid(-f)
        v = i.astype(F32).reshape(B, n, HG_H, HG_DV)
        return q, k, v, logf, g

    qc, kc, vc, fc, gc = project(h_ctx)
    ql, kl, vl, fl, gl = project(h_lat)
    S0 = jnp.zeros((h_lat.shape[0], HG_H, HG_DK, HG_DV), F32)
    o_c = 0.0
    o_l = 0.0
    for d in range(2):
        oc_d, S_c = chunk_gla(orient(qc, d), orient(kc[:, :, d], d), orient(vc, d),
                              orient(fc[:, :, d], d), S0)
        ol_d, _ = chunk_gla(orient(ql, d), orient(kl[:, :, d], d), orient(vl, d),
                            orient(fl[:, :, d], d), S_c)
        o_c = o_c + orient(oc_d, d)
        o_l = o_l + orient(ol_d, d)

    def readout(o, g):
        B, n = o.shape[:2]
        y = rms_norm_2(o, norm_w) * jax.nn.silu(g.astype(F32)).reshape(B, n, HG_H, HG_DV)
        return y.reshape(B, n, D_MODEL).astype(g.dtype) @ w_out

    y_ctx = readout(o_c, gc) if with_ctx_out else None
    return y_ctx, readout(o_l, gl)

def expert_choice_ffn(h, router_w, w_gate, w_up, w_down):
    B, n, D = h.shape
    cap = EC_CAPACITY * n // N_EXPERTS
    aff = jax.nn.softmax((h @ router_w).astype(F32), axis=-1)
    gate, idx = lax.top_k(jnp.swapaxes(aff, 1, 2), cap)
    xe = jax.vmap(lambda hb, ib: hb[ib])(h, idx)
    a = jnp.einsum('becd,edf->becf', xe, w_gate)
    u = jnp.einsum('becd,edf->becf', xe, w_up)
    ye = jnp.einsum('becf,efd->becd', jax.nn.silu(a) * u, w_down) * gate[..., None].astype(h.dtype)
    return jax.vmap(lambda ib, yb: jnp.zeros((n, D), h.dtype).at[ib.reshape(-1)].add(yb.reshape(-1, D)))(idx, ye)

def second_inputs(seed: int = 0) -> dict:
    key = jax.random.key(seed)
    keys = iter(jax.random.split(key, 48))

    def nrm(shape, std):
        return std * jax.random.normal(next(keys), shape, F32)

    def gain(shape):
        return 1.0 + nrm(shape, 0.02)

    D = D_MODEL
    gd_cols = 2 * GD_QK + 2 * GD_V + 4 * GD_H
    gd_a_log = jnp.log(jax.random.uniform(next(keys), (2, GD_H), F32, 1.0, 16.0))
    dt = jnp.exp(jax.random.uniform(next(keys), (2, GD_H), F32, math.log(1e-3), math.log(1e-1)))
    gd_dt_bias = jnp.log(jnp.expm1(dt))
    return {
        'x': nrm((BATCH, SEQ, D), 1.0),
        'c': nrm((BATCH, D), 1.0),
        'ctx': nrm((BATCH, CTX_LEN, D), 1.0),
        'c_ctx': nrm((D,), 1.0),
        'ada_w': nrm((DEPTH, D, 6 * D), 0.5 * D ** -0.5),
        'ada_b': nrm((DEPTH, 6 * D), 0.02),
        'norm1_w': gain((DEPTH, D)),
        'norm2_w': gain((DEPTH, D)),
        'final_norm_w': gain((D,)),
        'hy_w_in': nrm((D, 3 * D), D ** -0.5),
        'hy_b_in': nrm((3 * D,), 0.02),
        'hy_short_w': nrm((HY_SHORT, 3 * D), HY_SHORT ** -0.5),
        'hy_short_b': nrm((3 * D,), 0.02),
        'hy_ffn_w1': nrm((HY_EMB, HY_FFN), HY_EMB ** -0.5),
        'hy_ffn_b1': nrm((HY_FFN,), 0.02),
        'hy_ffn_w2': nrm((HY_FFN, HY_FFN), HY_FFN ** -0.5),
        'hy_ffn_b2': nrm((HY_FFN,), 0.02),
        'hy_ffn_w3': nrm((HY_FFN, HY_ORDER * 2 * D), 0.01),
        'hy_sin_freq': gain((2, HY_FFN)),
        'hy_filter_bias': nrm((HY_ORDER, D), 0.5),
        'hy_w_out': nrm((D, D), D ** -0.5),
        'hy_b_out': nrm((D,), 0.02),
        'sw_w_in': nrm((D, (SW_HQ + 2 * SW_HKV) * SW_HD), D ** -0.5),
        'sw_sink': nrm((SW_HQ,), 0.5),
        'sw_w_out': nrm((SW_HQ * SW_HD, D), (SW_HQ * SW_HD) ** -0.5),
        'gd_w_in': nrm((D, gd_cols), D ** -0.5),
        'gd_conv_w': nrm((GD_CONV, 2 * GD_QK + GD_V), GD_CONV ** -0.5),
        'gd_a_log': gd_a_log,
        'gd_dt_bias': gd_dt_bias,
        'gd_norm_w': gain((GD_DV,)),
        'gd_w_out': nrm((GD_V, D), GD_V ** -0.5),
        'hg_w_in': nrm((D, 5 * D), D ** -0.5),
        'hg_lb': nrm((DEPTH, D), 1.0),
        'hg_norm_w': gain((HG_DV,)),
        'hg_w_out': nrm((D, D), D ** -0.5),
        'moe_router': nrm((DEPTH, D, N_EXPERTS), D ** -0.5),
        'moe_w_gate': nrm((DEPTH, N_EXPERTS, D, EXPERT_FF), D ** -0.5),
        'moe_w_up': nrm((DEPTH, N_EXPERTS, D, EXPERT_FF), D ** -0.5),
        'moe_w_down': nrm((DEPTH, N_EXPERTS, EXPERT_FF, D), EXPERT_FF ** -0.5),
    }

def second_block(x, c, ctx, c_ctx, ada_w, ada_b, norm1_w, norm2_w, final_norm_w,
              hy_w_in, hy_b_in, hy_short_w, hy_short_b, hy_ffn_w1, hy_ffn_b1, hy_ffn_w2, hy_ffn_b2,
              hy_ffn_w3, hy_sin_freq, hy_filter_bias, hy_w_out, hy_b_out,
              sw_w_in, sw_sink, sw_w_out,
              gd_w_in, gd_conv_w, gd_a_log, gd_dt_bias, gd_norm_w, gd_w_out,
              hg_w_in, hg_lb, hg_norm_w, hg_w_out,
              moe_router, moe_w_gate, moe_w_up, moe_w_down):
    lat, cx = x, ctx
    lb_all = jnp.cumsum(jax.nn.softmax(hg_lb.astype(F32), axis=0), axis=0)
    for layer in range(DEPTH):
        kind = layer % N_MIXERS
        keep_ctx = layer < DEPTH - 1
        mod_l = [m[:, None, :] for m in jnp.split(jax.nn.silu(c) @ ada_w[layer] + ada_b[layer], 6, axis=-1)]
        mod_c = jnp.split(jax.nn.silu(c_ctx) @ ada_w[layer] + ada_b[layer], 6, axis=-1)
        h_l = rms_norm_2(lat, norm1_w[layer]) * (1.0 + mod_l[1]) + mod_l[0]
        h_c = rms_norm_2(cx, norm1_w[layer]) * (1.0 + mod_c[1]) + mod_c[0]
        if kind == 0:
            hy_args = (hy_w_in, hy_b_in, hy_short_w, hy_short_b, hy_ffn_w1, hy_ffn_b1, hy_ffn_w2,
                       hy_ffn_b2, hy_ffn_w3, hy_sin_freq, hy_filter_bias, hy_w_out, hy_b_out)
            y_l = hyena_mixer(h_l, *hy_args)
            y_c = hyena_mixer(h_c, *hy_args) if keep_ctx else None
        elif kind == 1:
            y_c, y_l = swa_mixer(h_c, h_l, sw_w_in, sw_sink, sw_w_out, keep_ctx)
        elif kind == 2:
            y_c, y_l = gdn_mixer(h_c, h_l, gd_w_in, gd_conv_w, gd_a_log, gd_dt_bias, gd_norm_w,
                                 gd_w_out, keep_ctx)
        else:
            lb = lb_all[layer] - lb_all[0]
            y_c, y_l = hgrn2_mixer(h_c, h_l, hg_w_in, lb, hg_norm_w, hg_w_out, keep_ctx)
        lat = lat + mod_l[2] * y_l
        h_l = rms_norm_2(lat, norm2_w[layer]) * (1.0 + mod_l[4]) + mod_l[3]
        lat = lat + mod_l[5] * expert_choice_ffn(h_l, moe_router[layer], moe_w_gate[layer],
                                                 moe_w_up[layer], moe_w_down[layer])
        if keep_ctx:
            cx = cx + mod_c[2] * y_c
            h_c = rms_norm_2(cx, norm2_w[layer]) * (1.0 + mod_c[4]) + mod_c[3]
            cx = cx + mod_c[5] * expert_choice_ffn(h_c, moe_router[layer], moe_w_gate[layer],
                                                   moe_w_up[layer], moe_w_down[layer])
    return rms_norm_2(lat, final_norm_w)


def setup_inputs(seed=0):
    out = dict(first_inputs(seed))
    for name, value in second_inputs(seed + 1).items():
        if name != "x":
            out[name + "_2"] = value
    return out


def reference(
    x, w_in, forget_bias, diff_lambda, diff_subln, w_out, pre_norm, post_norm, c_2, ctx_2,
    c_ctx_2, ada_w_2, ada_b_2, norm1_w_2, norm2_w_2, final_norm_w_2, hy_w_in_2, hy_b_in_2,
    hy_short_w_2, hy_short_b_2, hy_ffn_w1_2, hy_ffn_b1_2, hy_ffn_w2_2, hy_ffn_b2_2, hy_ffn_w3_2,
    hy_sin_freq_2, hy_filter_bias_2, hy_w_out_2, hy_b_out_2, sw_w_in_2, sw_sink_2, sw_w_out_2,
    gd_w_in_2, gd_conv_w_2, gd_a_log_2, gd_dt_bias_2, gd_norm_w_2, gd_w_out_2, hg_w_in_2,
    hg_lb_2, hg_norm_w_2, hg_w_out_2, moe_router_2, moe_w_gate_2, moe_w_up_2, moe_w_down_2,
):
    x = first_block(
        x, w_in, forget_bias, diff_lambda, diff_subln, w_out, pre_norm, post_norm,
    )
    return second_block(
        x, c_2, ctx_2, c_ctx_2, ada_w_2, ada_b_2, norm1_w_2, norm2_w_2, final_norm_w_2,
        hy_w_in_2, hy_b_in_2, hy_short_w_2, hy_short_b_2, hy_ffn_w1_2, hy_ffn_b1_2, hy_ffn_w2_2,
        hy_ffn_b2_2, hy_ffn_w3_2, hy_sin_freq_2, hy_filter_bias_2, hy_w_out_2, hy_b_out_2,
        sw_w_in_2, sw_sink_2, sw_w_out_2, gd_w_in_2, gd_conv_w_2, gd_a_log_2, gd_dt_bias_2,
        gd_norm_w_2, gd_w_out_2, hg_w_in_2, hg_lb_2, hg_norm_w_2, hg_w_out_2, moe_router_2,
        moe_w_gate_2, moe_w_up_2, moe_w_down_2,
    )


_drawn_inputs = setup_inputs


def setup_inputs(seed=0):
    import zlib

    import numpy as np

    out = dict(_drawn_inputs(seed))
    spreads = {}
    factors = {'diff_subln': 3.566,
     'ctx_2': 4.753,
     'ada_b_2': 3.944,
     'norm1_w_2': 8.0,
     'norm2_w_2': 39.707,
     'final_norm_w_2': 8.675,
     'hy_b_in_2': 7.938,
     'hy_short_b_2': 7.566,
     'hy_ffn_b1_2': 5.915,
     'hy_ffn_b2_2': 4.331,
     'hy_sin_freq_2': 8.0,
     'hy_b_out_2': 64.0,
     'sw_sink_2': 8.0}
    for name, (base, spread) in spreads.items():
        noise = np.random.default_rng([zlib.crc32(name.encode()), seed]).standard_normal(out[name].shape)
        drawn = base * np.exp(spread * noise) if base else spread * noise
        out[name] = jnp.asarray(drawn.astype(out[name].dtype))
    for name, factor in factors.items():
        out[name] = (out[name] * factor).astype(out[name].dtype)
    return out
```

```python
from contextlib import ExitStack
import math

import numpy as np
import concourse.bass as bass
from concourse import mybir

F32 = mybir.dt.float32
ALU = mybir.AluOpType
ACT = mybir.ActivationFunctionType
AX_X = mybir.AxisListType.X

P = 128
D = 1024
KD = D // P
T = 512
TC = 256
DEPTH = 2
HD = 64
NQ = T // P
EPS = 1e-6
NEG = -1e30
N_EXP = 16
CAP_L = 2 * T // N_EXP
CAP_C = 2 * TC // N_EXP
TWO_PI = 2 * math.pi

WSLOTS = 3
WCH = 4096

LAYER_COLS = {}
GLOBAL_COLS = {}


def _cols(table, spec):
    at = 0
    for name, n in spec:
        table[name] = (at, n)
        at += n
    return at


N_LV = _cols(LAYER_COLS, [("g_pre", KD), ("g_post", KD), ("subln", 1), ("lam_vec", 4), ("f_bias", 1),
                          ("lam_init", 1), ("one_minus", 1)])
N_GV = _cols(GLOBAL_COLS, [("c", 2 * KD), ("ada_b", 2 * 48), ("norm1", 2 * KD), ("norm2", 2 * KD), ("final", KD),
                           ("hy_b_in", 24), ("hy_sw", 72), ("hy_sb", 24), ("hy_b_out", KD),
                           ("ffn_b1", 1), ("ffn_b2", 1), ("freq", 2), ("sink", 16),
                           ("not0", 1), ("is0", 1), ("dft_l", 2), ("dft_c", 2)])


def shape_constants():
    c = {}
    c["ident"] = np.eye(P, dtype=np.float32)
    i, j = np.arange(P)[:, None], np.arange(P)[None, :]
    m = lambda ok: np.where(ok, 0.0, NEG).astype(np.float32)
    c["masks"] = np.concatenate([m(j // 64 <= i // 64), m(j < i), m(j <= i), m(j >= i)], axis=1)
    inv = np.float32(500000.0) ** (-np.arange(0, 16, 2, dtype=np.float32) / np.float32(16))
    ang = (np.arange(T, dtype=np.float32)[:, None] * inv[None, :]).astype(np.float32)
    cos, sin = np.cos(ang).T, np.sin(ang).T
    rc, rs = np.ones((64, T), np.float32), np.zeros((64, T), np.float32)
    rc[0:8], rc[8:16], rs[0:8], rs[8:16] = cos, cos, -sin, sin
    perm = np.zeros((64, 64), np.float32)
    for a in range(8):
        perm[a, a + 8] = perm[a + 8, a] = 1
    two = lambda a: np.concatenate([a, a], axis=0)
    blk = lambda a: np.block([[a, np.zeros_like(a)], [np.zeros_like(a), a]]).astype(np.float32)
    c["rope"] = np.concatenate([two(rc), two(rs), blk(perm)], axis=1)
    row = np.repeat(np.arange(T // 64, dtype=np.float32), 64)
    col = np.tile(np.arange(64, dtype=np.float32), T // 64)
    inv = np.float32(10000.0) ** (-np.arange(16, dtype=np.float32) / np.float32(16))
    ang = np.concatenate([row[:, None] * inv, col[:, None] * inv], axis=-1).astype(np.float32)
    cos, sin = np.cos(ang).T, np.sin(ang).T
    perm = np.zeros((64, 64), np.float32)
    for a in range(32):
        perm[a, a + 32] = perm[a + 32, a] = 1
    c["axial"] = np.concatenate([two(np.concatenate([cos, cos])), two(np.concatenate([-sin, sin])), blk(perm)],
                                axis=1).astype(np.float32)
    f = np.arange(T)
    th = 2 * np.pi * ((f[:, None] * f[None, :]) % (2 * T)) / (2 * T)
    tiled = lambda a: a.reshape(-1, P, a.shape[1]).transpose(1, 0, 2).reshape(P, -1)
    c["dft"] = np.concatenate([tiled(np.cos(th)), tiled(-np.sin(th))], axis=1).astype(np.float32)
    for n, L in (("l", T), ("c", TC)):
        t = np.arange(L)
        g = np.arange(P)
        th = 2 * np.pi * ((t[:, None] * g[None, :]) % (2 * L)) / (2 * L)
        fw = -np.sin(th)
        fw[:, 0] = np.where(t % 2, -1.0, 1.0)
        ny = np.zeros((L, P))
        ny[:, 0] = 2 * fw[:, 0]
        c[f"fs0_{n}"] = tiled(fw).astype(np.float32)
        c[f"gs0_{n}"] = np.ascontiguousarray(fw.T).astype(np.float32)
        c[f"nyq_{n}"] = tiled(ny).astype(np.float32)
        tt = np.linspace(0.0, 1.0, L, dtype=np.float32)[:, None]
        w = (np.float32(2.0 * math.pi) * np.arange(L, dtype=np.float32)[:, None] / np.float32(L)).astype(np.float32)
        fr = np.linspace(1e-4, 15, 16, dtype=np.float32)[None, :]
        fw_ = (fr * w).astype(np.float32)
        z = np.concatenate([tt, np.cos(fw_), -np.sin(fw_)], axis=-1)
        c[f"pos_{n}"] = np.ascontiguousarray(z.T).astype(np.float32)
        deltas = np.abs(np.linspace(math.log(1e-2) / 1.5, math.log(1e-2) / 0.3, D, dtype=np.float32))
        c[f"win_{n}"] = (np.exp(-tt * deltas) + np.float32(0.05)).astype(np.float32)
    c["iota"] = np.broadcast_to(np.arange(CAP_L, dtype=np.float32), (P, CAP_L)).copy()
    return c


class Map:
    def __init__(self, at=0):
        self.at = at

    def take(self, n):
        a = self.at
        self.at += n
        return a


class Engine:

    def __init__(self, e, name, sems):
        self.e, self.name, self.sems = e, name, sems
        self.counts = {}
        self.last = None
        self.phase = 0
        self.loop = None

    def mark(self, sem=None):
        sem = sem or f"{self.name}_step"
        self.counts[sem] = self.counts.get(sem, 0) + 1
        self.last = (self.sems[sem], self.counts[sem])
        return self.sems[sem]

    def opened(self):
        self.phase += 1
        self.counts = {}
        self.last = None
        return self.phase if self.loop is None else self.loop[0] * self.loop[1] + self.phase

    def leave(self, turns):
        self.phase += self.loop[1] * (turns - 1)
        self.loop = None


def end_phase(A):
    if A.last:
        A.e.wait_ge(*A.last)
    A.e.sem_inc(A.sems["arrived"], 1)
    A.e.wait_ge(A.sems["phase_open"], A.opened())
    A.e.sem_inc(A.sems["resumed"], 1)


def open_next_phase(A):
    A.e.wait_ge(A.sems["arrived"], 3)
    first, last = A.sems["_range"]
    A.e.sem_clear(range(first, last + 1))
    A.e.sem_inc(A.sems["phase_open"], 1)


def nth(who, t):
    return sum(1 for x in who[:t + 1] if x == who[t])


PHASE_SEMS = ["arrived", "pe_step", "act_step", "dve_step", "pool_step",
              "const_in", "const2_in", "psum_full", "act_out", "dve_out", "squares", "stat", "rstd", "h_ready",
              "scores", "maxima", "probs", "weights", "turned", "turned_out", "o_full", "o_out",
              "a_ready", "b_ready", "c_ready", "d_ready", "e_ready", "f_ready", "g_ready",
              "i_ready", "j_ready", "k_ready", "m_ready", "n_ready"]


def build(nc, a, out):
    with ExitStack() as ctx:
        S = {}
        S["phase_open"] = ctx.enter_context(nc.semaphore("phase_open"))
        S["resumed"] = ctx.enter_context(nc.semaphore("resumed"))
        for i in range(WSLOTS):
            S[f"w_in{i}"] = ctx.enter_context(nc.semaphore(f"w_in{i}"))
        S["w_used"] = ctx.enter_context(nc.semaphore("w_used"))
        S["ff_in"] = ctx.enter_context(nc.semaphore("ff_in"))
        S["stored"] = ctx.enter_context(nc.semaphore("stored"))
        nums = []
        for n in PHASE_SEMS:
            S[n] = ctx.enter_context(nc.semaphore(n))
            nums.append(S[n].num)
        assert max(nums) - min(nums) == len(nums) - 1
        S["_range"] = (min(nums), max(nums))

        total = Map()
        XT_, CT_, HT_, W_ = total.take(KD * T), total.take(KD * TC), total.take(KD * (T + TC)), total.take(WSLOTS * WCH)
        ID_, ON_, GV_, LV_, LS_, MOD_ = (total.take(P), total.take(P), total.take(N_GV), total.take(N_LV),
                                         total.take(DEPTH * N_LV), total.take(2 * 96))
        MISC_ = total.take(96)
        AR_ = total.at
        AR_END = 53150
        M = ctx.enter_context(nc.sbuf_tensor("mem", [P, AR_END], F32))
        ps = ctx.enter_context(nc.psum_tensor("ps", [P, 8, 512], F32))

        def v(at, *dims, p=P, p0=0):
            n = int(np.prod(dims))
            x = M[p0:p0 + p, at:at + n]
            if len(dims) == 2:
                x = x.rearrange("p (a b) -> p a b", b=dims[1])
            if len(dims) == 3:
                x = x.rearrange("p (a b c) -> p a b c", b=dims[1], c=dims[2])
            return x

        XT, CT, HT = v(XT_, KD, T), v(CT_, KD, TC), v(HT_, KD, T + TC)
        HTL = v(HT_, KD, T)
        Wc = [v(W_ + i * WCH, KD, 512) for i in range(WSLOTS)]
        Wr = [v(W_ + i * WCH, 4, 1024) for i in range(WSLOTS)]
        IDENT, ONES = v(ID_, P), v(ON_, P)
        MISC = v(MISC_, 96)

        def gv(name, i=0, n=1, p=P):
            at = GV_ + GLOBAL_COLS[name][0] + i
            return M[0:p, at:at + n]

        def lv(name, i=0, n=1, p=P):
            at = LV_ + LAYER_COLS[name][0] + i
            return M[0:p, at:at + n]

        def mod(layer, which, k, side):
            at = MOD_ + layer * 96 + (which * KD + k) * 2 + side
            return M[:, at:at + 1]

        block = ctx.enter_context(nc.Block())
        eps_col = MISC[:, 0:1]
        one_col = MISC[:, 1:2]
        mm = nc.tensor.matmul
        tr = nc.tensor.transpose
        act = nc.scalar.activation
        tt, ts, stt = nc.vector.tensor_tensor, nc.vector.tensor_scalar, nc.vector.scalar_tensor_tensor

        class Stream:

            def __init__(self, e):
                self.e, self.n, self.loop = e, 0, None

            def number(self, extra=0):
                if self.loop is None:
                    return self.n + extra
                reg, per = self.loop
                return reg * per + (self.n + extra)

            def enter(self, reg, per):
                assert per % WSLOTS == 0
                self.loop = (reg, per)

            def leave(self, turns):
                per = self.loop[1]
                self.loop = None
                self.n += per * (turns - 1)

            def load(self, src, dst=None, first=False):
                s = self.n % WSLOTS
                if self.n >= WSLOTS or self.loop is not None:
                    self.e.wait_ge(S["w_used"], self.number(1 - WSLOTS))
                self.e.dma_start(Wc[s] if dst is None else dst[s], src).then_inc(S[f"w_in{s}"], 16)
                self.n += 1

            def get(self):
                s = self.n % WSLOTS
                if self.loop is None:
                    val = 16 * (self.n // WSLOTS + 1)
                else:
                    reg, per = self.loop
                    val = reg * (16 * per // WSLOTS) + 16 * (self.n // WSLOTS + 1)
                self.e.wait_ge(S[f"w_in{s}"], val)
                return s

            def done(self, pe):
                self.e.wait_ge(*pe.last)
                self.e.sem_inc(S["w_used"], 1)
                self.n += 1

        def cols(w, c):
            return w[:, c * 512:(c + 1) * 512].rearrange("(k p) n -> p k n", p=P)

        N_HYB = 15

        EB = 4

        def sp_moe(sp, st, layer):
            with sp.Fori(0, N_EXP // EB) as i:
                st.enter(i, 6 * EB)
                for e in range(EB):
                    g, u, dn = (a[n][layer][bass.ds(i * EB + e, 1)].rearrange("o r n -> (o r) n")
                                for n in ("moe_w_gate_2", "moe_w_up_2", "moe_w_down_2"))
                    for c in range(2):
                        st.load(cols(g, c))
                        st.load(cols(u, c))
                    for c in range(2):
                        st.load(cols(dn, c))
            st.leave(N_EXP // EB)

        def act_setup(A):
            e = A.e
            loads = [(v(ID_, P), a["k_ident"]), (v(GV_, N_GV), a["k_gvec"]), (v(LS_, DEPTH * N_LV), a["k_lvec"]),
                     (XT, a["x"]), ]
            for dst, src in loads:
                e.dma_start(dst, src).then_inc(S["const_in"], 16)
            A.e.wait_ge(S["const_in"], 16 * len(loads))
            act(MISC[:, 16:32], gv("c", 0, 16), ACT.Silu).then_inc(A.mark("a_ready"), 1)
            end_phase(A)

        def pe_setup(A, st):
            A.e.wait_ge(S["const_in"], 64)
            A.e.wait_ge(S["a_ready"], 1)
            for l in range(DEPTH):
                for c in range(12):
                    s = st.get()
                    for b in range(4):
                        col = (c * 4 + b) * 2
                        for k in range(KD):
                            m = mm(ps[:, l, col:col + 2], Wc[s][:, k, b * P:(b + 1) * P],
                                   MISC[:, 16 + 2 * k:18 + 2 * k], start=(k == 0), stop=(k == KD - 1))
                    m.then_inc(A.mark("psum_full"), 1)
                    st.done(A)
            end_phase(A)

        def dve_setup(A):
            nc.vector.memset(ONES, 1.0).then_inc(A.mark(), 1)
            nc.vector.memset(MISC[:, 0:1], EPS).then_inc(A.mark(), 1)
            nc.vector.memset(MISC[:, 1:2], 1.0).then_inc(A.mark(), 1)
            nc.vector.memset(MISC[:, 2:3], 0.0).then_inc(A.mark(), 1)
            A.e.wait_ge(S["const_in"], 64)
            for l in range(DEPTH):
                A.e.wait_ge(S["psum_full"], 12 * (l + 1))
                dst = v(MOD_ + 96 * l, 48, 2)
                tt(dst, ps[:, l, 0:96].rearrange("p (a b) -> p a b", b=2),
                          gv("ada_b", 48 * l, 48).unsqueeze(2).to_broadcast([P, 48, 2]), ALU.add).then_inc(A.mark(), 1)
            end_phase(A)

        def act_norm(A, src, sq, rs, n, bank, turn, div=D, kt=KD):
            act(sq, src, ACT.Square).then_inc(A.mark("squares"), 1)
            A.e.wait_ge(S["stat"], turn)
            act(rs, ps[:, bank, 0:n], ACT.Sqrt, bias=eps_col, scale=1.0 / div).then_inc(A.mark("rstd"), 1)

        def pe_norm(A, sq, n, bank, turn, kt=KD):
            A.e.wait_ge(S["squares"], turn)
            for k in range(kt):
                m = mm(ps[:, bank, 0:n], ONES, sq[:, k, :], start=(k == 0), stop=(k == kt - 1))
            m.then_inc(A.mark("stat"), 1)

        def dve_recip(A, rs, turn):
            A.e.wait_ge(S["rstd"], turn)
            nc.vector.reciprocal(rs, rs).then_inc(A.mark(), 1)
            A.e.wait_ge(*A.last)

        hm = Map(AR_)
        QT_ = hm.take(12 * 512)
        KT_ = hm.take(12 * 512)
        GT_ = hm.take(12 * 512)
        VN_ = hm.take(12 * 512)
        MASK_ = hm.take(4 * P)
        PERM_ = hm.take(P)
        TMP_ = hm.take(1100)
        WFF_ = hm.take(64)
        assert hm.at <= AR_END, hm.at
        QT, KT, GT = v(QT_, 12, 512), v(KT_, 12, 512), v(GT_, 12, 512)
        VN = v(VN_, 12, 512)
        ROPE = v(CT_, 2, 512)
        CUM, NCUM = v(CT_ + 1024, 512, p=8), v(CT_ + 1536, 512, p=8)
        WFF = v(WFF_, KD, 8)
        MASK = v(MASK_, 4, P)
        PERM = v(PERM_, P)
        WT = [v(HT_ + i * 2048, 4, 512) for i in range(2)]
        PB = [v(HT_ + 4096 + i * 516, 513) for i in range(3)]
        PB1 = [v(TMP_, 513), v(TMP_ + 516, 513)]
        SMALL = MISC[:, 32:96]
        H_PHASES = 5
        HK = [(kind, which, t) for kind in range(3) for which in "qkvg" for t in range(4)]
        HWHO = ["act" if w == "g" else "dve" if (w == "v" or t % 2) else "act" for _, w, t in HK]
        HWHO.append("dve")

        def hyb_dest(j):
            kind, w, t = HK[j]
            return {"q": QT, "k": KT, "g": GT, "v": VN}[w][:, kind * 4 + t, :]

        def pe_hyb_proj(A, st):
            pe_norm(A, SQ, T, 7, 1)
            A.e.wait_ge(S["h_ready"], 1)
            for j in range(len(HK) + 1):
                if j < len(HK) and j % 4 == 0:
                    s = st.get()
                if j >= 4:
                    who = HWHO[j - 4]
                    A.e.wait_ge(S[f"{who}_out"], nth(HWHO, j - 4))
                if j < len(HK):
                    kind, w, t = HK[j]
                    for k in range(KD):
                        if w == "v":
                            m = mm(ps[:, j % 4, :], HTL[:, k, t * P:(t + 1) * P], Wc[s][:, k, :],
                                   start=(k == 0), stop=(k == KD - 1))
                        else:
                            m = mm(ps[:, j % 4, :], Wc[s][:, k, t * P:(t + 1) * P], HTL[:, k, :],
                                   start=(k == 0), stop=(k == KD - 1))
                else:
                    A.e.wait_ge(S["const2_in"], 16)
                    for k in range(KD):
                        m = mm(ps[0:8, j % 4, :], WFF[:, k, :], HTL[:, k, :], start=(k == 0), stop=(k == KD - 1))
                m.then_inc(A.mark("psum_full"), 1)
                if j % 4 == 3:
                    st.done(A)
            end_phase(A)

        SQ = v(QT_, KD, 512)
        RS = v(TMP_, 512)

        def act_hyb_proj(A, l):
            e = A.e
            wff = a["w_in"][bass.ds(l, 1)].rearrange("o r n -> (o r) n")[:, 6144:6152].rearrange("(k p) n -> p k n", p=P)
            e.dma_start(WFF, wff).then_inc(S["const2_in"], 16)
            for dst, src in ((v(CT_, 1024), a["k_rope"][:, 0:1024]), (PERM, a["k_rope"][:, 1024:1152]),
                             (v(MASK_, 512), a["k_masks"])):
                e.dma_start(dst, src).then_inc(S["const_in"], 16)
            act_norm(A, XT, SQ, RS, T, 7, 1)
            for j in range(len(HK)):
                if HWHO[j] != "act":
                    continue
                A.e.wait_ge(S["psum_full"], j + 1)
                if j == 0:
                    A.e.wait_ge(S["h_ready"], 1)
                fn = {"g": ACT.Silu}.get(HK[j][1], ACT.Copy)
                act(hyb_dest(j), ps[:, j % 4, :], fn, scale=0.125 if HK[j][1] == "q" else 1.0).then_inc(A.mark("act_out"), 1)
            FT = SMALLROW
            A.e.wait_ge(S["b_ready"], 1)
            act(FT[1], FT[1], ACT.Exp, scale=-1.0).then_inc(A.mark(), 1)
            A.e.wait_ge(*A.last)
            act(FT[1], FT[1], ACT.Ln, bias=MISC[0:8, 1:2]).then_inc(A.mark("c_ready"), 1)
            A.e.wait_ge(S["const_in"], 48)
            end_phase(A)

        SMALLROW = [v(TMP_, 512, p=8), v(TMP_ + 512, 512, p=8)]

        def dve_hyb_proj(A, l):
            LSV = v(LS_, DEPTH, N_LV)
            nc.vector.tensor_copy(v(LV_, N_LV), LSV[:, bass.ds(l, 1), :].rearrange("p o n -> p (o n)")).then_inc(A.mark(), 1)
            A.e.wait_ge(*A.last)
            dve_recip(A, RS, 1)
            for k in range(KD):
                stt(HTL[:, k, :], XT[:, k, :], lv("g_pre", k), RS, ALU.mult, ALU.mult).then_inc(A.mark(), 1)
            A.e.wait_ge(*A.last)
            nc.vector.memset(MISC[:, 3:4], 0.0).then_inc(A.mark("h_ready"), 1)
            for j in range(len(HK)):
                if HWHO[j] != "dve":
                    continue
                A.e.wait_ge(S["psum_full"], j + 1)
                if HK[j][1] == "q":
                    ins = ts(hyb_dest(j), ps[:, j % 4, :], 0.125, None, ALU.mult)
                else:
                    ins = nc.vector.tensor_copy(hyb_dest(j), ps[:, j % 4, :])
                ins.then_inc(A.mark("dve_out"), 1)
            A.e.wait_ge(S["psum_full"], len(HK) + 1)
            FT = SMALLROW
            j = len(HK)
            ts(FT[0], ps[0:8, j % 4, :], lv("f_bias", p=8), None, ALU.add).then_inc(A.mark(), 1)
            A.e.wait_ge(*A.last)
            ts(FT[1], FT[0], -1.0, None, ALU.mult).then_inc(A.mark(), 1)
            A.e.wait_ge(*A.last)
            tt(FT[1], FT[1], FT[0], ALU.max).then_inc(A.mark("b_ready"), 1)
            ts(FT[0], FT[0], 0.0, None, ALU.min).then_inc(A.mark(), 1)
            A.e.wait_ge(S["c_ready"], 1)
            A.e.wait_ge(*A.last)
            tt(FT[0], FT[0], FT[1], ALU.subtract).then_inc(A.mark(), 1)
            A.e.wait_ge(*A.last)
            nc.vector.tensor_tensor_scan(CUM, one_col[0:8].to_broadcast([8, 512]), FT[0], 0.0, ALU.mult, ALU.add).then_inc(A.mark(), 1)
            A.e.wait_ge(*A.last)
            ts(NCUM, CUM, -1.0, None, ALU.mult).then_inc(A.mark(), 1)
            tt(SMALL[:, 0:1], lv("lam_vec", 0), lv("lam_vec", 1), ALU.mult).then_inc(A.mark(), 1)
            tt(SMALL[:, 1:2], lv("lam_vec", 2), lv("lam_vec", 3), ALU.mult).then_inc(A.mark(), 1)
            tt(SMALL[:, 8:9], lv("subln"), lv("one_minus"), ALU.mult).then_inc(A.mark(), 1)
            end_phase(A)

        def pe_hyb_rope(A):
            mm(ps[:, 7, 0:2], ONES, SMALL[:, 0:2], start=True, stop=True)
            for j in range(8):
                if j >= 4:
                    A.e.wait_ge(S["dve_out"], j - 3)
                src = (QT, KT)[j // 4][:, j % 4, :]
                mm(ps[:, j % 4, :], PERM, src, start=True, stop=True).then_inc(A.mark("psum_full"), 1)
            end_phase(A)

        def act_hyb_rope(A):
            A.e.wait_ge(S["psum_full"], 1)
            act(SMALL[:, 2:4], ps[:, 7, 0:2], ACT.Exp).then_inc(A.mark("a_ready"), 1)
            end_phase(A)

        def dve_hyb_rope(A):
            RT = [v(TMP_, 512), v(TMP_ + 512, 512)]
            for j in range(8):
                x = (QT, KT)[j // 4][:, j % 4, :]
                A.e.wait_ge(S["psum_full"], j + 1)
                tt(RT[j % 2], ps[:, j % 4, :], ROPE[:, 1, :], ALU.mult).then_inc(A.mark("dve_out"), 1)
                tt(x, x, ROPE[:, 0, :], ALU.mult).then_inc(A.mark(), 1)
                A.e.wait_ge(*A.last)
                A.e.wait_ge(S["dve_out"], j + 1)
                tt(x, x, RT[j % 2], ALU.add).then_inc(A.mark(), 1)
            A.e.wait_ge(S["a_ready"], 1)
            tt(SMALL[:, 4:5], SMALL[:, 3:4], SMALL[:, 2:3], ALU.subtract).then_inc(A.mark(), 1)
            A.e.wait_ge(*A.last)
            tt(SMALL[:, 5:6], SMALL[:, 4:5], lv("lam_init"), ALU.subtract).then_inc(A.mark(), 1)
            end_phase(A)

        UN = [(kind, h, i) for kind, nh in ((0, 4), (1, 8), (2, 8)) for h in range(nh) for i in range(NQ)]
        LAG = 2
        HEADS = [(kind, h) for kind, nh in ((0, 4), (1, 8), (2, 8)) for h in range(nh)]

        def unit_banks(u):
            return (2 * (u % 2), 2 * (u % 2) + 1) if UN[u][0] == 0 else (u % 4,)

        def prev_user(u):
            for w in range(u - 1, -1, -1):
                if set(unit_banks(w)) & set(unit_banks(u)):
                    return w
            return None

        def pbuf(u, c):
            return PB[u % 3] if c == 0 else PB1[u % 2]

        def pe_attn(A):
            for s in range(len(UN) + LAG):
                if s < len(UN):
                    kind, h, i = UN[s]
                    w = prev_user(s)
                    if w is not None:
                        A.e.wait_ge(S["probs"], w + 1)
                    kw = (i + 1) * P
                    for c, bank in enumerate(unit_banks(s)):
                        if kind == 0:
                            tile, r = h, 64 * c
                        else:
                            tile, r = 4 * kind + h // 2, 64 * (h % 2)
                        o = ps[:, bank, 0:kw]
                        mm(o, QT[r:r + 64, tile, i * P:kw], KT[r:r + 64, tile, 0:kw], start=True, stop=False)
                        if kind == 2:
                            hot = IDENT[0:8, h:h + 1]
                            mm(o, CUM[:, i * P:kw], hot.to_broadcast([8, kw]), start=False, stop=False)
                            mm(o, hot.to_broadcast([8, P]), NCUM[:, 0:kw], start=False, stop=False)
                        m = mm(ps[:, bank, i * P:kw], IDENT, MASK[:, kind, :], start=False, stop=True)
                    m.then_inc(A.mark("scores"), 1)
                if s >= LAG:
                    u = s - LAG
                    kind, h, i = UN[u]
                    if u >= 2:
                        A.e.wait_ge(S["turned_out"], u - 1)
                    A.e.wait_ge(S["weights"], u + 1)
                    src = pbuf(u, 1 if kind == 1 else 0)
                    for j in range(i + 1):
                        m = tr(ps[:, 4 + u % 2, j * P:(j + 1) * P], src[:, j * P:(j + 1) * P], IDENT)
                    m.then_inc(A.mark("turned"), 1)
                    if i == 0 and u > 0:
                        pe_pv(A, u // NQ - 1)
            pe_pv(A, len(HEADS) - 1)
            end_phase(A)

        def pe_pv(A, hh):
            kind, h = HEADS[hh]
            A.e.wait_ge(S["turned_out"], NQ * (hh + 1))
            if hh >= 2:
                A.e.wait_ge(S["o_out"], hh - 1)
            M_, r, col = (P, 0, h * P) if kind == 0 else (64, 64 * (h % 2), h * 64)
            for j in range(NQ):
                m = mm(ps[r:r + M_, 6 + hh % 2, j * P:T], VN[:, kind * 4 + j, col:col + M_], WT[hh % 2][:, j, j * P:T],
                       start=(j == 0), stop=(j == NQ - 1))
            m.then_inc(A.mark("o_full"), 1)

        def act_attn(A):
            mxn = 0
            for s in range(len(UN) + LAG + 1):
                if s < len(UN):
                    kind, h, i = UN[s]
                    kw = (i + 1) * P
                    bk = unit_banks(s)
                    if s >= 2:
                        A.e.wait_ge(S["turned"], s - 1)
                    if kind == 1:
                        A.e.wait_ge(S["scores"], s + 1)
                        act(pbuf(s, 0)[:, 0:kw], ps[:, bk[0], 0:kw], ACT.Sigmoid, scale=-1.0).then_inc(A.mark(), 1)
                        act(pbuf(s, 1)[:, 0:kw], ps[:, bk[0], 0:kw], ACT.Sigmoid).then_inc(A.mark("probs"), 1)
                    else:
                        mxn += 1
                        A.e.wait_ge(S["maxima"], mxn)
                        for c, bank in enumerate(bk):
                            ins = act(pbuf(s, c)[:, 0:kw], ps[:, bank, 0:kw], ACT.Exp,
                                      bias=SMALL[:, 16 + 2 * (s % 4) + c:17 + 2 * (s % 4) + c],
                                      accum_out=SMALL[:, 32 + 2 * (s % 4) + c:33 + 2 * (s % 4) + c])
                            ins.then_inc(A.mark("probs" if c == len(bk) - 1 else None), 1)
                if s >= LAG + 1 - 1 and s - LAG < len(UN) and s - LAG >= 0:
                    u = s - LAG
                    kind, h, i = UN[u]
                    hh = u // NQ
                    A.e.wait_ge(S["turned"], u + 1)
                    if i == 0 and hh >= 2:
                        A.e.wait_ge(S["o_full"], hh - 1)
                    act(WT[hh % 2][:, 0:i + 1, i * P:(i + 1) * P],
                               ps[:, 4 + u % 2, 0:(i + 1) * P].rearrange("p (j q) -> p j q", q=P), ACT.Copy).then_inc(A.mark("turned_out"), 1)
            end_phase(A)

        def dve_attn(A):
            def evac_o(hh):
                kind, h = HEADS[hh]
                A.e.wait_ge(S["o_full"], hh + 1)
                if kind == 0:
                    nc.vector.tensor_copy(QT[:, h, :], ps[:, 6 + hh % 2, :]).then_inc(A.mark("o_out"), 1)
                else:
                    r = 64 * (h % 2)
                    g = GT[r:r + 64, 4 * kind + h // 2, :]
                    tt(g, ps[r:r + 64, 6 + hh % 2, :], g, ALU.mult).then_inc(A.mark("o_out"), 1)

            for s in range(len(UN) + LAG + 1):
                if s < len(UN):
                    kind, h, i = UN[s]
                    kw = (i + 1) * P
                    if kind != 1:
                        A.e.wait_ge(S["scores"], s + 1)
                        for c, bank in enumerate(unit_banks(s)):
                            ins = nc.vector.tensor_reduce(SMALL[:, 16 + 2 * (s % 4) + c:17 + 2 * (s % 4) + c],
                                                          ps[:, bank, 0:kw], AX_X, ALU.max, negate=True)
                            ins.then_inc(A.mark("maxima" if c == len(unit_banks(s)) - 1 else None), 1)
                if 1 <= s <= len(UN):
                    u = s - 1
                    kind, h, i = UN[u]
                    kw = (i + 1) * P
                    p0, p1 = pbuf(u, 0), pbuf(u, 1)
                    sums = SMALL[:, 32 + 2 * (u % 4):34 + 2 * (u % 4)]
                    inv = SMALL[:, 40 + 2 * (u % 4):42 + 2 * (u % 4)]
                    A.e.wait_ge(S["probs"], u + 1)
                    if kind == 0:
                        nc.vector.reciprocal(inv, sums).then_inc(A.mark(), 1)
                        A.e.wait_ge(*A.last)
                        tt(inv[:, 1:2], inv[:, 1:2], SMALL[:, 5:6], ALU.mult).then_inc(A.mark(), 1)
                        A.e.wait_ge(*A.last)
                        ts(p1[:, 0:kw], p1[:, 0:kw], inv[:, 1:2], None, ALU.mult).then_inc(A.mark(), 1)
                        A.e.wait_ge(*A.last)
                        stt(p0[:, 0:kw], p0[:, 0:kw], inv[:, 0:1], p1[:, 0:kw], ALU.mult, ALU.add).then_inc(A.mark("weights"), 1)
                    elif kind == 1:
                        nc.vector.memset(p0[:, kw:kw + 1], 1.0).then_inc(A.mark(), 1)
                        nc.vector.tensor_tensor_scan(p0[:, 0:kw][:, ::-1], p0[:, 0:kw][:, ::-1],
                                                            one_col.to_broadcast([P, kw]), 1.0, ALU.mult, ALU.mult).then_inc(A.mark(), 1)
                        A.e.wait_ge(*A.last)
                        tt(p1[:, 0:kw], p1[:, 0:kw], p0[:, 1:kw + 1], ALU.mult).then_inc(A.mark("weights"), 1)
                    else:
                        nc.vector.reciprocal(inv[:, 0:1], sums[:, 0:1]).then_inc(A.mark(), 1)
                        A.e.wait_ge(*A.last)
                        ts(p0[:, 0:kw], p0[:, 0:kw], inv[:, 0:1], None, ALU.mult).then_inc(A.mark("weights"), 1)
                if s >= LAG + 2 and (s - LAG - 2) % NQ == 0 and (s - LAG - 2) // NQ >= 1:
                    evac_o((s - LAG - 2) // NQ - 1)
            evac_o(len(HEADS) - 1)
            end_phase(A)

        def pe_hyb_out(A, st):
            for h in range(4):
                A.e.wait_ge(S["squares"], h + 1)
                mm(ps[:, h, :], ONES, SQS[:, h, :], start=True, stop=True).then_inc(A.mark("stat"), 1)
            A.e.wait_ge(S["h_ready"], 1)
            for c in range(3):
                s = st.get()
                for b in range(KD):
                    for k in range(4):
                        m = mm(ps[:, b, :], Wr[s][:, k, b * P:(b + 1) * P], GT[:, 4 * c + k, :],
                               start=(c == 0 and k == 0), stop=(c == 2 and k == 3))
                    if c == 2:
                        m.then_inc(A.mark("psum_full"), 1)
                if c < 2:
                    m.then_inc(A.mark(), 1)
                st.done(A)
            A.e.wait_ge(S["squares"], 5)
            A.e.wait_ge(S["a_ready"], 1)
            for k in range(KD):
                m = mm(ps[:, 0, :], ONES, SQY[:, k, :], start=(k == 0), stop=(k == KD - 1))
            m.then_inc(A.mark("stat"), 1)
            end_phase(A)

        SQS = v(QT_ + 2048, 4, 512)
        RSH = v(QT_ + 4096, 4, 512)
        YS = v(HT_, KD, 512)
        SQY = v(QT_, KD, 512)

        def act_hyb_out(A):
            for h in range(4):
                act(SQS[:, h, :], QT[:, h, :], ACT.Square).then_inc(A.mark("squares"), 1)
            for h in range(4):
                A.e.wait_ge(S["stat"], h + 1)
                act(RSH[:, h, :], ps[:, h, :], ACT.Sqrt, bias=eps_col, scale=1.0 / P).then_inc(A.mark("rstd"), 1)
            for b in range(KD):
                A.e.wait_ge(S["psum_full"], b + 1)
                act(YS[:, b, :], ps[:, b, :], ACT.Copy).then_inc(A.mark("a_ready" if b == KD - 1 else None), 1)
            A.e.wait_ge(*A.last)
            act(SQY, YS, ACT.Square).then_inc(A.mark("squares"), 1)
            A.e.wait_ge(S["stat"], 5)
            act(RS, ps[:, 0, :], ACT.Sqrt, bias=eps_col, scale=1.0 / D).then_inc(A.mark("rstd"), 1)
            end_phase(A)

        def dve_hyb_out(A):
            for h in range(4):
                dve_recip(A, RSH[:, h, :], h + 1)
                stt(QT[:, h, :], QT[:, h, :], SMALL[:, 8:9], RSH[:, h, :], ALU.mult, ALU.mult).then_inc(A.mark(), 1)
                A.e.wait_ge(*A.last)
                tt(GT[:, h, :], GT[:, h, :], QT[:, h, :], ALU.mult).then_inc(A.mark(), 1)
            A.e.wait_ge(*A.last)
            nc.vector.memset(MISC[:, 3:4], 0.0).then_inc(A.mark("h_ready"), 1)
            dve_recip(A, RS, 5)
            for k in range(KD):
                stt(YS[:, k, :], YS[:, k, :], lv("g_post", k), RS, ALU.mult, ALU.mult).then_inc(A.mark(), 1)
            A.e.wait_ge(*A.last)
            tt(XT, XT, YS, ALU.add).then_inc(A.mark(), 1)
            end_phase(A)

        def side(n):
            return (T, XT, HTL) if n == 0 else (TC, CT, v(HT_ + KD * T, KD, TC))

        def act_mod_norm(A, n, sq, rs, layer, which, turn):
            L, X, H = side(n)
            act_norm(A, X, sq, rs, L, 7, turn)
            A.e.wait_ge(S["a_ready"], turn)
            for k in range(KD):
                act(H[:, k, :], H[:, k, :], ACT.Identity, bias=mod(layer, which, k, n)).then_inc(A.mark("h_ready" if k == KD - 1 else None), 1)

        def dve_mod_norm(A, n, rs, layer, which, norm, turn):
            L, X, H = side(n)
            sc = v(MOD_ + layer * 96, 48, 2)[:, (which + 1) * KD:(which + 2) * KD, n]
            g = MISC[:, 40:48]
            stt(g, sc, 1.0, gv(norm, layer * KD, KD), ALU.add, ALU.mult).then_inc(A.mark(), 1)
            dve_recip(A, rs, turn)
            for k in range(KD):
                stt(H[:, k, :], X[:, k, :], g[:, k:k + 1], rs, ALU.mult, ALU.mult).then_inc(A.mark("a_ready" if k == KD - 1 else None), 1)
            A.e.wait_ge(*A.last)

        ym = Map(AR_)
        U3_, DC_, DS_ = ym.take(24 * 512), ym.take(2048), ym.take(2048)
        FS_, GS_, NY_, KS_ = ym.take(512), ym.take(512), ym.take(512), ym.take(4096)
        WIN_, H2_, T_, W3_, FB_ = ym.take(1024), ym.take(512), ym.take(1024), ym.take(1024), ym.take(512)
        assert ym.at <= AR_END, ym.at
        DC, DS = v(DC_, 4, 512), v(DS_, 4, 512)
        FB = v(FB_, 512, p=1)
        UT_ = KS_

        class Hy:
            def __init__(s, n):
                s.n = n
                s.L = L = (T, TC)[n]
                s.tag = "lc"[n]
                s.nt = L // P
                s.step = T // L
                s.U3 = v(U3_, 24, L)
                s.FS, s.NY = v(FS_, s.nt, P), v(NY_, s.nt, P)
                s.GS = v(GS_, L)
                s.UT = [v(UT_ + i * 516, L + 2) for i in range(2)]
                s.H2 = v(H2_, L, p=64)
                s.H1 = v(H2_, L, p=64)
                s.HE, s.HO, s.HB = (v(HT_ + i * 2048, 4, 512) for i in range(3))
                s.VN = s.HE

            def fwd(s, table, t, f):
                lo = f * P * s.step
                return table[:, t, lo:lo + P * s.step:s.step]

            def inv(s, table, f):
                return table[:, f, 0:T:s.step]

        def act_hy_a(A, y):
            e = A.e
            L = y.L
            pairs = [(v(DC_, 4096), a["k_dft"]), (v(FS_, y.nt * P), a[f"k_fs0_{y.tag}"]),
                     (v(NY_, y.nt * P), a[f"k_nyq_{y.tag}"]), (v(GS_, L), a[f"k_gs0_{y.tag}"]),
                     (v(W3_, L, p=33), a[f"k_pos_{y.tag}"]), (v(W3_ + 512, 64, p=33), a["hy_ffn_w1_2"]),
                     (v(W3_ + 576, 64, p=64), a["hy_ffn_w2_2"])]
            for dst, src in pairs:
                e.dma_start(dst, src).then_inc(S["const_in"], 16)
            act_mod_norm(A, y.n, v(KS_, KD, L), v(T_, L), 0, 0, 1)
            for r in range(2):
                A.e.wait_ge(S["b_ready"], r + 1)
                act(y.H2, v(T_, L, p=64), ACT.Sin).then_inc(A.mark("c_ready"), 1)
            for j in range(24):
                A.e.wait_ge(S["psum_full"], j + 1)
                if j >= 2:
                    A.e.wait_ge(S["dve_out"], j - 1)
                if j == 0:
                    A.e.wait_ge(S["d_ready"], 1)
                act(y.UT[j % 2][:, 1:L + 1], ps[:, j % 4, 0:L], ACT.Identity, bias=gv("hy_b_in", j)).then_inc(A.mark("act_out"), 1)
            A.e.wait_ge(S["const_in"], 16 * 7)
            end_phase(A)

        def pe_hy_a(A, y, st):
            L = y.L
            pe_norm(A, v(KS_, KD, L), L, 7, 1)
            A.e.wait_ge(S["const_in"], 16 * 7)
            mm(ps[0:64, 6, 0:L], v(W3_ + 512, 64, p=33), v(W3_, L, p=33), start=True, stop=True).then_inc(A.mark("e_ready"), 1)
            A.e.wait_ge(S["c_ready"], 1)
            mm(ps[0:64, 5, 0:L], v(W3_ + 576, 64, p=64), y.H1, start=True, stop=True).then_inc(A.mark("e_ready"), 1)
            A.e.wait_ge(S["h_ready"], 1)
            _, _, H = side(y.n)
            for j in range(24):
                if j % 4 == 0:
                    s = st.get()
                if j >= 4:
                    A.e.wait_ge(S["act_out"], j - 3)
                for k in range(KD):
                    m = mm(ps[:, j % 4, 0:L], Wc[s][:, k, (j % 4) * P:(j % 4 + 1) * P], H[:, k, :],
                           start=(k == 0), stop=(k == KD - 1))
                m.then_inc(A.mark("psum_full"), 1)
                if j % 4 == 3:
                    st.done(A)
            end_phase(A)

        MAGIC = 1.5 * 2.0 ** 23
        PI2_HI = 6.28125
        PI2_LO = TWO_PI - PI2_HI
        PI_IN = 3.1415925

        def dve_hy_a(A, y):
            L = y.L
            dve_mod_norm(A, y.n, v(T_, L), 0, 0, "norm1", 1)
            x, n = v(T_, L, p=64), v(T_ + 512, L, p=64)
            for r in range(2):
                A.e.wait_ge(S["e_ready"], r + 1)
                src = ps[0:64, 6 - r, 0:L]
                ts(x, src, gv("ffn_b1" if r == 0 else "ffn_b2", p=64), gv("freq", r, p=64), ALU.add, ALU.mult).then_inc(A.mark(), 1)
                A.e.wait_ge(*A.last)
                ts(n, x, 1 / TWO_PI, MAGIC, ALU.mult, ALU.add).then_inc(A.mark(), 1)
                A.e.wait_ge(*A.last)
                ts(n, n, -MAGIC, None, ALU.add).then_inc(A.mark(), 1)
                A.e.wait_ge(*A.last)
                stt(x, n, -PI2_HI, x, ALU.mult, ALU.add).then_inc(A.mark(), 1)
                A.e.wait_ge(*A.last)
                stt(x, n, -PI2_LO, x, ALU.mult, ALU.add).then_inc(A.mark(), 1)
                A.e.wait_ge(*A.last)
                ts(x, x, PI_IN, -PI_IN, ALU.min, ALU.max).then_inc(A.mark("b_ready"), 1)
                A.e.wait_ge(S["c_ready"], r + 1)
            A.e.wait_ge(S["stat"], 1)
            A.e.wait_ge(S["squares"], 1)
            for u in y.UT:
                nc.vector.memset(u[:, 0:1], 0.0).then_inc(A.mark(), 1)
                nc.vector.memset(u[:, L + 1:L + 2], 0.0).then_inc(A.mark("d_ready" if u is y.UT[1] else None), 1)
            for j in range(24):
                u, o = y.UT[j % 2], y.U3[:, j, :]
                A.e.wait_ge(S["act_out"], j + 1)
                ts(o, u[:, 1:L + 1], gv("hy_sw", 24 + j), gv("hy_sb", j), ALU.mult, ALU.add).then_inc(A.mark(), 1)
                A.e.wait_ge(*A.last)
                stt(o, u[:, 0:L], gv("hy_sw", j), o, ALU.mult, ALU.add).then_inc(A.mark(), 1)
                A.e.wait_ge(*A.last)
                stt(o, u[:, 2:L + 2], gv("hy_sw", 48 + j), o, ALU.mult, ALU.add).then_inc(A.mark("dve_out"), 1)
            end_phase(A)

        def act_hy_b(A, y, c, o):
            e = A.e
            for d in range(2):
                lo = o * 2048 + d * 1024 + c * 512
                e.dma_start(v(W3_ + d * 512, 512, p=64), a["hy_ffn_w3_2"][:, lo:lo + 512]).then_inc(S["const_in"], 16)
            e.dma_start(FB, a["hy_filter_bias_2"][o:o + 1, c * 512:(c + 1) * 512]).then_inc(S["const_in"], 16)
            for t in range(y.nt):
                if t >= 2:
                    A.e.wait_ge(S["dve_out"], t - 1)
                e.dma_start(v(WIN_ + (t % 2) * 512, 512),
                            a[f"k_win_{y.tag}"][t * P:(t + 1) * P, c * 512:(c + 1) * 512])\
                    .then_inc(S[("m_ready", "n_ready")[t % 2]], 16)
            for f in range(2 * y.nt):
                A.e.wait_ge(S["psum_full"], f + 1)
                act(v(KS_, 8, 512)[:, f, :], ps[:, f % 4, :], ACT.Copy,
                           scale=gv("dft_" + y.tag, 0 if f % y.nt == 0 else 1)).then_inc(A.mark("act_out"), 1)
            for t in range(y.nt):
                A.e.wait_ge(S["turned"], t + 1)
                act(y.VN[:, t, :], ps[:, 4 + t, :], ACT.Copy).then_inc(A.mark("turned_out"), 1)
            end_phase(A)

        def pe_hy_b(A, y, c, o):
            nt = y.nt
            A.e.wait_ge(S["const_in"], 48)
            for t in range(nt):
                if t >= 2:
                    A.e.wait_ge(S["dve_out"], t - 1)
                for d in range(2):
                    m = mm(ps[:, 4 + 2 * (t % 2) + d, :], y.H2[:, t * P:(t + 1) * P], v(W3_ + d * 512, 512, p=64),
                           start=True, stop=True)
                m.then_inc(A.mark("a_ready"), 1)
            A.e.wait_ge(S["dve_out"], nt)
            for g in range(2 * nt):
                f = g % nt
                if g >= 4:
                    A.e.wait_ge(S["act_out"], g - 3)
                for t in range(nt):
                    if g < nt:
                        m = mm(ps[:, g % 4, :], y.fwd(DC, t, f), y.HE[:, t, :], start=(t == 0), stop=(t == nt - 1))
                    elif f:
                        m = mm(ps[:, g % 4, :], y.fwd(DS, t, f), y.HO[:, t, :], start=(t == 0), stop=(t == nt - 1))
                    else:
                        mm(ps[:, g % 4, :], y.FS[:, t, :], y.HO[:, t, :], start=(t == 0), stop=False)
                        m = mm(ps[:, g % 4, :], y.NY[:, t, :], y.HB[:, t, :], start=False, stop=(t == nt - 1))
                m.then_inc(A.mark("psum_full"), 1)
            A.e.wait_ge(*A.last)
            for t in range(nt):
                for b in range(4):
                    m = tr(ps[:, 4 + t, b * P:(b + 1) * P], y.U3[:, c * 4 + b, t * P:(t + 1) * P], IDENT)
                m.then_inc(A.mark("turned"), 1)
            A.e.wait_ge(S["turned_out"], nt)
            A.e.wait_ge(S["act_out"], 2 * nt)
            for f in range(nt):
                if f >= 2:
                    A.e.wait_ge(S["b_ready"], f - 1)
                for part in range(2):
                    for t in range(nt):
                        w = y.fwd(DC, t, f) if part == 0 else y.fwd(DS, t, f) if f else y.FS[:, t, :]
                        m = mm(ps[:, 2 * (f % 2) + part, :], w, y.VN[:, t, :], start=(t == 0), stop=(t == nt - 1))
                m.then_inc(A.mark("c_ready"), 1)
            A.e.wait_ge(S["d_ready"], nt)
            for b in range(4):
                for f in range(2 * nt):
                    rhs = y.inv(DC, f) if f < nt else y.GS if f == nt else y.inv(DS, f - nt)
                    m = mm(ps[:, 4 + b, 0:y.L], v(KS_, 8, 512)[:, f, b * P:(b + 1) * P], rhs,
                           start=(f == 0), stop=(f == 2 * nt - 1))
                m.then_inc(A.mark("o_full"), 1)
            end_phase(A)

        def dve_hy_b(A, y, c, o):
            nt = y.nt
            KS = v(KS_, 8, 512)
            t0, t1 = v(T_, 512), v(T_ + 512, 512)
            for t in range(nt):
                w = v(WIN_ + (t % 2) * 512, 512)
                A.e.wait_ge(S["a_ready"], t + 1)
                A.e.wait_ge(S[("m_ready", "n_ready")[t % 2]], 16 * (t // 2 + 1))
                fw, bw = ps[:, 4 + 2 * (t % 2), :], ps[:, 5 + 2 * (t % 2), :]
                hb = y.HB[:, t, :]
                tt(t0, fw, w, ALU.mult).then_inc(A.mark(), 1)
                if t == 0:
                    stt(hb, bw, gv("not0"), w, ALU.mult, ALU.mult).then_inc(A.mark(), 1)
                    A.e.wait_ge(S["const_in"], 48)
                    A.e.wait_ge(*A.last)
                    tt(t0[0:1], t0[0:1], FB, ALU.add).then_inc(A.mark(), 1)
                else:
                    tt(hb, bw, w, ALU.mult).then_inc(A.mark(), 1)
                A.e.wait_ge(*A.last)
                tt(y.HE[:, t, :], t0, hb, ALU.add).then_inc(A.mark(), 1)
                tt(y.HO[:, t, :], t0, hb, ALU.subtract).then_inc(A.mark("dve_out"), 1)
                A.e.wait_ge(*A.last)
            krp, kip = y.HO[:, 0, :], y.HO[:, 1, :]
            A.e.wait_ge(S["act_out"], nt + 1)
            A.e.wait_ge(S["psum_full"], 2 * nt)
            ts(kip, KS[:, nt, :], gv("not0"), None, ALU.mult).then_inc(A.mark(), 1)
            ts(krp, KS[:, 0, :], gv("not0"), None, ALU.mult).then_inc(A.mark(), 1)
            A.e.wait_ge(*A.last)
            stt(krp, KS[:, nt, :], gv("is0"), krp, ALU.mult, ALU.add).then_inc(A.mark(), 1)
            A.e.wait_ge(*A.last)
            q = [t0, t1, v(WIN_, 512), v(WIN_ + 512, 512)]
            A.e.wait_ge(S["act_out"], 2 * nt)
            for f in range(nt):
                A.e.wait_ge(S["c_ready"], f + 1)
                ur, ui = ps[:, 2 * (f % 2), :], ps[:, 2 * (f % 2) + 1, :]
                kr, ki = KS[:, f, :], KS[:, nt + f, :]
                kr_i, ki_ = (krp, kip) if f == 0 else (kr, ki)
                tt(q[0], ur, kr, ALU.mult).then_inc(A.mark(), 1)
                tt(q[1], ui, ki_, ALU.mult).then_inc(A.mark(), 1)
                tt(q[2], ur, ki_, ALU.mult).then_inc(A.mark(), 1)
                tt(q[3], ui, kr_i, ALU.mult).then_inc(A.mark("b_ready"), 1)
                A.e.wait_ge(*A.last)
                tt(kr, q[0], q[1], ALU.subtract).then_inc(A.mark(), 1)
                tt(ki, q[2], q[3], ALU.add).then_inc(A.mark("d_ready"), 1)
                A.e.wait_ge(*A.last)
            for b in range(4):
                A.e.wait_ge(S["o_full"], b + 1)
                tt(y.U3[:, c * 4 + b, :], ps[:, 4 + b, 0:y.L], y.U3[:, 8 * (o + 1) + c * 4 + b, :], ALU.mult).then_inc(A.mark(), 1)
            end_phase(A)

        def pe_proj_out(A, st, src, L):
            for b in range(KD):
                if b % 4 == 0:
                    s = st.get()
                for k in range(KD):
                    m = mm(ps[:, b, 0:L], Wc[s][:, k, (b % 4) * P:(b % 4 + 1) * P], src[:, k, :],
                           start=(k == 0), stop=(k == KD - 1))
                m.then_inc(A.mark("psum_full"), 1)
                if b % 4 == 3:
                    st.done(A)
            end_phase(A)

        def dve_proj_out(A, n, tmp, layer, bias):
            L, X, _ = side(n)
            for b in range(KD):
                A.e.wait_ge(S["psum_full"], b + 1)
                g = mod(layer, 2, b, n)
                if bias:
                    ts(tmp, ps[:, b, 0:L], gv(bias, b), g, ALU.add, ALU.mult).then_inc(A.mark(), 1)
                    A.e.wait_ge(*A.last)
                    tt(X[:, b, :], X[:, b, :], tmp, ALU.add).then_inc(A.mark(), 1)
                    A.e.wait_ge(*A.last)
                else:
                    stt(X[:, b, :], ps[:, b, 0:L], g, X[:, b, :], ALU.mult, ALU.add).then_inc(A.mark(), 1)
            end_phase(A)

        em = Map(AR_)
        XE_, B_ = em.take(KD * N_EXP * 96), em.at
        HN_, SEL_ = em.take(6 * 1024), em.take(4096 + 1024)
        em.at = B_
        YE_ = em.take(12 * 1024)
        XS_, AT_, IO_, RT_, AF_, SL_ = (em.take(2 * KD * 96), em.take(KD * 96), em.take(CAP_L), em.take(KD * 16),
                                        em.take(96), em.take(96))
        assert em.at <= AR_END and HN_ + 6144 + 5120 <= XS_
        GS2_, GSC_, AB_ = HT_, HT_ + 4096, HT_ + 5120
        IO = v(IO_, CAP_L)
        RTR = v(RT_, KD, 16)
        AFF, SLOT = v(AF_, 6, 16), v(SL_, 6, 16)

        class Moe:
            def __init__(s, layer):
                s.layer = layer
                s.sides = (0, 1) if layer == 0 else (0,)
                s.S = CAP_L + (CAP_C if layer == 0 else 0)
                s.XE = v(XE_, KD, N_EXP * s.S).rearrange("p k (e s) -> p k e s", s=s.S)
                s.XS = [v(XS_ + i * KD * 96, KD, s.S) for i in range(2)]
                s.AT = v(AT_, KD, s.S)
                s.A = v(AB_, 1024, p=s.S)

            def side(s, n):
                if n == 0:
                    return T, CAP_L, 0, v(HN_, 4, 1024), v(SEL_, 4, 1024), v(GS2_, 8, 512), v(YE_, 8, 1024)
                return (TC, CAP_C, 4, v(HN_ + 4096, 2, 1024), v(SEL_ + 4096, 2, 512), v(GSC_, 4, 256),
                        v(YE_ + 8192, 4, 1024))

        SQM = lambda L: v(XE_, KD, L)
        RSM = lambda L: v(XE_ + 4096, L)

        def act_moe_a(A, m_):
            e = A.e
            e.dma_start(IO, a["k_iota"]).then_inc(S["const_in"], 16)
            e.dma_start(RTR, a["moe_router_2"][m_.layer].rearrange("(k p) n -> p k n", p=P)).then_inc(S["const_in"], 16)
            for z, n in enumerate(m_.sides):
                L = side(n)[0]
                if z:
                    A.e.wait_ge(S["stat"], z)
                act_mod_norm(A, n, SQM(L), RSM(L), m_.layer, 3, z + 1)
            x = 0
            for z, n in enumerate(m_.sides):
                L, _, t0 = m_.side(n)[0:3]
                A.e.wait_ge(S["maxima"], z + 1)
                for t in range(L // P):
                    act(AFF[:, t0 + t, :], ps[:, 6 - z, (t0 + t) * 16:(t0 + t + 1) * 16], ACT.Exp,
                               bias=MISC[:, 48 + t0 + t:49 + t0 + t], accum_out=MISC[:, 56 + t0 + t:57 + t0 + t]).then_inc(A.mark(), 1)
                act(MISC[:, 4:5], MISC[:, 2:3], ACT.Copy).then_inc(A.mark("probs"), 1)
            A.e.wait_ge(S["const_in"], 32)
            end_phase(A)

        def pe_moe_a(A, m_):
            for z, n in enumerate(m_.sides):
                L, _, H = side(n)
                pe_norm(A, SQM(L), L, 7, z + 1)
            A.e.wait_ge(S["const_in"], 32)
            for z, n in enumerate(m_.sides):
                L, _, H = side(n)
                t0 = m_.side(n)[2]
                A.e.wait_ge(S["h_ready"], z + 1)
                for t in range(L // P):
                    for k in range(KD):
                        m = mm(ps[:, 6 - z, (t0 + t) * 16:(t0 + t + 1) * 16], H[:, k, t * P:(t + 1) * P], RTR[:, k, :],
                               start=(k == 0), stop=(k == KD - 1))
                m.then_inc(A.mark("scores"), 1)
            end_phase(A)

        def dve_moe_a(A, m_):
            for z, n in enumerate(m_.sides):
                L = side(n)[0]
                dve_mod_norm(A, n, RSM(L), m_.layer, 3, "norm2", z + 1)
            for z, n in enumerate(m_.sides):
                L, _, t0 = m_.side(n)[0:3]
                nt = L // P
                A.e.wait_ge(S["scores"], z + 1)
                nc.vector.tensor_reduce(MISC[:, 48 + t0:48 + t0 + nt],
                                               ps[:, 6 - z, t0 * 16:(t0 + nt) * 16].rearrange("p (t x) -> p t x", x=16),
                                               AX_X, ALU.max, negate=True).then_inc(A.mark("maxima"), 1)
                A.e.wait_ge(S["probs"], z + 1)
                inv = MISC[:, 64 + t0:64 + t0 + nt]
                nc.vector.reciprocal(inv, MISC[:, 56 + t0:56 + t0 + nt]).then_inc(A.mark(), 1)
                A.e.wait_ge(*A.last)
                tt(AFF[:, t0:t0 + nt, :], AFF[:, t0:t0 + nt, :], inv.unsqueeze(2).to_broadcast([P, nt, 16]),
                          ALU.mult).then_inc(A.mark(), 1)
            end_phase(A)

        ROW = [v(XE_ + i * 768, 768, p=16) for i in range(6)]
        SM = lambda i, n=1: MISC[0:16, 72 + i:72 + i + n]

        def pe_moe_b(A, m_):
            for z, n in enumerate(m_.sides):
                L, _, t0 = m_.side(n)[0:3]
                for t in range(L // P):
                    m = tr(ps[0:16, 6 + z, t * P:(t + 1) * P], AFF[:, t0 + t, :], IDENT)
                m.then_inc(A.mark("a_ready"), 1)
            g = 0
            for z, n in enumerate(m_.sides):
                H = side(n)[2]
                for t in range(side(n)[0] // P):
                    for half in range(2):
                        if g >= 4:
                            A.e.wait_ge(S["turned_out"], g - 3)
                        for k in range(4):
                            m = tr(ps[:, g % 4, k * P:(k + 1) * P], H[:, half * 4 + k, t * P:(t + 1) * P], IDENT)
                        m.then_inc(A.mark("turned"), 1)
                        g += 1
            for z, n in enumerate(m_.sides):
                L, _, t0 = m_.side(n)[0:3]
                A.e.wait_ge(S["b_ready"], z + 1)
                for t in range(L // P):
                    m = tr(ps[:, 4 + z, (t0 + t) * 16:(t0 + t + 1) * 16], ROW[5][:, (t0 + t) * P:(t0 + t + 1) * P],
                           IDENT[0:16, 0:16])
                m.then_inc(A.mark("c_ready"), 1)
            end_phase(A)

        def act_moe_b(A, m_):
            for z, n in enumerate(m_.sides):
                L, _, t0 = m_.side(n)[0:3]
                A.e.wait_ge(S["a_ready"], z + 1)
                act(ROW[0][:, t0 * P:t0 * P + L], ps[0:16, 6 + z, 0:L], ACT.Copy).then_inc(A.mark("d_ready"), 1)
            g = 0
            for n in m_.sides:
                HN = m_.side(n)[3]
                for t in range(side(n)[0] // P):
                    for half in range(2):
                        A.e.wait_ge(S["turned"], g + 1)
                        act(HN[:, t, half * 512:(half + 1) * 512], ps[:, g % 4, :], ACT.Copy).then_inc(A.mark("turned_out"), 1)
                        g += 1
            end_phase(A)

        def dve_moe_b(A, m_):
            for z, n in enumerate(m_.sides):
                L, cap, t0 = m_.side(n)[0:3]
                af, wk, gt, eq, ce, sl = (r[:, t0 * P:t0 * P + L] for r in ROW)
                A.e.wait_ge(S["d_ready"], z + 1)
                nc.vector.tensor_copy(wk, af).then_inc(A.mark(), 1)
                A.e.wait_ge(*A.last)
                top = SM(0, 8)
                for r in range(cap // 8):
                    nc.vector.max(top, wk).then_inc(A.mark(), 1)
                    A.e.wait_ge(*A.last)
                    if r < cap // 8 - 1:
                        nc.vector.match_replace(wk, top, wk, -1.0).then_inc(A.mark(), 1)
                        A.e.wait_ge(*A.last)
                thr = SM(7)
                ts(gt, af, thr, None, ALU.is_gt).then_inc(A.mark(), 1)
                ts(eq, af, thr, None, ALU.is_equal).then_inc(A.mark(), 1)
                A.e.wait_ge(*A.last)
                nc.vector.tensor_reduce(SM(8), gt, AX_X, ALU.add).then_inc(A.mark(), 1)
                nc.vector.tensor_tensor_scan(ce, one_col[0:16].to_broadcast([16, L]), eq, 0.0, ALU.mult, ALU.add).then_inc(A.mark(), 1)
                A.e.wait_ge(*A.last)
                ts(SM(9), SM(8), -1.0, float(cap), ALU.mult, ALU.add).then_inc(A.mark(), 1)
                A.e.wait_ge(*A.last)
                stt(eq, ce, SM(9), eq, ALU.is_le, ALU.mult).then_inc(A.mark(), 1)
                A.e.wait_ge(*A.last)
                tt(gt, gt, eq, ALU.add).then_inc(A.mark(), 1)
                A.e.wait_ge(*A.last)
                nc.vector.tensor_tensor_scan(ce, one_col[0:16].to_broadcast([16, L]), gt, 0.0, ALU.mult, ALU.add).then_inc(A.mark(), 1)
                A.e.wait_ge(*A.last)
                tt(sl, ce, gt, ALU.mult).then_inc(A.mark(), 1)
                A.e.wait_ge(*A.last)
                ts(sl, sl, -1.0, None, ALU.add).then_inc(A.mark("b_ready"), 1)
            for z, n in enumerate(m_.sides):
                L, cap, t0, _, SEL = m_.side(n)[0:5]
                nt = L // P
                A.e.wait_ge(S["c_ready"], z + 1)
                nc.vector.tensor_copy(SLOT[:, t0:t0 + nt, :], ps[:, 4 + z, t0 * 16:(t0 + nt) * 16]
                                             .rearrange("p (t x) -> p t x", x=16)).then_inc(A.mark(), 1)
                A.e.wait_ge(*A.last)
                for t in range(nt):
                    tt(SEL[:, t, :].rearrange("p (e s) -> p e s", s=cap),
                              SLOT[:, t0 + t, :].unsqueeze(2).to_broadcast([P, 16, cap]),
                              IO[:, 0:cap].unsqueeze(1).to_broadcast([P, 16, cap]), ALU.is_equal).then_inc(A.mark(), 1)
            end_phase(A)

        def moe_gathers(m_):
            g = [(k, 0, half) for k in range(KD) for half in range(2)]
            if 1 in m_.sides:
                g += [(k, 1, 0) for k in range(KD)]
            return g

        def pe_moe_c(A, m_):
            for j, (k, n, half) in enumerate(moe_gathers(m_)):
                L, _, _, HN, SEL = m_.side(n)[0:5]
                if j >= 4:
                    A.e.wait_ge(S["act_out" if j % 2 == 0 else "dve_out"], (j - 4) // 2 + 1)
                nt = L // P
                for t in range(nt):
                    m = mm(ps[:, j % 4, :], HN[:, t, k * P:(k + 1) * P], SEL[:, t, half * 512:(half + 1) * 512],
                           start=(t == 0), stop=(t == nt - 1))
                m.then_inc(A.mark("psum_full"), 1)
            A.e.wait_ge(S["a_ready"], 1)
            g = 0
            for n in m_.sides:
                L, cap, _, _, SEL = m_.side(n)[0:5]
                for p_ in range(16 * cap // P):
                    if g >= 2:
                        A.e.wait_ge(S["turned_out"], g - 1)
                    for t in range(L // P):
                        m = tr(ps[:, 4 + g % 2, t * P:(t + 1) * P], SEL[:, t, p_ * P:(p_ + 1) * P], IDENT)
                    m.then_inc(A.mark("turned"), 1)
                    g += 1
            end_phase(A)

        def gather_out(m_, j):
            k, n, half = moe_gathers(m_)[j]
            if n == 0:
                return m_.XE[:, k, half * 8:(half + 1) * 8, 0:CAP_L], ps[:, j % 4, :].rearrange("p (e s) -> p e s", s=CAP_L)
            return m_.XE[:, k, :, CAP_L:], ps[:, j % 4, :].rearrange("p (e s) -> p e s", s=CAP_C)

        def act_moe_c(A, m_):
            for j in range(0, len(moe_gathers(m_)), 2):
                A.e.wait_ge(S["psum_full"], j + 1)
                o, i = gather_out(m_, j)
                act(o, i, ACT.Copy).then_inc(A.mark("act_out"), 1)
            g = 0
            for n in m_.sides:
                L, cap = m_.side(n)[0:2]
                G = m_.side(n)[5]
                for p_ in range(16 * cap // P):
                    A.e.wait_ge(S["turned"], g + 1)
                    act(G[:, p_, :], ps[:, 4 + g % 2, 0:L], ACT.Copy).then_inc(A.mark("turned_out"), 1)
                    g += 1
            end_phase(A)

        def dve_moe_c(A, m_):
            n_g = len(moe_gathers(m_))
            for j in range(1, n_g, 2):
                A.e.wait_ge(S["psum_full"], j + 1)
                o, i = gather_out(m_, j)
                nc.vector.tensor_copy(o, i).then_inc(A.mark("dve_out"), 1)
            A.e.wait_ge(S["psum_full"], n_g)
            for n in m_.sides:
                L, cap, t0, _, SEL = m_.side(n)[0:5]
                for t in range(L // P):
                    x = SEL[:, t, :].rearrange("p (e s) -> p e s", s=cap)
                    tt(x, x, AFF[:, t0 + t, :].unsqueeze(2).to_broadcast([P, 16, cap]), ALU.mult).then_inc(A.mark(), 1)
            A.e.wait_ge(*A.last)
            nc.vector.memset(MISC[:, 3:4], 0.0).then_inc(A.mark("a_ready"), 1)
            end_phase(A)

        def pe_moe_d(A, m_, st):
            S_ = m_.S
            for e in range(EB):
                XS = m_.XS[e % 2]
                A.e.wait_ge(S["a_ready"], e + 1)
                for q in range(4):
                    half, up = q // 2, q % 2
                    s = st.get()
                    if e:
                        A.e.wait_ge(S["c_ready"], 2 * (e - 1) + half + 1)
                    for k in range(KD):
                        m = mm(ps[0:S_, q, :], XS[:, k, :], Wc[s][:, k, :], start=(k == 0), stop=(k == KD - 1))
                    m.then_inc(A.mark("psum_full"), 1)
                    st.done(A)
                    if q == 2:
                        pe_turn(A, m_, e, 0)
                s = st.get()
                if e:
                    A.e.wait_ge(S["e_ready"], 2 * (e - 1) + 1)
                    if m_.layer == 0:
                        A.e.wait_ge(S["f_ready"], 2 * (e - 1) + 1)
                A.e.wait_ge(S["turned_out"], 2 * e + 1)
                for k in range(4):
                    mm(ps[0:S_, 6, :], m_.AT[:, k, :], Wc[s][:, k, :], start=(k == 0), stop=False)
                pe_turn(A, m_, e, 1)
                A.e.wait_ge(S["turned_out"], 2 * e + 2)
                for k in range(4, KD):
                    m = mm(ps[0:S_, 6, :], m_.AT[:, k, :], Wc[s][:, k, :], start=False, stop=(k == KD - 1))
                m.then_inc(A.mark("o_full"), 1)
                st.done(A)
                s = st.get()
                if e:
                    A.e.wait_ge(S["e_ready"], 2 * (e - 1) + 2)
                    if m_.layer == 0:
                        A.e.wait_ge(S["f_ready"], 2 * (e - 1) + 2)
                for k in range(KD):
                    m = mm(ps[0:S_, 7, :], m_.AT[:, k, :], Wc[s][:, k, :], start=(k == 0), stop=(k == KD - 1))
                m.then_inc(A.mark("o_full"), 1)
                st.done(A)
            end_phase(A)

        def pe_turn(A, m_, e, half):
            A.e.wait_ge(S["c_ready"], 2 * e + half + 1)
            for k in range(4):
                m = tr(ps[:, 4 + half, k * m_.S:(k + 1) * m_.S], m_.A[:, half * 512 + k * P:half * 512 + (k + 1) * P],
                       IDENT[0:m_.S, 0:m_.S])
            m.then_inc(A.mark("turned"), 1)

        def act_moe_d(A, m_, i):
            S_ = m_.S
            YE = m_.side(0)[6]

            def silu(e, half):
                A.e.wait_ge(S["psum_full"], 4 * e + 2 * half + 1)
                if e:
                    A.e.wait_ge(S["turned"], 2 * (e - 1) + half + 1)
                act(m_.A[:, half * 512:(half + 1) * 512], ps[0:S_, 2 * half, :], ACT.Silu).then_inc(A.mark("b_ready"), 1)

            def at(e, half):
                A.e.wait_ge(S["turned"], 2 * e + half + 1)
                if e and half == 0:
                    A.e.wait_ge(S["o_full"], 2 * e)
                act(m_.AT[:, half * 4:(half + 1) * 4, :],
                           ps[:, 4 + half, 0:4 * S_].rearrange("p (k s) -> p k s", s=S_), ACT.Copy).then_inc(A.mark("turned_out"), 1)

            def y_out(e, dh):
                A.e.wait_ge(S["o_full"], 2 * e + dh + 1)
                r = 64 * (e % 2)
                dst = YE[r:r + 64, bass.ds(i * (EB // 2) + e // 2, 1), dh * 512:(dh + 1) * 512]
                act(dst.rearrange("p o n -> p (o n)"), ps[0:64, 6 + dh, :], ACT.Copy).then_inc(A.mark("e_ready"), 1)

            for e in range(EB):
                silu(e, 0)
                silu(e, 1)
                at(e, 0)
                at(e, 1)
                y_out(e, 0)
                y_out(e, 1)
            end_phase(A)

        def dve_moe_d(A, m_, i):
            S_ = m_.S

            def tokens(e):
                if e >= 2:
                    A.e.wait_ge(S["psum_full"], 4 * (e - 1))
                src = m_.XE[:, :, bass.ds(i * EB + e, 1), :].rearrange("p k o s -> p k (o s)")
                nc.vector.tensor_copy(m_.XS[e % 2], src).then_inc(A.mark("a_ready"), 1)

            tokens(0)
            for e in range(EB):
                for half in range(2):
                    A.e.wait_ge(S["b_ready"], 2 * e + half + 1)
                    A.e.wait_ge(S["psum_full"], 4 * e + 2 * half + 2)
                    x = m_.A[:, half * 512:(half + 1) * 512]
                    tt(x, x, ps[0:S_, 2 * half + 1, :], ALU.mult).then_inc(A.mark("c_ready"), 1)
                    if half == 0 and e + 1 < EB:
                        tokens(e + 1)
                if m_.layer == 0:
                    YC = m_.side(1)[6]
                    r = 32 * (e % 4)
                    for dh in range(2):
                        A.e.wait_ge(S["o_full"], 2 * e + dh + 1)
                        dst = YC[r:r + 32, bass.ds(i, 1), dh * 512:(dh + 1) * 512].rearrange("p o n -> p (o n)")
                        nc.vector.tensor_copy(dst, ps[64:96, 6 + dh, :]).then_inc(A.mark("f_ready"), 1)
            end_phase(A)

        def pe_moe_e(A, m_):
            j = 0
            for n in m_.sides:
                L, cap, _, _, _, G, YE = m_.side(n)
                npair = 16 * cap // P
                for k in range(KD):
                    if j >= 4:
                        A.e.wait_ge(S["dve_out"], j - 3)
                    for p_ in range(npair):
                        m = mm(ps[:, j % 4, 0:L], YE[:, p_, k * P:(k + 1) * P], G[:, p_, :],
                               start=(p_ == 0), stop=(p_ == npair - 1))
                    m.then_inc(A.mark("psum_full"), 1)
                    j += 1
            end_phase(A)

        def dve_moe_e(A, m_):
            j = 0
            for n in m_.sides:
                L, X, _ = side(n)
                for k in range(KD):
                    A.e.wait_ge(S["psum_full"], j + 1)
                    stt(X[:, k, :], ps[:, j % 4, 0:L], mod(m_.layer, 5, k, n), X[:, k, :], ALU.mult, ALU.add).then_inc(A.mark("dve_out"), 1)
                    j += 1
            end_phase(A)

        wm = Map(AR_)
        QS_, K2_, VS_, PT_, PP_, OS_ = (wm.take(4096), wm.take(4 * 768), wm.take(6 * 256), wm.take(2 * 2560),
                                        wm.take(3 * 640), wm.take(4096))
        AX_, AP_, MK_, RT2_ = wm.take(1024), wm.take(P), wm.take(512), wm.take(1024)
        assert wm.at <= AR_END
        QS, K2, VS = v(QS_, 8, 512), v(K2_, 4, 768), v(VS_, 6, 256)
        PT = [v(PT_ + i * 2560, 5, 4, P) for i in range(2)]
        PW = [v(PP_ + i * 640, 640) for i in range(3)]
        OS = v(OS_, 8, 512)
        AXT, APM, WMASK = v(AX_, 2, 512), v(AP_, P), v(MK_, 4, P)
        SQW = lambda L: v(PT_, KD, L)
        SWT = [("q", 0, t) for t in range(8)] + [("k", n, t) for n in (0, 1) for t in range(2)] + \
              [("v", 0, t) for t in range(4)] + [("v", 1, t) for t in range(2)]

        def act_sw_a(A):
            e = A.e
            for dst, src in ((v(AX_, 1024), a["k_axial"][:, 0:1024]), (APM, a["k_axial"][:, 1024:1152]),
                             (v(MK_, 512), a["k_masks"])):
                e.dma_start(dst, src).then_inc(S["const_in"], 16)
            for n in (0, 1):
                L = side(n)[0]
                act_mod_norm(A, n, SQW(L), v(RT2_ + 512 * n, L), 1, 0, n + 1)
            for j, (w, n, t) in enumerate(SWT):
                if j % 2:
                    continue
                A.e.wait_ge(S["psum_full"], j + 1)
                for i, (dst, src, sc) in enumerate(sw_dests(j)):
                    last = i == len(sw_dests(j)) - 1
                    act(dst, src, ACT.Copy, scale=sc).then_inc(A.mark("act_out" if last else None), 1)
            A.e.wait_ge(S["const_in"], 48)
            end_phase(A)

        def sw_dests(j):
            w, n, t = SWT[j]
            L = (T, TC)[n]
            b = ps[:, j % 4, :]
            if w == "q":
                return [(QS[:, t, :], b, 0.125)]
            if w == "v":
                return [(VS[:, (2 + t) if n == 0 else t, :], b[:, 0:256], 1.0)]
            lo = TC if n == 0 else 0
            return [(K2[r:r + 64, 2 * t + s, lo:lo + L], ps[64 * s:64 * s + 64, j % 4, 0:L], 1.0)
                    for s in range(2) for r in (0, 64)]

        def pe_sw_a(A, st):
            for n in (0, 1):
                L = side(n)[0]
                pe_norm(A, SQW(L), L, 7, n + 1)
            A.e.wait_ge(S["h_ready"], 2)
            for j, (w, n, t) in enumerate(SWT):
                L, _, H = side(n)
                if j in (0, 4, 8):
                    s = st.get()
                if j >= 4:
                    A.e.wait_ge(S["act_out" if j % 2 == 0 else "dve_out"], (j - 4) // 2 + 1)
                for k in range(KD):
                    if w == "v":
                        m = mm(ps[:, j % 4, 0:256], H[:, k, t * P:(t + 1) * P], Wc[s][:, k, 256:512],
                               start=(k == 0), stop=(k == KD - 1))
                    else:
                        c = t % 4
                        m = mm(ps[:, j % 4, 0:L], Wc[s][:, k, c * P:(c + 1) * P], H[:, k, :],
                               start=(k == 0), stop=(k == KD - 1))
                m.then_inc(A.mark("psum_full"), 1)
                if j in (3, 7, len(SWT) - 1):
                    st.done(A)
            end_phase(A)

        def dve_sw_a(A):
            for n in (0, 1):
                L = side(n)[0]
                dve_mod_norm(A, n, v(RT2_ + 512 * n, L), 1, 0, "norm1", n + 1)
            ts(MISC[:, 80:96], gv("sink", 0, 16), -1.0, None, ALU.mult).then_inc(A.mark(), 1)
            for j, (w, n, t) in enumerate(SWT):
                if j % 2 == 0:
                    continue
                A.e.wait_ge(S["psum_full"], j + 1)
                for i, (dst, src, sc) in enumerate(sw_dests(j)):
                    last = i == len(sw_dests(j)) - 1
                    ts(dst, src, sc, None, ALU.mult).then_inc(A.mark("dve_out" if last else None), 1)
            end_phase(A)

        SW_ROPE = [QS[:, t, :] for t in range(8)] + [K2[:, g, TC:TC + T] for g in range(4)]

        def pe_sw_b(A):
            for j, x in enumerate(SW_ROPE):
                if j >= 4:
                    A.e.wait_ge(S["dve_out"], j - 3)
                mm(ps[:, j % 4, :], APM, x, start=True, stop=True).then_inc(A.mark("psum_full"), 1)
            end_phase(A)

        def dve_sw_b(A):
            r2 = [v(RT2_, 512), v(RT2_ + 512, 512)]
            for j, x in enumerate(SW_ROPE):
                A.e.wait_ge(S["psum_full"], j + 1)
                tt(r2[j % 2], ps[:, j % 4, :], AXT[:, 1, :], ALU.mult).then_inc(A.mark("dve_out"), 1)
                tt(x, x, AXT[:, 0, :], ALU.mult).then_inc(A.mark(), 1)
                A.e.wait_ge(*A.last)
                A.e.wait_ge(S["dve_out"], j + 1)
                tt(x, x, r2[j % 2], ALU.add).then_inc(A.mark(), 1)
            end_phase(A)

        SU = [(g, i, r) for g in range(4) for i in range(NQ) for r in range(4)]

        def window(i):
            return list(range(max(0, i - 1), min(NQ, i + 2)))

        def pe_sw_c(A):
            for s in range(len(SU) + LAG):
                if s < len(SU):
                    g, i, r = SU[s]
                    if s >= 2:
                        A.e.wait_ge(S["probs"], s - 1)
                    hd, rr = g * 4 + r, 64 * (r % 2)
                    q = QS[rr:rr + 64, hd // 2, i * P:(i + 1) * P]
                    w = window(i)
                    b = 2 * (s % 2)
                    lo = TC + w[0] * P
                    mm(ps[:, b, 0:TC], q, K2[rr:rr + 64, g, 0:TC], start=True, stop=True)
                    m = mm(ps[:, b, TC:512], q, K2[rr:rr + 64, g, lo:lo + 256], start=True, stop=False)
                    if len(w) == 3:
                        mm(ps[:, b + 1, 0:P], q, K2[rr:rr + 64, g, lo + 256:lo + 384], start=True, stop=False)
                    masked = [(x, 3 if kb < i else 2) for x, kb in enumerate(w) if kb != i]
                    for x, msk in masked:
                        bb, cc = (b, TC + x * P) if x < 2 else (b + 1, 0)
                        m = mm(ps[:, bb, cc:cc + P], IDENT, WMASK[:, msk, :], start=False, stop=True)
                    m.then_inc(A.mark("scores"), 1)
                if s >= LAG:
                    u = s - LAG
                    g, i, r = SU[u]
                    nk = 2 + len(window(i))
                    if u >= 2:
                        A.e.wait_ge(S["turned_out"], u - 1)
                    if u:
                        A.e.wait_ge(S["i_ready"], u)
                    A.e.wait_ge(S["weights"], u + 1)
                    for j in range(nk):
                        o = ps[:, 4 + u % 2, j * P:(j + 1) * P] if j < 4 else ps[:, 6, 0:P]
                        m = tr(o, PW[u % 3][:, j * P:(j + 1) * P], IDENT)
                    m.then_inc(A.mark("turned"), 1)
                    if r == 0 and u:
                        pe_sw_pv(A, u // 4 - 1)
            pe_sw_pv(A, len(SU) // 4 - 1)
            end_phase(A)

        def pe_sw_pv(A, gi):
            g, i, _ = SU[4 * gi]
            w = window(i)
            A.e.wait_ge(S["turned_out"], 4 * (gi + 1))
            A.e.wait_ge(S["i_ready"], 4 * (gi + 1))
            if gi >= 2:
                A.e.wait_ge(S["o_out"], gi - 1)
            h = 64 * (gi % 2)
            blocks = [0, 1] + [2 + kb for kb in w]
            for j, kb in enumerate(blocks):
                m = mm(ps[h:h + 64, 7, :], VS[:, kb, g * 64:(g + 1) * 64], PT[gi % 2][:, j, :, :],
                       start=(j == 0), stop=(j == len(blocks) - 1))
            m.then_inc(A.mark("o_full"), 1)

        def act_sw_c(A):
            for s in range(len(SU) + LAG + 1):
                if s < len(SU):
                    g, i, r = SU[s]
                    hd = g * 4 + r
                    wd = (2 + len(window(i))) * P
                    b = 2 * (s % 2)
                    A.e.wait_ge(S["maxima"], s + 1)
                    if s >= 3:
                        A.e.wait_ge(S["turned"], s - 2)
                    nm = MISC[:, 32 + s % 4:33 + s % 4]
                    act(PW[s % 3][:, 0:wd], ps[:, b:b + 2, :].rearrange("p a n -> p (a n)")[:, 0:wd], ACT.Exp,
                               bias=nm, accum_out=MISC[:, 36 + s % 4:37 + s % 4]).then_inc(A.mark(), 1)
                    act(MISC[:, 48 + s % 4:49 + s % 4], gv("sink", hd), ACT.Exp, bias=nm).then_inc(A.mark("probs"), 1)
                if LAG <= s < len(SU) + LAG:
                    u = s - LAG
                    g, i, r = SU[u]
                    gi = u // 4
                    A.e.wait_ge(S["turned"], u + 1)
                    if r == 0 and gi >= 2:
                        A.e.wait_ge(S["o_full"], gi - 1)
                    act(PT[gi % 2][:, 0:4, r, :], ps[:, 4 + u % 2, :].rearrange("p (j q) -> p j q", q=P),
                               ACT.Copy).then_inc(A.mark("turned_out"), 1)
            end_phase(A)

        def dve_sw_c(A):
            def evac_o(gi):
                g, i, _ = SU[4 * gi]
                A.e.wait_ge(S["o_full"], gi + 1)
                h = 64 * (gi % 2)
                src = ps[h:h + 64, 7, :].rearrange("p (a b q) -> p a b q", a=2, b=2)
                for rp in range(2):
                    nc.vector.tensor_copy(OS[64 * rp:64 * rp + 64, 2 * g:2 * g + 2, i * P:(i + 1) * P],
                                                 src[:, :, rp, :]).then_inc(A.mark("o_out" if rp else None), 1)

            for s in range(len(SU) + LAG + 2):
                if s < len(SU):
                    g, i, r = SU[s]
                    wd = (2 + len(window(i))) * P
                    b = 2 * (s % 2)
                    nm = MISC[:, 32 + s % 4:33 + s % 4]
                    A.e.wait_ge(S["scores"], s + 1)
                    nc.vector.tensor_reduce(nm, ps[:, b:b + 2, :].rearrange("p a n -> p (a n)")[:, 0:wd], AX_X,
                                                   ALU.max, negate=True).then_inc(A.mark(), 1)
                    A.e.wait_ge(*A.last)
                    tt(nm, nm, MISC[:, 80 + g * 4 + r:81 + g * 4 + r], ALU.min).then_inc(A.mark("maxima"), 1)
                if 1 <= s <= len(SU):
                    u = s - 1
                    wd = (2 + len(window(SU[u][1]))) * P
                    A.e.wait_ge(S["probs"], u + 1)
                    sm, es = MISC[:, 36 + u % 4:37 + u % 4], MISC[:, 48 + u % 4:49 + u % 4]
                    tt(sm, sm, es, ALU.add).then_inc(A.mark(), 1)
                    A.e.wait_ge(*A.last)
                    nc.vector.reciprocal(sm, sm).then_inc(A.mark(), 1)
                    A.e.wait_ge(*A.last)
                    ts(PW[u % 3][:, 0:wd], PW[u % 3][:, 0:wd], sm, None, ALU.mult).then_inc(A.mark("weights"), 1)
                if LAG + 0 <= s - 0 and s - LAG < len(SU):
                    u = s - LAG
                    g, i, r = SU[u]
                    gi = u // 4
                    A.e.wait_ge(S["turned"], u + 1)
                    if r == 0 and gi >= 2:
                        A.e.wait_ge(S["o_full"], gi - 1)
                    if len(window(i)) == 3:
                        ins = nc.vector.tensor_copy(PT[gi % 2][:, 4, r, :], ps[:, 6, 0:P])
                    else:
                        ins = nc.vector.memset(MISC[:, 5:6], 0.0)
                    ins.then_inc(A.mark("i_ready"), 1)
                if s >= LAG + 4 and (s - LAG) % 4 == 1 and (s - LAG) // 4 - 1 < len(SU) // 4 - 1:
                    evac_o((s - LAG) // 4 - 1)
            evac_o(len(SU) // 4 - 1)
            end_phase(A)

        def act_final(A):
            act_norm(A, XT, v(AR_, KD, T), v(AR_ + 4096, T), T, 7, 1)
            A.e.wait_ge(S["a_ready"], 1)
            A.e.dma_start(out, HTL).then_inc(S["stored"], 16)
            A.e.wait_ge(S["stored"], 16)

        def dve_final(A):
            dve_recip(A, v(AR_ + 4096, T), 1)
            for k in range(KD):
                stt(HTL[:, k, :], XT[:, k, :], gv("final", k), v(AR_ + 4096, T), ALU.mult, ALU.mult)\
                    .then_inc(A.mark("a_ready" if k == KD - 1 else None), 1)

        HYENAS = [Hy(0), Hy(1)]
        MOES = [Moe(0), Moe(1)]
        H_PHASES = 4
        TURNS = N_EXP // EB

        @block.sync
        def _(sp):
            st = Stream(sp)

            def experts(layer):
                with sp.Fori(0, TURNS) as i:
                    st.enter(i, 6 * EB)
                    for e in range(EB):
                        g, u, dn = (a[n][layer][bass.ds(i * EB + e, 1)].rearrange("o r n -> (o r) n")
                                    for n in ("moe_w_gate_2", "moe_w_up_2", "moe_w_down_2"))
                        for c in range(2):
                            st.load(cols(g, c))
                            st.load(cols(u, c))
                        for c in range(2):
                            st.load(cols(dn, c))
                st.leave(TURNS)

            for l in range(DEPTH):
                for c in range(12):
                    st.load(cols(a["ada_w_2"][l], c))
            with sp.Fori(0, DEPTH) as l:
                st.enter(l, N_HYB)
                wi = a["w_in"][bass.ds(l, 1)].rearrange("o r n -> (o r) n")
                wo = a["w_out"][bass.ds(l, 1)].rearrange("o r n -> (o r) n")
                for c in range(12):
                    st.load(cols(wi, c))
                for c in range(3):
                    st.load(wo[c * 512:(c + 1) * 512, :].rearrange("(k p) n -> p k n", p=P), Wr)
            st.leave(DEPTH)
            for _y in HYENAS:
                for c in range(6):
                    st.load(cols(a["hy_w_in_2"], c))
                for c in range(2):
                    st.load(cols(a["hy_w_out_2"], c))
            experts(0)
            for c in range(3):
                st.load(cols(a["sw_w_in_2"], c))
            for c in range(2):
                st.load(cols(a["sw_w_out_2"], c))
            experts(1)

        @block.tensor
        def _(e):
            A = Engine(e, "pe", S)
            st = Stream(e)

            def moe(m_):
                pe_moe_a(A, m_)
                pe_moe_b(A, m_)
                pe_moe_c(A, m_)
                with e.Fori(0, TURNS) as i:
                    A.loop = (i, 1)
                    st.enter(i, 6 * EB)
                    pe_moe_d(A, m_, st)
                A.leave(TURNS)
                st.leave(TURNS)
                pe_moe_e(A, m_)

            pe_setup(A, st)
            with e.Fori(0, DEPTH) as l:
                A.loop = (l, H_PHASES)
                st.enter(l, N_HYB)
                pe_hyb_proj(A, st)
                pe_hyb_rope(A)
                pe_attn(A)
                pe_hyb_out(A, st)
            A.leave(DEPTH)
            st.leave(DEPTH)
            end_phase(A)
            for y in HYENAS:
                pe_hy_a(A, y, st)
                for c in range(2):
                    for o in range(2):
                        pe_hy_b(A, y, c, o)
                pe_proj_out(A, st, y.U3, y.L)
            moe(MOES[0])
            pe_sw_a(A, st)
            pe_sw_b(A)
            pe_sw_c(A)
            pe_proj_out(A, st, OS, T)
            moe(MOES[1])
            pe_norm(A, v(AR_, KD, T), T, 7, 1)

        @block.scalar
        def _(e):
            A = Engine(e, "act", S)

            def moe(m_):
                act_moe_a(A, m_)
                act_moe_b(A, m_)
                act_moe_c(A, m_)
                with e.Fori(0, TURNS) as i:
                    A.loop = (i, 1)
                    act_moe_d(A, m_, i)
                A.leave(TURNS)
                end_phase(A)

            act_setup(A)
            with e.Fori(0, DEPTH) as l:
                A.loop = (l, H_PHASES)
                act_hyb_proj(A, l)
                act_hyb_rope(A)
                act_attn(A)
                act_hyb_out(A)
            A.leave(DEPTH)
            e.dma_start(CT, a["ctx"]).then_inc(S["const_in"], 16)
            e.wait_ge(S["const_in"], 16)
            end_phase(A)
            for y in HYENAS:
                act_hy_a(A, y)
                for c in range(2):
                    for o in range(2):
                        act_hy_b(A, y, c, o)
                end_phase(A)
            moe(MOES[0])
            act_sw_a(A)
            end_phase(A)
            act_sw_c(A)
            end_phase(A)
            moe(MOES[1])
            act_final(A)

        @block.vector
        def _(e):
            A = Engine(e, "dve", S)

            def moe(m_):
                dve_moe_a(A, m_)
                dve_moe_b(A, m_)
                dve_moe_c(A, m_)
                with e.Fori(0, TURNS) as i:
                    A.loop = (i, 1)
                    dve_moe_d(A, m_, i)
                A.leave(TURNS)
                dve_moe_e(A, m_)

            dve_setup(A)
            with e.Fori(0, DEPTH) as l:
                A.loop = (l, H_PHASES)
                dve_hyb_proj(A, l)
                dve_hyb_rope(A)
                dve_attn(A)
                dve_hyb_out(A)
            A.leave(DEPTH)
            end_phase(A)
            for y in HYENAS:
                dve_hy_a(A, y)
                for c in range(2):
                    for o in range(2):
                        dve_hy_b(A, y, c, o)
                dve_proj_out(A, y.n, v(T_, y.L), 0, "hy_b_out")
            moe(MOES[0])
            dve_sw_a(A)
            dve_sw_b(A)
            dve_sw_c(A)
            dve_proj_out(A, 0, None, 1, None)
            moe(MOES[1])
            dve_final(A)

        @block.gpsimd
        def _(e):
            A = Engine(e, "pool", S)
            open_next_phase(A)
            with e.Fori(0, DEPTH) as l:
                for _p in range(H_PHASES):
                    open_next_phase(A)
            for _p in range(1 + 2 * (1 + 4 + 1)):
                open_next_phase(A)
            for layer in range(2):
                for _p in range(3):
                    open_next_phase(A)
                with e.Fori(0, TURNS) as i:
                    open_next_phase(A)
                open_next_phase(A)
                if layer == 0:
                    for _p in range(4):
                        open_next_phase(A)


def pack_vectors(inp):
    f = lambda x: np.asarray(x, np.float32)
    col = lambda x: f(x).reshape(-1, P).T

    def short(x):
        x = f(x)
        o = np.zeros((P, x.shape[-1]), np.float32)
        o[:x.shape[0]] = x
        return o

    lvs = []
    for l in range(DEPTH):
        li = 0.8 - 0.6 * math.exp(-0.3 * l)
        parts = {
            "g_pre": col(inp["pre_norm"][l]), "g_post": col(inp["post_norm"][l]), "subln": col(inp["diff_subln"][l]),
            "lam_vec": short(f(inp["diff_lambda"][l]).T), "f_bias": short(f(inp["forget_bias"][l])[:, None]),
            "lam_init": np.full((P, 1), li, np.float32), "one_minus": np.full((P, 1), 1.0 - li, np.float32),
        }
        lvs.append(np.concatenate([parts[n] for n in LAYER_COLS], axis=1))
    cc = np.stack([col(inp["c_2"][0]), col(inp["c_ctx_2"])], axis=2).reshape(P, -1)
    one0 = np.zeros((P, 1), np.float32)
    one0[0] = 1
    dft = lambda L: np.concatenate([np.where(one0 > 0, 1.0, 2.0) / (2 * L), np.full((P, 1), 2.0) / (2 * L)], axis=1)
    g = {
        "c": cc, "ada_b": np.concatenate([col(inp["ada_b_2"][l]) for l in range(2)], axis=1),
        "norm1": np.concatenate([col(inp["norm1_w_2"][l]) for l in range(2)], axis=1),
        "norm2": np.concatenate([col(inp["norm2_w_2"][l]) for l in range(2)], axis=1),
        "final": col(inp["final_norm_w_2"]), "hy_b_in": col(inp["hy_b_in_2"]),
        "hy_sw": np.concatenate([col(inp["hy_short_w_2"][i]) for i in range(3)], axis=1),
        "hy_sb": col(inp["hy_short_b_2"]), "hy_b_out": col(inp["hy_b_out_2"]),
        "ffn_b1": short(f(inp["hy_ffn_b1_2"])[:, None]), "ffn_b2": short(f(inp["hy_ffn_b2_2"])[:, None]),
        "freq": short(f(inp["hy_sin_freq_2"]).T), "sink": np.broadcast_to(f(inp["sw_sink_2"])[None], (P, 16)),
        "not0": 1 - one0, "is0": one0, "dft_l": dft(T), "dft_c": dft(TC),
    }
    gvec = np.concatenate([g[n] for n in GLOBAL_COLS], axis=1)
    return (np.ascontiguousarray(gvec, dtype=np.float32),
            np.ascontiguousarray(np.concatenate(lvs, axis=1), dtype=np.float32))


WEIGHTS = ["w_in", "w_out", "ada_w_2", "hy_w_in_2", "hy_ffn_w1_2", "hy_ffn_w2_2", "hy_ffn_w3_2", "hy_filter_bias_2",
           "hy_w_out_2", "sw_w_in_2", "sw_w_out_2", "moe_router_2", "moe_w_gate_2", "moe_w_up_2", "moe_w_down_2"]


def transposed(x):
    return np.ascontiguousarray(np.asarray(x, np.float32).T.reshape(KD, P, -1).transpose(1, 0, 2))


def prepare(inputs):
    gvec, lvec = pack_vectors(inputs)
    arrays = {n: np.ascontiguousarray(np.asarray(inputs[n])) for n in WEIGHTS}
    arrays["x"] = transposed(inputs["x"][0])
    arrays["ctx"] = transposed(inputs["ctx_2"][0])
    arrays["k_gvec"], arrays["k_lvec"] = gvec, lvec
    for n, x in shape_constants().items():
        arrays["k_" + n] = np.ascontiguousarray(x)
    return arrays


def kernel(**inputs):
    import concourse.bacc as bacc
    from concourse.bass_utils import run_bass_kernel_spmd

    arrays = prepare(inputs)
    nc = bacc.Bacc("TRN2", target_bir_lowering=False, num_devices=1)
    aps = {n: nc.dram_tensor("in_" + n, x.shape, F32, kind="ExternalInput").ap() for n, x in arrays.items()}
    out = nc.dram_tensor("out_x", (P, KD, T), F32, kind="ExternalOutput").ap()
    build(nc, aps, out)
    r = run_bass_kernel_spmd(nc, [{"in_" + n: x for n, x in arrays.items()}], core_ids=[0])
    o = np.asarray(r.results[0]["out_x"])
    return np.ascontiguousarray(o.transpose(2, 1, 0).reshape(1, T, D))
```

```python
from contextlib import ExitStack
import math

import numpy as np
import concourse.bass as bass
from concourse import mybir

F32 = mybir.dt.float32
BF16 = mybir.dt.bfloat16
ALU = mybir.AluOpType
ACT = mybir.ActivationFunctionType
AX_X = mybir.AxisListType.X

P = 128
D = 1024
KD = D // P
T = 512
TC = 256
DEPTH = 2
NQ = T // P
EPS = 1e-6
NEG = -1e30
N_EXP = 16
CAP_L = 2 * T // N_EXP
CAP_C = 2 * TC // N_EXP
TWO_PI = 2 * math.pi

WSLOTS = 6
WCH = 2048

LAYER_COLS = {}
GLOBAL_COLS = {}


def _cols(table, spec):
    at = 0
    for name, n in spec:
        table[name] = (at, n)
        at += n
    return at


N_LV = _cols(LAYER_COLS, [("g_pre", KD), ("g_post", KD), ("subln", 1), ("lam_vec", 4), ("f_bias", 1),
                          ("lam_init", 1), ("one_minus", 1), ("ada_b", 48)])
N_GV = _cols(GLOBAL_COLS, [("c", 2 * KD), ("pick", 2), ("norm1", 2 * KD), ("norm2", 2 * KD), ("final", KD),
                           ("hy_b_in", 24), ("hy_sw", 72), ("hy_sb", 24), ("hy_b_out", KD),
                           ("ffn_b1", 1), ("ffn_b2", 1), ("freq", 2), ("sink", 16),
                           ("not0", 1), ("is0", 1), ("dft_l", 2), ("dft_c", 2)])


def shape_constants():
    c = {}
    c["ident"] = np.eye(P, dtype=np.float32)
    i, j = np.arange(P)[:, None], np.arange(P)[None, :]
    m = lambda ok: np.where(ok, 0.0, NEG).astype(np.float32)
    c["masks"] = np.concatenate([m(j // 64 <= i // 64), m(j < i), m(j <= i), m(j >= i)], axis=1)
    inv = np.float32(500000.0) ** (-np.arange(0, 16, 2, dtype=np.float32) / np.float32(16))
    ang = (np.arange(T, dtype=np.float32)[:, None] * inv[None, :]).astype(np.float32)
    cos, sin = np.cos(ang).T, np.sin(ang).T
    rc, rs = np.ones((64, T), np.float32), np.zeros((64, T), np.float32)
    rc[0:8], rc[8:16], rs[0:8], rs[8:16] = cos, cos, -sin, sin
    perm = np.zeros((64, 64), np.float32)
    for a in range(8):
        perm[a, a + 8] = perm[a + 8, a] = 1
    two = lambda a: np.concatenate([a, a], axis=0)
    blk = lambda a: np.block([[a, np.zeros_like(a)], [np.zeros_like(a), a]]).astype(np.float32)
    c["rope"] = np.concatenate([two(rc), two(rs), blk(perm)], axis=1)
    row = np.repeat(np.arange(T // 64, dtype=np.float32), 64)
    col = np.tile(np.arange(64, dtype=np.float32), T // 64)
    inv = np.float32(10000.0) ** (-np.arange(16, dtype=np.float32) / np.float32(16))
    ang = np.concatenate([row[:, None] * inv, col[:, None] * inv], axis=-1).astype(np.float32)
    cos, sin = np.cos(ang).T, np.sin(ang).T
    perm = np.zeros((64, 64), np.float32)
    for a in range(32):
        perm[a, a + 32] = perm[a + 32, a] = 1
    c["axial"] = np.concatenate([two(np.concatenate([cos, cos])), two(np.concatenate([-sin, sin])), blk(perm)],
                                axis=1).astype(np.float32)
    f = np.arange(T)
    th = 2 * np.pi * ((f[:, None] * f[None, :]) % (2 * T)) / (2 * T)
    tiled = lambda a: a.reshape(-1, P, a.shape[1]).transpose(1, 0, 2).reshape(P, -1)
    c["dft"] = np.concatenate([tiled(np.cos(th)), tiled(-np.sin(th))], axis=1).astype(np.float32)
    for n, L in (("l", T), ("c", TC)):
        t = np.arange(L)
        g = np.arange(P)
        th = 2 * np.pi * ((t[:, None] * g[None, :]) % (2 * L)) / (2 * L)
        fw = -np.sin(th)
        fw[:, 0] = np.where(t % 2, -1.0, 1.0)
        ny = np.zeros((L, P))
        ny[:, 0] = 2 * fw[:, 0]
        c[f"fs0_{n}"] = tiled(fw).astype(np.float32)
        c[f"gs0_{n}"] = np.ascontiguousarray(fw.T).astype(np.float32)
        c[f"nyq_{n}"] = tiled(ny).astype(np.float32)
        tt = np.linspace(0.0, 1.0, L, dtype=np.float32)[:, None]
        w = (np.float32(2.0 * math.pi) * np.arange(L, dtype=np.float32)[:, None] / np.float32(L)).astype(np.float32)
        fr = np.linspace(1e-4, 15, 16, dtype=np.float32)[None, :]
        fw_ = (fr * w).astype(np.float32)
        z = np.concatenate([tt, np.cos(fw_), -np.sin(fw_)], axis=-1)
        c[f"pos_{n}"] = np.ascontiguousarray(z.T).astype(np.float32)
        deltas = np.abs(np.linspace(math.log(1e-2) / 1.5, math.log(1e-2) / 0.3, D, dtype=np.float32))
        c[f"win_{n}"] = (np.exp(-tt * deltas) + np.float32(0.05)).astype(np.float32)
    pair = np.zeros((P, 2 * CAP_C), np.float32)
    for q in range(4):
        pair[q * CAP_C:(q + 1) * CAP_C, (q // 2) * CAP_C:(q // 2 + 1) * CAP_C] = np.eye(CAP_C)
    c["pair"] = pair
    c["iota"] = np.broadcast_to(np.arange(CAP_L, dtype=np.float32), (P, CAP_L)).copy()
    return c


class Map:
    def __init__(self, at=0):
        self.at = at

    def take(self, n):
        a = self.at
        self.at += n
        return a


class Engine:

    def __init__(self, e, name, sems):
        self.e, self.name, self.sems = e, name, sems
        self.counts = {}
        self.last = None
        self.phase = 0
        self.loop = None

    def mark(self, sem=None):
        sem = sem or f"{self.name}_step"
        self.counts[sem] = self.counts.get(sem, 0) + 1
        self.last = (self.sems[sem], self.counts[sem])
        return self.sems[sem]

    def opened(self):
        self.phase += 1
        self.counts = {}
        self.last = None
        return self.phase if self.loop is None else self.loop[0] * self.loop[1] + self.phase

    def leave(self, turns):
        self.phase += self.loop[1] * (turns - 1)
        self.loop = None


def end_phase(A):
    if A.last:
        A.e.wait_ge(*A.last)
    A.e.sem_inc(A.sems["arrived"], 1)
    A.e.wait_ge(A.sems["phase_open"], A.opened())
    A.e.sem_inc(A.sems["resumed"], 1)


def open_next_phase(A):
    A.e.wait_ge(A.sems["arrived"], 3)
    first, last = A.sems["_range"]
    A.e.sem_clear(range(first, last + 1))
    A.e.sem_inc(A.sems["phase_open"], 1)


def nth(who, t):
    return sum(1 for x in who[:t + 1] if x == who[t])


PHASE_SEMS = ["arrived", "pe_step", "act_step", "dve_step", "pool_step",
              "const_in", "const2_in", "psum_full", "act_out", "dve_out", "squares", "squares_v", "stat", "rstd", "scaled", "h_ready",
              "scores", "maxima", "probs", "weights", "turned", "turned_out", "o_full", "o_out",
              "a_ready", "b_ready", "c_ready", "d_ready", "e_ready", "f_ready", "g_ready",
              "ctx_full", "ctx_out", "ctx_turned", "ctx_silu", "ctx_hidden", "ctx_o_full", "ctx_o_out",
              "i_ready", "j_ready", "k_ready", "m_ready", "n_ready"]


def build(nc, a, out):
    with ExitStack() as ctx:
        S = {}
        S["phase_open"] = ctx.enter_context(nc.semaphore("phase_open"))
        S["resumed"] = ctx.enter_context(nc.semaphore("resumed"))
        for i in range(WSLOTS):
            S[f"w_in{i}"] = ctx.enter_context(nc.semaphore(f"w_in{i}"))
        S["w_used"] = ctx.enter_context(nc.semaphore("w_used"))
        S["ff_in"] = ctx.enter_context(nc.semaphore("ff_in"))
        S["stored"] = ctx.enter_context(nc.semaphore("stored"))
        nums = []
        for n in PHASE_SEMS:
            S[n] = ctx.enter_context(nc.semaphore(n))
            nums.append(S[n].num)
        assert max(nums) - min(nums) == len(nums) - 1
        S["_range"] = (min(nums), max(nums))

        total = Map()
        XT_, CT_, HT_, W_ = total.take(KD * T), total.take(KD * TC), total.take(KD * (T + TC)), total.take(WSLOTS * WCH)
        ID_, ON_, GV_, LV_, LS_, MOD_ = (total.take(P), total.take(P), total.take(N_GV), total.take(N_LV),
                                         total.take(DEPTH * N_LV), total.take(2 * 96))
        MISC_ = total.take(96)
        SC_ = total.take(KD * 32)
        IDB_ = total.take(64)
        AR_ = total.at
        AR_END = 53150
        M = ctx.enter_context(nc.sbuf_tensor("mem", [P, AR_END], F32))
        ps = ctx.enter_context(nc.psum_tensor("ps", [P, 8, 512], F32))

        def v(at, *dims, p=P, p0=0):
            n = int(np.prod(dims))
            x = M[p0:p0 + p, at:at + n]
            if len(dims) == 2:
                x = x.rearrange("p (a b) -> p a b", b=dims[1])
            if len(dims) == 3:
                x = x.rearrange("p (a b c) -> p a b c", b=dims[1], c=dims[2])
            return x

        XT, CT, HT = v(XT_, KD, T), v(CT_, KD, TC), v(HT_, KD, T + TC)
        HTL = v(HT_, KD, T)
        Wh = [v(W_ + i * WCH, 4, 512) for i in range(WSLOTS)]
        Wr2 = [v(W_ + i * WCH, 2, 1024) for i in range(WSLOTS)]
        Wc = [v(W_ + i * WCH, KD, 512) if i % 2 == 0 else None for i in range(WSLOTS)]
        Wr = [v(W_ + i * WCH, 4, 1024) if i % 2 == 0 else None for i in range(WSLOTS)]
        IDENT, ONES = v(ID_, P), v(ON_, P)
        MISC = v(MISC_, 96)
        SC = v(SC_, KD, 32)

        def half_words(at, n):
            return M[:, at:at + n // 2].bitcast(BF16)

        IDB = half_words(IDB_, P)

        def gv(name, i=0, n=1, p=P):
            at = GV_ + GLOBAL_COLS[name][0] + i
            return M[0:p, at:at + n]

        def lv(name, i=0, n=1, p=P):
            at = LV_ + LAYER_COLS[name][0] + i
            return M[0:p, at:at + n]

        def mod(layer, which, k, side):
            at = MOD_ + layer * 96 + (which * KD + k) * 2 + side
            return M[:, at:at + 1]

        block = ctx.enter_context(nc.Block())
        eps_col = MISC[:, 0:1]
        one_col = MISC[:, 1:2]
        mm = nc.tensor.matmul
        tr = nc.tensor.transpose
        act = nc.scalar.activation
        tt, ts, stt = nc.vector.tensor_tensor, nc.vector.tensor_scalar, nc.vector.scalar_tensor_tensor

        class Stream:

            def __init__(self, e):
                self.e, self.n, self.loop = e, 0, None

            def number(self, extra=0):
                if self.loop is None:
                    return self.n + extra
                reg, per = self.loop
                return reg * per + (self.n + extra)

            def enter(self, reg, per):
                assert per % WSLOTS == 0
                self.loop = (reg, per)

            def leave(self, turns):
                per = self.loop[1]
                self.loop = None
                self.n += per * (turns - 1)

            def load_half(self, dst, src):
                s = self.n % WSLOTS
                self.e.wait_ge(S["w_used"], self.number(1))
                self.e.dma_start(dst[s], src).then_inc(S[f"w_in{s}"], 16)
                self.n += 1

            def load(self, src):
                self.load_half(Wh, src[:, 0:4, :])
                self.load_half(Wh, src[:, 4:8, :])

            def get_half(self, extra=0):
                n = self.n + extra
                s = n % WSLOTS
                val = 16 * (n // WSLOTS + 1)
                if self.loop is not None:
                    reg, per = self.loop
                    val = reg * (16 * per // WSLOTS) + val
                self.e.wait_ge(S[f"w_in{s}"], val)
                return s

            def get(self):
                s = self.get_half()
                self.get_half(1)
                return s

            def next(self, halves=2):
                self.n += halves

            def done(self, pe, halves=2):
                self.e.wait_ge(*pe.last)
                self.e.sem_inc(S["w_used"], halves)
                self.n += halves

        def cols(w, c):
            return w[:, c * 512:(c + 1) * 512].rearrange("(k p) n -> p k n", p=P)

        N_HYB = 2 * (12 + 12 + 3)

        EB = 8

        def act_setup(A):
            e = A.e
            loads = [(v(ID_, P), a["k_ident"]), (v(GV_, N_GV), a["k_gvec"]), (v(LS_, DEPTH * N_LV), a["k_lvec"]),
                     (XT, a["x"])]
            for dst, src in loads:
                e.dma_start(dst, src).then_inc(S["const_in"], 16)
            e.wait_ge(S["const_in"], 16 * len(loads))
            e.wait_ge(S["a_ready"], 1)
            act(SC[:, :, 0:2], gv("c", 0, 16).rearrange("p (k s) -> p k s", s=2), ACT.Silu).then_inc(A.mark(), 1)
            for k in range(KD):
                act(SQ[:, k, :], XT[:, k, :], ACT.Square).then_inc(A.mark("squares"), 1)
            end_phase(A)

        def dve_setup(A):
            nc.vector.memset(v(SC_, KD * 32), 0.0).then_inc(A.mark("a_ready"), 1)
            nc.vector.memset(ONES, 1.0).then_inc(A.mark("a_ready"), 1)
            nc.vector.memset(MISC[:, 0:1], EPS).then_inc(A.mark(), 1)
            nc.vector.memset(MISC[:, 1:2], 1.0).then_inc(A.mark(), 1)
            nc.vector.memset(MISC[:, 2:3], 0.0).then_inc(A.mark(), 1)
            A.e.wait_ge(S["const_in"], 64)
            nc.vector.tensor_copy(IDB, IDENT).then_inc(A.mark(), 1)
            end_phase(A)

        def act_norm(A, src, sq, rs, n, bank, turn):
            for k in range(0, KD, 2):
                act(sq[:, k, :], src[:, k, :], ACT.Square).then_inc(A.mark("squares"), 1)
            A.e.wait_ge(S["stat"], turn)
            act(rs, ps[:, bank, 0:n], ACT.Sqrt, bias=eps_col, scale=1.0 / D).then_inc(A.mark("rstd"), 1)

        def dve_squares(A, src, sq):
            for k in range(1, KD, 2):
                tt(sq[:, k, :], src[:, k, :], src[:, k, :], ALU.mult).then_inc(A.mark("squares_v"), 1)

        def pe_norm(A, sq, n, bank, turn):
            for k in range(KD):
                A.e.wait_ge(S["squares_v" if k % 2 else "squares"], (turn - 1) * 4 + k // 2 + 1)
                m = mm(ps[:, bank, 0:n], ONES, sq[:, k, :], start=(k == 0), stop=(k == KD - 1))
            m.then_inc(A.mark("stat"), 1)

        def dve_recip(A, rs, turn):
            A.e.wait_ge(S["rstd"], turn)
            nc.vector.reciprocal(rs, rs).then_inc(A.mark(), 1)
            A.e.wait_ge(*A.last)

        hm = Map(AR_)
        QT_ = hm.take(12 * 512)
        KT_ = hm.take(12 * 512)
        GT_ = hm.take(12 * 512)
        VN_ = hm.take(12 * 512)
        MASK_ = hm.take(4 * P // 2)
        PERM_ = hm.take(P)
        TMP_ = hm.take(1100)
        WFF_ = hm.take(64)
        PB3_ = hm.take(513)
        MROW_ = hm.take(512)
        assert hm.at <= AR_END, hm.at
        QT, KT, GT = v(QT_, 12, 512), v(KT_, 12, 512), v(GT_, 12, 512)
        VN = v(VN_, 12, 512)
        ROPE = v(CT_, 2, 512)
        FQ, FK = v(CT_ + 1024, 512), v(CT_ + 1536, 512)
        CUM = v(CT_ + 1024, 512, p=8)
        NCUM = M[32:40, CT_ + 1536:CT_ + 2048]
        FH = [v(CT_ + i * 512, 512) for i in range(2)]
        HOT = MISC[:, 16:24]
        WFF = v(WFF_, KD, 8)
        MASK = half_words(MASK_, 4 * P).rearrange("p (a b) -> p a b", b=P)
        MROW = [v(CT_ + 1536, 512), v(MROW_, 512)]
        PERM = v(PERM_, P)
        WT = [v(HT_ + i * 2048, 4, 512) for i in range(2)]
        PB = [v(HT_ + 4096 + i * 516, 513) for i in range(3)] + [v(PB3_, 513)]
        PB1 = [v(TMP_, 513), v(TMP_ + 516, 513)]
        SMALL = MISC[:, 32:96]
        HK = [(kind, which, t) for kind in range(3) for which in "qkvg" for t in range(4)]
        HWHO = ["act" if w == "g" else "dve" if (w == "v" or t % 2) else "act" for _, w, t in HK]

        def hyb_dest(j):
            kind, w, t = HK[j]
            return {"q": QT, "k": KT, "g": GT, "v": VN}[w][:, kind * 4 + t, :]

        def pe_hyb_proj(A, st):
            A.e.wait_ge(S["rstd"], 1)
            for j in range(len(HK)):
                if j % 4 == 0:
                    s = st.get()
                if j >= 4:
                    who = HWHO[j - 4]
                    A.e.wait_ge(S[f"{who}_out"], nth(HWHO, j - 4))
                kind, w, t = HK[j]
                for k in range(KD):
                    if j == 0:
                        A.e.wait_ge(S["h_ready"], k + 1)
                    if w == "v":
                        m = mm(ps[:, j % 4, :], HTL[:, k, t * P:(t + 1) * P], Wc[s][:, k, :],
                               start=(k == 0), stop=(k == KD - 1))
                    else:
                        m = mm(ps[:, j % 4, :], Wc[s][:, k, t * P:(t + 1) * P], HTL[:, k, :],
                               start=(k == 0), stop=(k == KD - 1))
                    if k == 0 and j % 4 == 0 and j:
                        m.then_inc(S["w_used"], 2)
                m.then_inc(A.mark("psum_full"), 1)
                if j == 3:
                    A.e.wait_ge(S["const2_in"], 16)
                    for k in range(KD):
                        m = mm(ps[0:8, 7, :], WFF[:, k, :], HTL[:, k, :], start=(k == 0), stop=(k == KD - 1))
                    m.then_inc(A.mark("f_ready"), 1)
                if j >= 12 and j % 2 == 0 and (j - 12) // 2 < 8:
                    pe_rope(A, (j - 12) // 2)
                if j == 28:
                    A.e.wait_ge(S["g_ready"], 8)
                    mm(ps[:, 7, 0:2], ONES, SMALL[:, 0:2], start=True, stop=True).then_inc(A.mark("d_ready"), 1)
                if j % 4 == 3:
                    st.next()
                    c = j // 4
                    s = st.get()
                    if c >= 2:
                        A.e.wait_ge(S["m_ready"], c - 1)
                    for k in range(KD):
                        g = k % 4
                        m = mm(ps[32 * g:32 * g + 32, 4 + c % 2, :], SC[:, k, :], Wc[s][:, k, :],
                               start=(k < 4), stop=(k >= 4))
                        if k == 0:
                            m.then_inc(S["w_used"], 2)
                    m.then_inc(A.mark("k_ready"), 1)
                    if c == 11:
                        st.done(A)
                    else:
                        st.next()
                    if c:
                        pe_mod_cols(A, c - 1)
            pe_mod_cols(A, 11)
            end_phase(A)

        def pe_mod_cols(A, c):
            A.e.wait_ge(S["m_ready"], c + 1)
            if c:
                A.e.wait_ge(S["n_ready"], c)
            for b in range(4):
                m = mm(ps[:, 6, 2 * b:2 * b + 2], MROW[c % 2][:, b * P:(b + 1) * P], gv("pick", 0, 2), start=True, stop=True)
            m.then_inc(A.mark("j_ready"), 1)

        def act_mod_rows(A, c):
            A.e.wait_ge(S["k_ready"], c + 1)
            if c >= 2:
                A.e.wait_ge(S["j_ready"], c - 1)
            act(MROW[c % 2], ps[:, 4 + c % 2, :], ACT.Copy).then_inc(A.mark("m_ready"), 1)

        def dve_mod_cols(A, l, c):
            A.e.wait_ge(S["j_ready"], c + 1)
            dst = v(MOD_, DEPTH, 96)[:, bass.ds(l, 1), 8 * c:8 * c + 8].rearrange("p o (a b) -> p (o a) b", b=2)
            tt(dst, ps[:, 6, 0:8].rearrange("p (a b) -> p a b", b=2),
               lv("ada_b", 4 * c, 4).unsqueeze(2).to_broadcast([P, 4, 2]), ALU.add).then_inc(A.mark("n_ready"), 1)

        SQ = v(QT_, KD, 512)
        RS = v(TMP_, 512)

        def act_hyb_proj(A, l):
            e = A.e
            act(RS, ps[:, 7, :], ACT.Sqrt, bias=eps_col, scale=1.0 / D).then_inc(A.mark("rstd"), 1)
            wff = a["w_in"][bass.ds(l, 1)].rearrange("o r n -> (o r) n")[:, 6144:6152].rearrange("(k p) n -> p k n", p=P)
            e.dma_start(WFF, wff).then_inc(S["const2_in"], 16)
            for dst, src in ((v(CT_, 1024), a["k_rope"][:, 0:1024]), (PERM, a["k_rope"][:, 1024:1152]),
                             (v(TMP_ + 512, 512), a["k_masks"])):
                e.dma_start(dst, src).then_inc(S["const_in"], 16)
            for j in range(len(HK)):
                if HWHO[j] == "act":
                    A.e.wait_ge(S["psum_full"], j + 1)
                    fn = {"g": ACT.Silu}.get(HK[j][1], ACT.Copy)
                    act(hyb_dest(j), ps[:, j % 4, :], fn, scale=0.125 if HK[j][1] == "q" else 1.0)\
                        .then_inc(A.mark("act_out"), 1)
                if j % 4 == 3:
                    act_mod_rows(A, j // 4)
                if j == 35:
                    A.e.wait_ge(S["d_ready"], 1)
                    act(SMALL[:, 2:4], ps[:, 7, 0:2], ACT.Exp).then_inc(A.mark("a_ready"), 1)
                if j == 11:
                    FT = SMALLROW
                    A.e.wait_ge(S["b_ready"], 1)
                    act(FT[1], FT[1], ACT.Exp, scale=-1.0).then_inc(A.mark(), 1)
                    A.e.wait_ge(*A.last)
                    act(FT[1], FT[1], ACT.Ln, bias=MISC[0:8, 1:2]).then_inc(A.mark("c_ready"), 1)
            A.e.wait_ge(S["const_in"], 48)
            end_phase(A)

        def dve_forget_arguments(A):
            FT = SMALLROW
            A.e.wait_ge(S["f_ready"], 1)
            ts(FT[0], ps[0:8, 7, :], lv("f_bias", p=8), None, ALU.add).then_inc(A.mark(), 1)
            A.e.wait_ge(*A.last)
            ts(FT[1], FT[0], -1.0, None, ALU.mult).then_inc(A.mark(), 1)
            A.e.wait_ge(*A.last)
            tt(FT[1], FT[1], FT[0], ALU.max).then_inc(A.mark("b_ready"), 1)
            ts(FT[0], FT[0], 0.0, None, ALU.min).then_inc(A.mark(), 1)
            A.e.wait_ge(*A.last)

        def dve_forget_sums(A):
            FT = SMALLROW
            A.e.wait_ge(S["c_ready"], 1)
            A.e.wait_ge(S["j_ready"], 12)
            tt(FT[0], FT[0], FT[1], ALU.subtract).then_inc(A.mark(), 1)
            nc.vector.memset(FQ, 0.0).then_inc(A.mark(), 1)
            A.e.wait_ge(*A.last)
            nc.vector.memset(FQ[32:40], 1.0).then_inc(A.mark(), 1)
            nc.vector.memset(FK, 1.0).then_inc(A.mark(), 1)
            A.e.wait_ge(*A.last)
            nc.vector.tensor_tensor_scan(CUM, one_col[0:8].to_broadcast([8, 512]), FT[0], 0.0, ALU.mult, ALU.add).then_inc(A.mark(), 1)
            A.e.wait_ge(*A.last)
            ts(NCUM, CUM, -1.0, None, ALU.mult).then_inc(A.mark(), 1)

        SMALLROW = [v(TMP_, 512, p=8), v(TMP_ + 512, 512, p=8)]

        def dve_hyb_proj(A, l):
            LSV = v(LS_, DEPTH, N_LV)
            nc.vector.tensor_copy(v(LV_, N_LV), LSV[:, bass.ds(l, 1), :].rearrange("p o n -> p (o n)")).then_inc(A.mark(), 1)
            dve_recip(A, RS, 1)
            for k in range(KD):
                stt(HTL[:, k, :], XT[:, k, :], lv("g_pre", k), RS, ALU.mult, ALU.mult).then_inc(A.mark("h_ready"), 1)
            A.e.wait_ge(S["const_in"], 48)
            nc.vector.tensor_copy(half_words(MASK_, 4 * P), v(TMP_ + 512, 512)).then_inc(A.mark(), 1)
            tt(SMALL[:, 0:1], lv("lam_vec", 0), lv("lam_vec", 1), ALU.mult).then_inc(A.mark(), 1)
            tt(SMALL[:, 1:2], lv("lam_vec", 2), lv("lam_vec", 3), ALU.mult).then_inc(A.mark(), 1)
            tt(SMALL[:, 8:9], lv("subln"), lv("one_minus"), ALU.mult).then_inc(A.mark(), 1)
            for j in range(len(HK)):
                if HWHO[j] == "dve":
                    A.e.wait_ge(S["psum_full"], j + 1)
                    if HK[j][1] == "q":
                        ins = ts(hyb_dest(j), ps[:, j % 4, :], 0.125, None, ALU.mult)
                    else:
                        ins = nc.vector.tensor_copy(hyb_dest(j), ps[:, j % 4, :])
                    ins.then_inc(A.mark("dve_out"), 1)
                if j % 4 == 3 and j > 3:
                    dve_mod_cols(A, l, j // 4 - 1)
                if j == 7:
                    dve_forget_arguments(A)
                if j >= 13 and (j - 13) % 2 == 0 and (j - 13) // 2 < 8:
                    dve_rope(A, (j - 13) // 2)
            dve_mod_cols(A, l, 11)
            dve_forget_sums(A)
            A.e.wait_ge(S["a_ready"], 1)
            tt(SMALL[:, 4:5], SMALL[:, 3:4], SMALL[:, 2:3], ALU.subtract).then_inc(A.mark(), 1)
            A.e.wait_ge(*A.last)
            tt(SMALL[:, 5:6], SMALL[:, 4:5], lv("lam_init"), ALU.subtract).then_inc(A.mark(), 1)
            end_phase(A)

        def rope_tile(r):
            return (QT, KT)[r // 4][:, r % 4, :]

        def pe_rope(A, r):
            if r == 0:
                A.e.wait_ge(S["b_ready"], 1)
                A.e.wait_ge(S["const_in"], 48)
                A.e.wait_ge(S["act_out"], nth(HWHO, 6))
                A.e.wait_ge(S["dve_out"], nth(HWHO, 7))
            else:
                A.e.wait_ge(S["g_ready"], r)
            mm(ps[:, 7, :], PERM, rope_tile(r), start=True, stop=True).then_inc(A.mark("e_ready"), 1)

        def dve_rope(A, r):
            x = rope_tile(r)
            A.e.wait_ge(S["e_ready"], r + 1)
            tt(RT, ps[:, 7, :], ROPE[:, 1, :], ALU.mult).then_inc(A.mark("g_ready"), 1)
            tt(x, x, ROPE[:, 0, :], ALU.mult).then_inc(A.mark(), 1)
            A.e.wait_ge(*A.last)
            A.e.wait_ge(S["g_ready"], r + 1)
            tt(x, x, RT, ALU.add).then_inc(A.mark(), 1)
            A.e.wait_ge(*A.last)

        RT = v(GT_ + 11 * 512, 512)

        UN = [(kind, h, i) for kind, nh in ((0, 4), (1, 8), (2, 8)) for h in range(nh) for i in range(NQ)]
        LAG = 3
        HEADS = [(kind, h) for kind, nh in ((0, 4), (1, 8), (2, 8)) for h in range(nh)]

        def unit_banks(u):
            return (2 * (u % 2), 2 * (u % 2) + 1) if UN[u][0] == 0 else (u % 4,)

        def prev_user(u):
            for w in range(u - 1, -1, -1):
                if set(unit_banks(w)) & set(unit_banks(u)):
                    return w
            return None

        def pbuf(u, c):
            return PB[u % 4] if c == 0 else PB1[u % 2]

        def pe_attn(A):
            for s in range(len(UN) + LAG):
                if s < len(UN):
                    kind, h, i = UN[s]
                    w = prev_user(s)
                    if w is not None:
                        A.e.wait_ge(S["probs"], w + 1)
                    kw = (i + 1) * P
                    for c, bank in enumerate(unit_banks(s)):
                        if kind == 0:
                            tile, r = h, 64 * c
                        else:
                            tile, r = 4 * kind + h // 2, 64 * (h % 2)
                        o = ps[:, bank, 0:kw]
                        mm(o, QT[r:r + 64, tile, i * P:kw], KT[r:r + 64, tile, 0:kw], start=True, stop=False)
                        if kind == 2:
                            if i == 0:
                                A.e.wait_ge(S["a_ready"], h + 1)
                            mm(o, FQ[:, i * P:kw], FH[h % 2][:, 0:kw], start=False, stop=False)
                        m = mm(ps[:, bank, i * P:kw], IDB, MASK[:, kind, :], start=False, stop=True)
                    m.then_inc(A.mark("scores"), 1)
                if s >= LAG:
                    u = s - LAG
                    kind, h, i = UN[u]
                    if u >= 2:
                        A.e.wait_ge(S["turned_out"], u - 1)
                    A.e.wait_ge(S["weights"], u + 1)
                    src = pbuf(u, 0)
                    for j in range(i + 1):
                        m = tr(ps[:, 4 + u % 2, j * P:(j + 1) * P], src[:, j * P:(j + 1) * P], IDENT)
                    m.then_inc(A.mark("turned"), 1)
                    if i == 0 and u > 0:
                        pe_pv(A, u // NQ - 1)
            pe_pv(A, len(HEADS) - 1)
            end_phase(A)

        def pe_pv(A, hh):
            kind, h = HEADS[hh]
            A.e.wait_ge(S["turned_out"], NQ * (hh + 1))
            if hh >= 2:
                A.e.wait_ge(S["o_out"], hh - 1)
            M_, r, col = (P, 0, h * P) if kind == 0 else (64, 64 * (h % 2), h * 64)
            for j in range(NQ):
                m = mm(ps[r:r + M_, 6 + hh % 2, j * P:T], VN[:, kind * 4 + j, col:col + M_], WT[hh % 2][:, j, j * P:T],
                       start=(j == 0), stop=(j == NQ - 1))
            m.then_inc(A.mark("o_full"), 1)

        def act_attn(A):
            mxn = 0
            for s in range(len(UN) + LAG + 1):
                if s < len(UN):
                    kind, h, i = UN[s]
                    kw = (i + 1) * P
                    bk = unit_banks(s)
                    if s >= 4:
                        A.e.wait_ge(S["turned"], s - 3)
                    if s >= 2:
                        A.e.wait_ge(S["weights"], s - 1)
                    if kind == 1:
                        A.e.wait_ge(S["scores"], s + 1)
                        act(pbuf(s, 0)[:, 0:kw], ps[:, bk[0], 0:kw], ACT.Sigmoid, scale=-1.0).then_inc(A.mark(), 1)
                        act(pbuf(s, 1)[:, 0:kw], ps[:, bk[0], 0:kw], ACT.Sigmoid).then_inc(A.mark("probs"), 1)
                    else:
                        mxn += 1
                        A.e.wait_ge(S["maxima"], mxn)
                        for c, bank in enumerate(bk):
                            ins = act(pbuf(s, c)[:, 0:kw], ps[:, bank, 0:kw], ACT.Exp,
                                      bias=SMALL[:, 16 + 2 * (s % 4) + c:17 + 2 * (s % 4) + c],
                                      accum_out=SMALL[:, 32 + 2 * (s % 4) + c:33 + 2 * (s % 4) + c])
                            ins.then_inc(A.mark("probs" if c == len(bk) - 1 else None), 1)
                if LAG <= s < len(UN) + LAG:
                    u = s - LAG
                    kind, h, i = UN[u]
                    hh = u // NQ
                    A.e.wait_ge(S["turned"], u + 1)
                    if i == 0 and hh >= 2:
                        A.e.wait_ge(S["o_full"], hh - 1)
                    act(WT[hh % 2][:, 0:i + 1, i * P:(i + 1) * P],
                               ps[:, 4 + u % 2, 0:(i + 1) * P].rearrange("p (j q) -> p j q", q=P), ACT.Copy).then_inc(A.mark("turned_out"), 1)
            end_phase(A)

        def dve_attn(A):
            def evac_o(hh):
                kind, h = HEADS[hh]
                A.e.wait_ge(S["o_full"], hh + 1)
                if kind == 0:
                    nc.vector.tensor_copy(QT[:, h, :], ps[:, 6 + hh % 2, :]).then_inc(A.mark("o_out"), 1)
                else:
                    r = 64 * (h % 2)
                    g = GT[r:r + 64, 4 * kind + h // 2, :]
                    tt(g, ps[r:r + 64, 6 + hh % 2, :], g, ALU.mult).then_inc(A.mark("o_out"), 1)

            tt(HOT, IDENT[:, 0:8], IDENT[:, 32:40], ALU.add).then_inc(A.mark(), 1)
            A.e.wait_ge(*A.last)
            for s in range(len(UN) + LAG + 1):
                if s + 3 < len(UN) and UN[s + 3][0] == 2 and UN[s + 3][2] == 0:
                    h = UN[s + 3][1]
                    if h >= 2:
                        A.e.wait_ge(S["scores"], s + 3 - NQ)
                    ts(FH[h % 2], FK, HOT[:, h:h + 1], None, ALU.mult).then_inc(A.mark("a_ready"), 1)
                if s < len(UN):
                    kind, h, i = UN[s]
                    kw = (i + 1) * P
                    if kind != 1:
                        A.e.wait_ge(S["scores"], s + 1)
                        for c, bank in enumerate(unit_banks(s)):
                            ins = nc.vector.tensor_reduce(SMALL[:, 16 + 2 * (s % 4) + c:17 + 2 * (s % 4) + c],
                                                          ps[:, bank, 0:kw], AX_X, ALU.max, negate=True)
                            ins.then_inc(A.mark("maxima" if c == len(unit_banks(s)) - 1 else None), 1)
                if 1 <= s <= len(UN):
                    u = s - 1
                    kind, h, i = UN[u]
                    kw = (i + 1) * P
                    p0, p1 = pbuf(u, 0), pbuf(u, 1)
                    sums = SMALL[:, 32 + 2 * (u % 4):34 + 2 * (u % 4)]
                    inv = SMALL[:, 40 + 2 * (u % 4):42 + 2 * (u % 4)]
                    A.e.wait_ge(S["probs"], u + 1)
                    if kind == 0:
                        nc.vector.reciprocal(inv, sums).then_inc(A.mark(), 1)
                        A.e.wait_ge(*A.last)
                        tt(inv[:, 1:2], inv[:, 1:2], SMALL[:, 5:6], ALU.mult).then_inc(A.mark(), 1)
                        A.e.wait_ge(*A.last)
                        ts(p1[:, 0:kw], p1[:, 0:kw], inv[:, 1:2], None, ALU.mult).then_inc(A.mark(), 1)
                        A.e.wait_ge(*A.last)
                        stt(p0[:, 0:kw], p0[:, 0:kw], inv[:, 0:1], p1[:, 0:kw], ALU.mult, ALU.add).then_inc(A.mark("weights"), 1)
                    elif kind == 1:
                        nc.vector.memset(p0[:, kw:kw + 1], 1.0).then_inc(A.mark(), 1)
                        nc.vector.tensor_tensor_scan(p0[:, 0:kw][:, ::-1], p0[:, 0:kw][:, ::-1],
                                                            one_col.to_broadcast([P, kw]), 1.0, ALU.mult, ALU.mult).then_inc(A.mark(), 1)
                        A.e.wait_ge(*A.last)
                        tt(p0[:, 0:kw], p1[:, 0:kw], p0[:, 1:kw + 1], ALU.mult).then_inc(A.mark("weights"), 1)
                    else:
                        nc.vector.reciprocal(inv[:, 0:1], sums[:, 0:1]).then_inc(A.mark(), 1)
                        A.e.wait_ge(*A.last)
                        ts(p0[:, 0:kw], p0[:, 0:kw], inv[:, 0:1], None, ALU.mult).then_inc(A.mark("weights"), 1)
                if s >= LAG + 2 and (s - LAG - 2) % NQ == 0 and (s - LAG - 2) // NQ >= 1:
                    evac_o((s - LAG - 2) // NQ - 1)
            evac_o(len(HEADS) - 1)
            end_phase(A)

        OUT_ORDER = (1, 2, 0)

        def pe_hyb_out(A, st):
            for h in range(4):
                A.e.wait_ge(S["squares"], h + 1)
                mm(ps[:, h, :], ONES, SQS[:, h, :], start=True, stop=True).then_inc(A.mark("stat"), 1)
            for n, c in enumerate(OUT_ORDER):
                s = st.get()
                for b in ((4, 5, 6, 7, 0, 1, 2, 3) if n == 0 else range(KD)):
                    if n == 0 and b < 4:
                        A.e.wait_ge(S["rstd"], b + 1)
                    for k in range(4):
                        if b == 0 and n == 2:
                            A.e.wait_ge(S["h_ready"], k + 1)
                        m = mm(ps[:, b, :], Wr[s][:, k, b * P:(b + 1) * P], GT[:, 4 * c + k, :],
                               start=(n == 0 and k == 0), stop=(n == 2 and k == 3))
                        if b == 0 and k == 0 and n:
                            m.then_inc(S["w_used"], 2)
                    if n == 2:
                        m.then_inc(A.mark("psum_full"), 1)
                        if b == KD - 1:
                            st.done(A)
                        if b >= 2:
                            pe_post_stat(A, b - 2)
                if n < 2:
                    st.next()
            pe_post_stat(A, KD - 2)
            pe_post_stat(A, KD - 1)
            pe_next_stat(A, 4 + KD)
            end_phase(A)

        def pe_post_stat(A, k):
            if k == 0:
                A.e.wait_ge(S["a_ready"], 1)
            A.e.wait_ge(S["squares"], 4 + k + 1)
            m = mm(ps[:, 0, :], ONES, SQY[:, k, :], start=(k == 0), stop=(k == KD - 1))
            if k == KD - 1:
                m.then_inc(A.mark("stat"), 1)

        def pe_next_stat(A, first):
            for k in range(KD):
                A.e.wait_ge(S["squares"], first + k + 1)
                m = mm(ps[:, 7, :], ONES, SQ[:, k, :], start=(k == 0), stop=(k == KD - 1))
            m.then_inc(A.mark(), 1)

        SQS = v(QT_ + 2048, 4, 512)
        RSH = v(QT_ + 4096, 4, 512)
        YS = v(HT_, KD, 512)
        SQY = v(QT_, KD, 512)

        def act_hyb_out(A):
            for h in range(4):
                act(SQS[:, h, :], QT[:, h, :], ACT.Square).then_inc(A.mark("squares"), 1)
            for h in range(4):
                A.e.wait_ge(S["stat"], h + 1)
                act(RSH[:, h, :], ps[:, h, :], ACT.Sqrt, bias=eps_col, scale=1.0 / P).then_inc(A.mark("rstd"), 1)
            for b in range(KD):
                A.e.wait_ge(S["psum_full"], b + 1)
                act(SQY[:, b, :], ps[:, b, :], ACT.Square).then_inc(A.mark("squares"), 1)
            A.e.wait_ge(S["stat"], 5)
            act(RS, ps[:, 0, :], ACT.Sqrt, bias=eps_col, scale=1.0 / D).then_inc(A.mark("rstd"), 1)
            for k in range(KD):
                A.e.wait_ge(S["b_ready"], k + 1)
                act(SQ[:, k, :], XT[:, k, :], ACT.Square).then_inc(A.mark("squares"), 1)
            end_phase(A)

        def dve_hyb_out(A):
            for h in range(4):
                dve_recip(A, RSH[:, h, :], h + 1)
                stt(QT[:, h, :], QT[:, h, :], SMALL[:, 8:9], RSH[:, h, :], ALU.mult, ALU.mult).then_inc(A.mark(), 1)
                A.e.wait_ge(*A.last)
                tt(GT[:, h, :], GT[:, h, :], QT[:, h, :], ALU.mult).then_inc(A.mark("h_ready"), 1)
            for b in range(KD):
                A.e.wait_ge(S["squares"], 4 + b + 1)
                nc.vector.tensor_copy(YS[:, b, :], ps[:, b, :]).then_inc(A.mark("a_ready"), 1)
            dve_recip(A, RS, 5)
            for k in range(KD):
                stt(YS[:, k, :], YS[:, k, :], lv("g_post", k), RS, ALU.mult, ALU.mult).then_inc(A.mark(), 1)
                scaled = A.last
                if k:
                    tt(XT[:, k - 1, :], XT[:, k - 1, :], YS[:, k - 1, :], ALU.add).then_inc(A.mark("b_ready"), 1)
                A.e.wait_ge(*scaled)
            tt(XT[:, KD - 1, :], XT[:, KD - 1, :], YS[:, KD - 1, :], ALU.add).then_inc(A.mark("b_ready"), 1)
            end_phase(A)

        def side(n):
            return (T, XT, HTL) if n == 0 else (TC, CT, v(HT_ + KD * T, KD, TC))

        def act_mod_norm(A, n, sq, rs, layer, which, turn, bank=7):
            L, X, H = side(n)
            act_norm(A, X, sq, rs, L, bank, turn)
            for k in range(KD):
                A.e.wait_ge(S["scaled"], (turn - 1) * KD + k + 1)
                act(H[:, k, :], H[:, k, :], ACT.Identity, bias=mod(layer, which, k, n)).then_inc(A.mark("h_ready"), 1)

        def dve_mod_norm(A, n, sq, rs, layer, which, norm, turn):
            L, X, H = side(n)
            sc = v(MOD_ + layer * 96, 48, 2)[:, (which + 1) * KD:(which + 2) * KD, n]
            g = MISC[:, 40:48]
            dve_squares(A, X, sq)
            stt(g, sc, 1.0, gv(norm, layer * KD, KD), ALU.add, ALU.mult).then_inc(A.mark(), 1)
            dve_recip(A, rs, turn)
            for k in range(KD):
                stt(H[:, k, :], X[:, k, :], g[:, k:k + 1], rs, ALU.mult, ALU.mult).then_inc(A.mark("scaled"), 1)
            A.e.wait_ge(*A.last)

        ym = Map(AR_)
        U3_, DC_, DS_ = ym.take(24 * 512), ym.take(2048), ym.take(2048)
        FS_, GS_, NY_, KS_ = ym.take(512), ym.take(512), ym.take(512), ym.take(4096)
        WIN_, H2_, T_, W3_, FB_ = ym.take(1024), ym.take(512), ym.take(1024), ym.take(1024), ym.take(512)
        assert ym.at <= AR_END, ym.at
        DC, DS = v(DC_, 4, 512), v(DS_, 4, 512)
        FB = v(FB_, 512, p=1)
        UT_ = KS_

        class Hy:
            def __init__(s, n):
                s.n = n
                s.L = L = (T, TC)[n]
                s.tag = "lc"[n]
                s.nt = L // P
                s.step = T // L
                s.U3 = v(U3_, 24, L)
                s.FS, s.NY = v(FS_, s.nt, P), v(NY_, s.nt, P)
                s.GS = v(GS_, L)
                s.UT = [v(UT_ + i * 516, L + 2) for i in range(2)]
                s.H2 = v(H2_, L, p=64)
                s.H1 = v(H2_, L, p=64)
                s.HE, s.HO, s.HB = (v(HT_ + i * 2048, 4, 512) for i in range(3))

            def natural(s, c):
                return v(U3_ + 4 * c * s.L, s.nt, 512)

            def fwd(s, table, t, f):
                lo = f * P * s.step
                return table[:, t, lo:lo + P * s.step:s.step]

            def inv(s, table, f):
                return table[:, f, 0:T:s.step]

        def load_filter_out(e, sem, c, o):
            for d in range(2):
                lo = o * 2048 + d * 1024 + c * 512
                e.dma_start(v(W3_ + d * 512, 512, p=64), a["hy_ffn_w3_2"][:, lo:lo + 512]).then_inc(sem, 16)
            e.dma_start(FB, a["hy_filter_bias_2"][o:o + 1, c * 512:(c + 1) * 512]).then_inc(sem, 16)

        def act_hy_a(A, y):
            e = A.e
            L = y.L
            pairs = [(v(DC_, 4096), a["k_dft"]), (v(FS_, y.nt * P), a[f"k_fs0_{y.tag}"]),
                     (v(NY_, y.nt * P), a[f"k_nyq_{y.tag}"]), (v(GS_, L), a[f"k_gs0_{y.tag}"]),
                     (v(W3_, L, p=33), a[f"k_pos_{y.tag}"]), (v(W3_ + 512, 64, p=33), a["hy_ffn_w1_2"]),
                     (v(W3_ + 576, 64, p=64), a["hy_ffn_w2_2"])]
            for dst, src in pairs:
                e.dma_start(dst, src).then_inc(S["const_in"], 16)
            act_mod_norm(A, y.n, v(KS_, KD, L), v(T_, L), 0, 0, 1)
            for r in range(2):
                A.e.wait_ge(S["b_ready"], r + 1)
                act(y.H2, v(T_, L, p=64), ACT.Sin).then_inc(A.mark("c_ready"), 1)
            for j in range(24):
                A.e.wait_ge(S["psum_full"], j + 1)
                if j >= 2:
                    A.e.wait_ge(S["dve_out"], j - 1)
                if j == 0:
                    A.e.wait_ge(S["d_ready"], 1)
                act(y.UT[j % 2][:, 1:L + 1], ps[:, j % 4, 0:L], ACT.Identity, bias=gv("hy_b_in", j)).then_inc(A.mark("act_out"), 1)
                if j == 3:
                    A.e.wait_ge(S["e_ready"], 2)
                    load_filter_out(e, S["const_in"], 0, 0)
            A.e.wait_ge(S["const_in"], 16 * 10)
            end_phase(A)

        def pe_hy_a(A, y, st):
            L = y.L
            pe_norm(A, v(KS_, KD, L), L, 7, 1)
            A.e.wait_ge(S["const_in"], 16 * 7)
            mm(ps[0:64, 6, 0:L], v(W3_ + 512, 64, p=33), v(W3_, L, p=33), start=True, stop=True).then_inc(A.mark("e_ready"), 1)
            _, _, H = side(y.n)
            for j in range(24):
                if j % 4 == 0:
                    s = st.get()
                if j >= 4:
                    A.e.wait_ge(S["act_out"], j - 3)
                for k in range(KD):
                    if j == 0:
                        A.e.wait_ge(S["h_ready"], k + 1)
                    m = mm(ps[:, j % 4, 0:L], Wc[s][:, k, (j % 4) * P:(j % 4 + 1) * P], H[:, k, :],
                           start=(k == 0), stop=(k == KD - 1))
                    if k == 0 and j % 4 == 0 and j:
                        m.then_inc(S["w_used"], 2)
                m.then_inc(A.mark("psum_full"), 1)
                if j == 1:
                    A.e.wait_ge(S["c_ready"], 1)
                    mm(ps[0:64, 5, 0:L], v(W3_ + 576, 64, p=64), y.H1, start=True, stop=True).then_inc(A.mark("e_ready"), 1)
                if j == 23:
                    st.done(A)
                elif j % 4 == 3:
                    st.next()
            end_phase(A)

        MAGIC = 1.5 * 2.0 ** 23
        PI2_HI = 6.28125
        PI2_LO = TWO_PI - PI2_HI
        PI_IN = 3.1415925

        def dve_hy_a(A, y):
            L = y.L
            dve_mod_norm(A, y.n, v(KS_, KD, L), v(T_, L), 0, 0, "norm1", 1)
            x, n = v(T_, L, p=64), v(T_ + 512, L, p=64)
            for r in range(2):
                A.e.wait_ge(S["e_ready"], r + 1)
                src = ps[0:64, 6 - r, 0:L]
                ts(x, src, gv("ffn_b1" if r == 0 else "ffn_b2", p=64), gv("freq", r, p=64), ALU.add, ALU.mult).then_inc(A.mark(), 1)
                A.e.wait_ge(*A.last)
                ts(n, x, 1 / TWO_PI, MAGIC, ALU.mult, ALU.add).then_inc(A.mark(), 1)
                A.e.wait_ge(*A.last)
                ts(n, n, -MAGIC, None, ALU.add).then_inc(A.mark(), 1)
                A.e.wait_ge(*A.last)
                stt(x, n, -PI2_HI, x, ALU.mult, ALU.add).then_inc(A.mark(), 1)
                A.e.wait_ge(*A.last)
                stt(x, n, -PI2_LO, x, ALU.mult, ALU.add).then_inc(A.mark(), 1)
                A.e.wait_ge(*A.last)
                ts(x, x, PI_IN, -PI_IN, ALU.min, ALU.max).then_inc(A.mark("b_ready"), 1)
                A.e.wait_ge(S["c_ready"], r + 1)
            A.e.wait_ge(S["stat"], 1)
            for u in y.UT:
                nc.vector.memset(u[:, 0:1], 0.0).then_inc(A.mark(), 1)
                nc.vector.memset(u[:, L + 1:L + 2], 0.0).then_inc(A.mark("d_ready" if u is y.UT[1] else None), 1)
            for j in range(24):
                u, o = y.UT[j % 2], y.U3[:, j, :]
                A.e.wait_ge(S["act_out"], j + 1)
                ts(o, u[:, 1:L + 1], gv("hy_sw", 24 + j), gv("hy_sb", j), ALU.mult, ALU.add).then_inc(A.mark(), 1)
                A.e.wait_ge(*A.last)
                stt(o, u[:, 0:L], gv("hy_sw", j), o, ALU.mult, ALU.add).then_inc(A.mark(), 1)
                A.e.wait_ge(*A.last)
                stt(o, u[:, 2:L + 2], gv("hy_sw", 48 + j), o, ALU.mult, ALU.add).then_inc(A.mark("dve_out"), 1)
            end_phase(A)

        def act_hy_b(A, y, c, o):
            e = A.e
            for t in range(y.nt):
                if t >= 2:
                    A.e.wait_ge(S["dve_out"], t - 1)
                e.dma_start(v(WIN_ + (t % 2) * 512, 512),
                            a[f"k_win_{y.tag}"][t * P:(t + 1) * P, c * 512:(c + 1) * 512])\
                    .then_inc(S[("m_ready", "n_ready")[t % 2]], 16)
            A.e.wait_ge(S["turned"], y.nt)
            for t in range(y.nt):
                act(y.natural(c)[:, t, :], ps[:, t, :], ACT.Copy).then_inc(A.mark("turned_out"), 1)
            if (c, o) != (1, 1):
                A.e.wait_ge(S["dve_out"], y.nt)
                load_filter_out(e, S["i_ready"], c + o, 1 - o)
            for f in range(2 * y.nt):
                A.e.wait_ge(S["psum_full"], f + 1)
                act(v(KS_, 8, 512)[:, f, :], ps[:, f % 4, :], ACT.Copy,
                           scale=gv("dft_" + y.tag, 0 if f % y.nt == 0 else 1)).then_inc(A.mark("act_out"), 1)
            if (c, o) != (1, 1):
                A.e.wait_ge(S["i_ready"], 48)
            end_phase(A)

        def pe_hy_b(A, y, c, o):
            nt = y.nt
            for t in range(nt):
                if t >= 2:
                    A.e.wait_ge(S["dve_out"], t - 1)
                for d in range(2):
                    m = mm(ps[:, 4 + 2 * (t % 2) + d, :], y.H2[:, t * P:(t + 1) * P], v(W3_ + d * 512, 512, p=64),
                           start=True, stop=True)
                m.then_inc(A.mark("a_ready"), 1)
                if t == 1:
                    for tn in range(nt):
                        for b in range(4):
                            m = tr(ps[:, tn, b * P:(b + 1) * P], y.U3[:, c * 4 + b, tn * P:(tn + 1) * P], IDENT)
                        m.then_inc(A.mark("turned"), 1)
            A.e.wait_ge(S["dve_out"], nt)
            for g in range(2 * nt):
                f = g % nt
                if g == 0:
                    A.e.wait_ge(S["turned_out"], nt)
                if g >= 4:
                    A.e.wait_ge(S["act_out"], g - 3)
                for t in range(nt):
                    if g < nt:
                        m = mm(ps[:, g % 4, :], y.fwd(DC, t, f), y.HE[:, t, :], start=(t == 0), stop=(t == nt - 1))
                    elif f:
                        m = mm(ps[:, g % 4, :], y.fwd(DS, t, f), y.HO[:, t, :], start=(t == 0), stop=(t == nt - 1))
                    else:
                        mm(ps[:, g % 4, :], y.FS[:, t, :], y.HO[:, t, :], start=(t == 0), stop=False)
                        m = mm(ps[:, g % 4, :], y.NY[:, t, :], y.HB[:, t, :], start=False, stop=(t == nt - 1))
                m.then_inc(A.mark("psum_full"), 1)
            A.e.wait_ge(S["act_out"], 2 * nt)
            for f in range(nt):
                if f >= 2:
                    A.e.wait_ge(S["b_ready"], f - 1)
                for part in range(2):
                    for t in range(nt):
                        w = y.fwd(DC, t, f) if part == 0 else y.fwd(DS, t, f) if f else y.FS[:, t, :]
                        m = mm(ps[:, 2 * (f % 2) + part, :], w, y.natural(c)[:, t, :], start=(t == 0), stop=(t == nt - 1))
                m.then_inc(A.mark("c_ready"), 1)
            A.e.wait_ge(S["d_ready"], nt)
            for b in range(4):
                for f in range(2 * nt):
                    rhs = y.inv(DC, f) if f < nt else y.GS if f == nt else y.inv(DS, f - nt)
                    m = mm(ps[:, 4 + b, 0:y.L], v(KS_, 8, 512)[:, f, b * P:(b + 1) * P], rhs,
                           start=(f == 0), stop=(f == 2 * nt - 1))
                m.then_inc(A.mark("o_full"), 1)
            end_phase(A)

        def dve_hy_b(A, y, c, o):
            nt = y.nt
            KS = v(KS_, 8, 512)
            t0, t1 = v(T_, 512), v(T_ + 512, 512)
            for t in range(nt):
                w = v(WIN_ + (t % 2) * 512, 512)
                A.e.wait_ge(S["a_ready"], t + 1)
                A.e.wait_ge(S[("m_ready", "n_ready")[t % 2]], 16 * (t // 2 + 1))
                fw, bw = ps[:, 4 + 2 * (t % 2), :], ps[:, 5 + 2 * (t % 2), :]
                hb = y.HB[:, t, :]
                tt(t0, fw, w, ALU.mult).then_inc(A.mark(), 1)
                if t == 0:
                    stt(hb, bw, gv("not0"), w, ALU.mult, ALU.mult).then_inc(A.mark(), 1)
                    A.e.wait_ge(*A.last)
                    tt(t0[0:1], t0[0:1], FB, ALU.add).then_inc(A.mark(), 1)
                else:
                    tt(hb, bw, w, ALU.mult).then_inc(A.mark(), 1)
                A.e.wait_ge(*A.last)
                tt(y.HE[:, t, :], t0, hb, ALU.add).then_inc(A.mark(), 1)
                tt(y.HO[:, t, :], t0, hb, ALU.subtract).then_inc(A.mark("dve_out"), 1)
                A.e.wait_ge(*A.last)
            krp, kip = y.HO[:, 0, :], y.HO[:, 1, :]
            A.e.wait_ge(S["act_out"], nt + 1)
            A.e.wait_ge(S["psum_full"], 2 * nt)
            ts(kip, KS[:, nt, :], gv("not0"), None, ALU.mult).then_inc(A.mark(), 1)
            ts(krp, KS[:, 0, :], gv("not0"), None, ALU.mult).then_inc(A.mark(), 1)
            A.e.wait_ge(*A.last)
            stt(krp, KS[:, nt, :], gv("is0"), krp, ALU.mult, ALU.add).then_inc(A.mark(), 1)
            A.e.wait_ge(*A.last)
            q = [t0, t1, v(WIN_, 512), v(WIN_ + 512, 512)]
            A.e.wait_ge(S["act_out"], 2 * nt)
            for f in range(nt):
                A.e.wait_ge(S["c_ready"], f + 1)
                ur, ui = ps[:, 2 * (f % 2), :], ps[:, 2 * (f % 2) + 1, :]
                kr, ki = KS[:, f, :], KS[:, nt + f, :]
                kr_i, ki_ = (krp, kip) if f == 0 else (kr, ki)
                tt(q[0], ur, kr, ALU.mult).then_inc(A.mark(), 1)
                tt(q[1], ui, ki_, ALU.mult).then_inc(A.mark(), 1)
                tt(q[2], ur, ki_, ALU.mult).then_inc(A.mark(), 1)
                tt(q[3], ui, kr_i, ALU.mult).then_inc(A.mark("b_ready"), 1)
                A.e.wait_ge(*A.last)
                tt(kr, q[0], q[1], ALU.subtract).then_inc(A.mark(), 1)
                tt(ki, q[2], q[3], ALU.add).then_inc(A.mark("d_ready"), 1)
                A.e.wait_ge(*A.last)
            for b in range(4):
                A.e.wait_ge(S["o_full"], b + 1)
                tt(y.U3[:, c * 4 + b, :], ps[:, 4 + b, 0:y.L], y.U3[:, 8 * (o + 1) + c * 4 + b, :], ALU.mult).then_inc(A.mark(), 1)
            end_phase(A)

        def pe_proj_out(A, st, src, L):
            for b in range(KD):
                if b % 4 == 0:
                    s = st.get()
                for k in range(KD):
                    m = mm(ps[:, b, 0:L], Wc[s][:, k, (b % 4) * P:(b % 4 + 1) * P], src[:, k, :],
                           start=(k == 0), stop=(k == KD - 1))
                    if k == 0 and b == 4:
                        m.then_inc(S["w_used"], 2)
                m.then_inc(A.mark("psum_full"), 1)
                if b == 3:
                    st.next()
            st.done(A)
            end_phase(A)

        def dve_proj_out(A, n, tmp, layer, bias):
            L, X, _ = side(n)
            for b in range(KD):
                A.e.wait_ge(S["psum_full"], b + 1)
                g = mod(layer, 2, b, n)
                if bias:
                    ts(tmp, ps[:, b, 0:L], gv(bias, b), g, ALU.add, ALU.mult).then_inc(A.mark(), 1)
                    A.e.wait_ge(*A.last)
                    tt(X[:, b, :], X[:, b, :], tmp, ALU.add).then_inc(A.mark(), 1)
                    A.e.wait_ge(*A.last)
                else:
                    stt(X[:, b, :], ps[:, b, 0:L], g, X[:, b, :], ALU.mult, ALU.add).then_inc(A.mark(), 1)
            end_phase(A)

        em = Map(AR_)
        XE_, B_ = em.take(KD * N_EXP * 96), em.at
        HN_, SEL_ = em.take(6 * 1024), em.take(4096 + 1024)
        em.at = B_
        YE_ = em.take(12 * 1024)
        XS_, AT_, IO_, RT_, AF_, SL_ = (em.take(2 * KD * 96), em.take(KD * 96), em.take(CAP_L), em.take(KD * 16),
                                        em.take(96), em.take(96))
        assert em.at <= AR_END and HN_ + 6144 + 5120 <= XS_
        GS2_, GSC_, AB_ = HT_, HT_ + 4096, HT_ + 5120
        IO = v(IO_, CAP_L)
        PAIR = v(SL_, 2 * CAP_C)
        RTR = v(RT_, KD, 16)
        AFF, SLOT = v(AF_, 6, 16), v(SL_, 6, 16)

        class Moe:
            def __init__(s, layer):
                s.layer = layer
                s.sides = (0, 1) if layer == 0 else (0,)
                s.S = CAP_L + (CAP_C if layer == 0 else 0)
                s.XE = v(XE_, KD, N_EXP * s.S).rearrange("p k (e s) -> p k e s", s=s.S)
                s.XS = [v(XS_ + i * KD * 96, KD, s.S) for i in range(2)]
                s.AT = v(AT_, KD, CAP_L)
                s.ATC = v(AT_ + KD * CAP_L, KD, CAP_C)
                s.GU = v(AB_, 512)
                s.GUC = v(AB_ + 512, 512)

            def side(s, n):
                if n == 0:
                    return T, CAP_L, 0, v(HN_, 4, 1024), v(SEL_, 4, 1024), v(GS2_, 8, 512), v(YE_, 8, 1024)
                return (TC, CAP_C, 4, v(HN_ + 4096, 2, 1024), v(SEL_ + 4096, 2, 512), v(GSC_, 4, 256),
                        v(YE_ + 8192, 4, 1024))

        SQM = lambda L: v(XE_, KD, L)
        RSM = lambda L: v(XE_ + 4096, L)
        LOGITS = v(XE_ + 5120, T + TC, p=16)

        def act_moe_a(A, m_):
            e = A.e
            e.dma_start(IO, a["k_iota"]).then_inc(S["const_in"], 16)
            e.dma_start(RTR, a["moe_router_2"][m_.layer].rearrange("(k p) n -> p k n", p=P)).then_inc(S["const_in"], 16)
            for z, n in enumerate(m_.sides):
                L = side(n)[0]
                if z:
                    A.e.wait_ge(S["stat"], z)
                act_mod_norm(A, n, SQM(L), RSM(L), m_.layer, 3, z + 1)
            for z, n in enumerate(m_.sides):
                L, _, t0 = m_.side(n)[0:3]
                A.e.wait_ge(S["psum_full"], z + 1)
                act(LOGITS[:, t0 * P:t0 * P + L], ps[0:16, 4 + z, 0:L], ACT.Copy).then_inc(A.mark("act_out"), 1)
            for z, n in enumerate(m_.sides):
                L, _, t0 = m_.side(n)[0:3]
                A.e.wait_ge(S["maxima"], z + 1)
                for t in range(L // P):
                    act(AFF[:, t0 + t, :], ps[:, 6 - z, (t0 + t) * 16:(t0 + t + 1) * 16], ACT.Exp,
                               bias=MISC[:, 48 + t0 + t:49 + t0 + t], accum_out=MISC[:, 56 + t0 + t:57 + t0 + t]).then_inc(A.mark(), 1)
                act(MISC[:, 4:5], MISC[:, 2:3], ACT.Copy).then_inc(A.mark("probs"), 1)
            A.e.wait_ge(S["const_in"], 32)
            end_phase(A)

        def pe_moe_a(A, m_):
            for z, n in enumerate(m_.sides):
                L, _, H = side(n)
                pe_norm(A, SQM(L), L, 7, z + 1)
            A.e.wait_ge(S["const_in"], 32)
            for z, n in enumerate(m_.sides):
                L, _, H = side(n)
                t0 = m_.side(n)[2]
                for k in range(KD):
                    A.e.wait_ge(S["h_ready"], z * KD + k + 1)
                    m = mm(ps[0:16, 4 + z, 0:L], RTR[:, k, :], H[:, k, :], start=(k == 0), stop=(k == KD - 1))
                m.then_inc(A.mark("psum_full"), 1)
            for z, n in enumerate(m_.sides):
                L, _, _ = side(n)
                t0 = m_.side(n)[2]
                A.e.wait_ge(S["act_out"], z + 1)
                for t in range(L // P):
                    m = tr(ps[:, 6 - z, (t0 + t) * 16:(t0 + t + 1) * 16], LOGITS[:, (t0 + t) * P:(t0 + t + 1) * P],
                           IDENT[0:16, 0:16])
                m.then_inc(A.mark("scores"), 1)
            end_phase(A)

        def dve_moe_a(A, m_):
            for z, n in enumerate(m_.sides):
                L = side(n)[0]
                if z:
                    A.e.wait_ge(S["stat"], z)
                dve_mod_norm(A, n, SQM(L), RSM(L), m_.layer, 3, "norm2", z + 1)
            for z, n in enumerate(m_.sides):
                L, _, t0 = m_.side(n)[0:3]
                nt = L // P
                A.e.wait_ge(S["scores"], z + 1)
                nc.vector.tensor_reduce(MISC[:, 48 + t0:48 + t0 + nt],
                                               ps[:, 6 - z, t0 * 16:(t0 + nt) * 16].rearrange("p (t x) -> p t x", x=16),
                                               AX_X, ALU.max, negate=True).then_inc(A.mark("maxima"), 1)
                A.e.wait_ge(S["probs"], z + 1)
                inv = MISC[:, 64 + t0:64 + t0 + nt]
                nc.vector.reciprocal(inv, MISC[:, 56 + t0:56 + t0 + nt]).then_inc(A.mark(), 1)
                A.e.wait_ge(*A.last)
                tt(AFF[:, t0:t0 + nt, :], AFF[:, t0:t0 + nt, :], inv.unsqueeze(2).to_broadcast([P, nt, 16]),
                          ALU.mult).then_inc(A.mark(), 1)
            end_phase(A)

        ROW = [v(XE_ + i * 768, 768, p=16) for i in range(6)]
        SM = lambda i, n=1: MISC[0:16, 72 + i:72 + i + n]

        def pe_moe_b(A, m_):
            for z, n in enumerate(m_.sides):
                L, _, t0 = m_.side(n)[0:3]
                for t in range(L // P):
                    m = tr(ps[0:16, 6 + z, t * P:(t + 1) * P], AFF[:, t0 + t, :], IDENT)
                m.then_inc(A.mark("a_ready"), 1)
            g = 0
            for z, n in enumerate(m_.sides):
                H = side(n)[2]
                for t in range(side(n)[0] // P):
                    for half in range(2):
                        if g >= 4:
                            A.e.wait_ge(S["turned_out"], g - 3)
                        for k in range(4):
                            m = tr(ps[:, g % 4, k * P:(k + 1) * P], H[:, half * 4 + k, t * P:(t + 1) * P], IDENT)
                        m.then_inc(A.mark("turned"), 1)
                        g += 1
            for z, n in enumerate(m_.sides):
                L, _, t0 = m_.side(n)[0:3]
                A.e.wait_ge(S["b_ready"], z + 1)
                for t in range(L // P):
                    m = tr(ps[:, 4 + z, (t0 + t) * 16:(t0 + t + 1) * 16], ROW[5][:, (t0 + t) * P:(t0 + t + 1) * P],
                           IDENT[0:16, 0:16])
                m.then_inc(A.mark("c_ready"), 1)
            end_phase(A)

        def act_moe_b(A, m_):
            for z, n in enumerate(m_.sides):
                L, _, t0 = m_.side(n)[0:3]
                A.e.wait_ge(S["a_ready"], z + 1)
                act(ROW[0][:, t0 * P:t0 * P + L], ps[0:16, 6 + z, 0:L], ACT.Copy).then_inc(A.mark("d_ready"), 1)
            g = 0
            for n in m_.sides:
                HN = m_.side(n)[3]
                for t in range(side(n)[0] // P):
                    for half in range(2):
                        A.e.wait_ge(S["turned"], g + 1)
                        act(HN[:, t, half * 512:(half + 1) * 512], ps[:, g % 4, :], ACT.Copy).then_inc(A.mark("turned_out"), 1)
                        g += 1
            end_phase(A)

        def dve_moe_b(A, m_):
            for z, n in enumerate(m_.sides):
                L, cap, t0 = m_.side(n)[0:3]
                af, wk, gt, eq, ce, sl = (r[:, t0 * P:t0 * P + L] for r in ROW)
                A.e.wait_ge(S["d_ready"], z + 1)
                nc.vector.tensor_copy(wk, af).then_inc(A.mark(), 1)
                A.e.wait_ge(*A.last)
                top = SM(0, 8)
                for r in range(cap // 8):
                    nc.vector.max(top, wk).then_inc(A.mark(), 1)
                    A.e.wait_ge(*A.last)
                    if r < cap // 8 - 1:
                        nc.vector.match_replace(wk, top, wk, -1.0).then_inc(A.mark(), 1)
                        A.e.wait_ge(*A.last)
                thr = SM(7)
                ts(gt, af, thr, None, ALU.is_gt).then_inc(A.mark(), 1)
                ts(eq, af, thr, None, ALU.is_equal).then_inc(A.mark(), 1)
                A.e.wait_ge(*A.last)
                nc.vector.tensor_reduce(SM(8), gt, AX_X, ALU.add).then_inc(A.mark(), 1)
                nc.vector.tensor_tensor_scan(ce, one_col[0:16].to_broadcast([16, L]), eq, 0.0, ALU.mult, ALU.add).then_inc(A.mark(), 1)
                A.e.wait_ge(*A.last)
                ts(SM(9), SM(8), -1.0, float(cap), ALU.mult, ALU.add).then_inc(A.mark(), 1)
                A.e.wait_ge(*A.last)
                stt(eq, ce, SM(9), eq, ALU.is_le, ALU.mult).then_inc(A.mark(), 1)
                A.e.wait_ge(*A.last)
                tt(gt, gt, eq, ALU.add).then_inc(A.mark(), 1)
                A.e.wait_ge(*A.last)
                nc.vector.tensor_tensor_scan(ce, one_col[0:16].to_broadcast([16, L]), gt, 0.0, ALU.mult, ALU.add).then_inc(A.mark(), 1)
                A.e.wait_ge(*A.last)
                tt(sl, ce, gt, ALU.mult).then_inc(A.mark(), 1)
                A.e.wait_ge(*A.last)
                ts(sl, sl, -1.0, None, ALU.add).then_inc(A.mark("b_ready"), 1)
            for z, n in enumerate(m_.sides):
                L, cap, t0, _, SEL = m_.side(n)[0:5]
                nt = L // P
                A.e.wait_ge(S["c_ready"], z + 1)
                nc.vector.tensor_copy(SLOT[:, t0:t0 + nt, :], ps[:, 4 + z, t0 * 16:(t0 + nt) * 16]
                                             .rearrange("p (t x) -> p t x", x=16)).then_inc(A.mark(), 1)
                A.e.wait_ge(*A.last)
                for t in range(nt):
                    tt(SEL[:, t, :].rearrange("p (e s) -> p e s", s=cap),
                              SLOT[:, t0 + t, :].unsqueeze(2).to_broadcast([P, 16, cap]),
                              IO[:, 0:cap].unsqueeze(1).to_broadcast([P, 16, cap]), ALU.is_equal).then_inc(A.mark(), 1)
            end_phase(A)

        def moe_gathers(m_):
            g = [(k, 0, half) for k in range(KD) for half in range(2)]
            if 1 in m_.sides:
                g += [(k, 1, 0) for k in range(KD)]
            return g

        def pe_moe_c(A, m_):
            for j, (k, n, half) in enumerate(moe_gathers(m_)):
                L, _, _, HN, SEL = m_.side(n)[0:5]
                if j >= 4:
                    A.e.wait_ge(S["act_out" if j % 2 == 0 else "dve_out"], (j - 4) // 2 + 1)
                nt = L // P
                for t in range(nt):
                    m = mm(ps[:, j % 4, :], HN[:, t, k * P:(k + 1) * P], SEL[:, t, half * 512:(half + 1) * 512],
                           start=(t == 0), stop=(t == nt - 1))
                m.then_inc(A.mark("psum_full"), 1)
            A.e.wait_ge(S["a_ready"], 1)
            g = 0
            for n in m_.sides:
                L, cap, _, _, SEL = m_.side(n)[0:5]
                for p_ in range(16 * cap // P):
                    if g >= 2:
                        A.e.wait_ge(S["turned_out"], g - 1)
                    for t in range(L // P):
                        m = tr(ps[:, 4 + g % 2, t * P:(t + 1) * P], SEL[:, t, p_ * P:(p_ + 1) * P], IDENT)
                    m.then_inc(A.mark("turned"), 1)
                    g += 1
            end_phase(A)

        def gather_out(m_, j):
            k, n, half = moe_gathers(m_)[j]
            if n == 0:
                return m_.XE[:, k, half * 8:(half + 1) * 8, 0:CAP_L], ps[:, j % 4, :].rearrange("p (e s) -> p e s", s=CAP_L)
            return m_.XE[:, k, :, CAP_L:], ps[:, j % 4, :].rearrange("p (e s) -> p e s", s=CAP_C)

        def act_moe_c(A, m_):
            A.e.dma_start(PAIR, a["k_pair"]).then_inc(S["const_in"], 16)
            for j in range(0, len(moe_gathers(m_)), 2):
                A.e.wait_ge(S["psum_full"], j + 1)
                o, i = gather_out(m_, j)
                act(o, i, ACT.Copy).then_inc(A.mark("act_out"), 1)
            g = 0
            for n in m_.sides:
                L, cap = m_.side(n)[0:2]
                G = m_.side(n)[5]
                for p_ in range(16 * cap // P):
                    A.e.wait_ge(S["turned"], g + 1)
                    act(G[:, p_, :], ps[:, 4 + g % 2, 0:L], ACT.Copy).then_inc(A.mark("turned_out"), 1)
                    g += 1
            A.e.wait_ge(S["const_in"], 16)
            end_phase(A)

        def dve_moe_c(A, m_):
            n_g = len(moe_gathers(m_))
            for j in range(1, n_g, 2):
                A.e.wait_ge(S["psum_full"], j + 1)
                o, i = gather_out(m_, j)
                nc.vector.tensor_copy(o, i).then_inc(A.mark("dve_out"), 1)
            A.e.wait_ge(S["psum_full"], n_g)
            for n in m_.sides:
                L, cap, t0, _, SEL = m_.side(n)[0:5]
                for t in range(L // P):
                    x = SEL[:, t, :].rearrange("p (e s) -> p e s", s=cap)
                    tt(x, x, AFF[:, t0 + t, :].unsqueeze(2).to_broadcast([P, 16, cap]), ALU.mult).then_inc(A.mark(), 1)
            A.e.wait_ge(*A.last)
            nc.vector.memset(MISC[:, 3:4], 0.0).then_inc(A.mark("a_ready"), 1)
            end_phase(A)

        def pe_moe_d(A, m_, st):
            ctx = m_.layer == 0
            for e in range(EB):
                XS = m_.XS[e % 2]
                A.e.wait_ge(S["a_ready"], e + 1)
                for pair in range(2):
                    for kh in range(2):
                        w = [Wh[st.get_half(x)] for x in range(2)]
                        if kh == 0 and e:
                            A.e.wait_ge(S["act_out"], 2 * (e - 1) + pair + 1)
                        for k in range(4 * kh, 4 * kh + 4):
                            for x in range(2):
                                m = mm(ps[64 * x:64 * x + 64, pair, :], XS[:, k, 0:CAP_L], w[x][:, k % 4, :],
                                       start=(k == 0), stop=(k == KD - 1))
                                if k == 4 * kh and x == 1 and (e or pair or kh):
                                    m.then_inc(S["w_used"], 2)
                        m.then_inc(A.mark("psum_full" if kh else None), 1)
                        if ctx:
                            if kh == 0 and e:
                                A.e.wait_ge(S["ctx_out"], 2 * (e - 1) + pair + 1)
                                if pair:
                                    A.e.wait_ge(S["ctx_o_out"], e)
                            for k in range(4 * kh, 4 * kh + 4):
                                for x in range(2):
                                    r = 64 * x + 32 * (k % 2)
                                    m = mm(ps[r:r + CAP_C, 4 + pair, :], XS[:, k, CAP_L:], w[x][:, k % 4, :],
                                           start=(k < 2), stop=(k >= KD - 2))
                            m.then_inc(A.mark("ctx_full" if kh else None), 1)
                        st.next()
                        if pair and kh == 0:
                            pe_turn(A, m_, e, 0)
                w = [Wh[st.get_half(x)] for x in range(2)]
                if e:
                    A.e.wait_ge(S["e_ready"], e)
                A.e.wait_ge(S["c_ready"], 2 * e + 1)
                for k in range(4):
                    for x in range(2):
                        m = mm(ps[64 * x:64 * x + 64, 7, :], m_.AT[:, k, :], w[x][:, k, :], start=(k == 0), stop=False)
                        if k == 0 and x == 1:
                            m.then_inc(S["w_used"], 2)
                    if k == 1:
                        pe_turn(A, m_, e, 1)
                if ctx:
                    A.e.wait_ge(S["ctx_hidden"], 2 * e + 1)
                    for k in range(4):
                        for x in range(2):
                            r = 64 * x + 32 * (k % 2)
                            m = mm(ps[r:r + CAP_C, 5, :], m_.ATC[:, k, :], w[x][:, k, :], start=(k < 2), stop=False)
                st.next()
                w = [Wh[st.get_half(x)] for x in range(2)]
                A.e.wait_ge(S["c_ready"], 2 * e + 2)
                for k in range(4, KD):
                    for x in range(2):
                        m = mm(ps[64 * x:64 * x + 64, 7, :], m_.AT[:, k, :], w[x][:, k - 4, :],
                               start=False, stop=(k == KD - 1))
                        if k == 4 and x == 1:
                            m.then_inc(S["w_used"], 2)
                m.then_inc(A.mark("o_full"), 1)
                if ctx:
                    A.e.wait_ge(S["ctx_hidden"], 2 * e + 2)
                    for k in range(4, KD):
                        for x in range(2):
                            r = 64 * x + 32 * (k % 2)
                            m = mm(ps[r:r + CAP_C, 5, :], m_.ATC[:, k, :], w[x][:, k - 4, :],
                                   start=False, stop=(k >= KD - 2))
                    m.then_inc(A.mark("ctx_o_full"), 1)
                if e == EB - 1:
                    st.done(A)
                else:
                    st.next()
            end_phase(A)

        def pe_turn(A, m_, e, pair):
            A.e.wait_ge(S["act_out"], 2 * e + pair + 1)
            if e:
                A.e.wait_ge(S["c_ready"], 2 * (e - 1) + pair + 1)
            for k in range(4):
                m = tr(ps[:, 2 + pair, k * P:(k + 1) * P], m_.GU[:, k * P:(k + 1) * P], IDENT)
            m.then_inc(A.mark("turned"), 1)
            if m_.layer == 0:
                A.e.wait_ge(S["ctx_out"], 2 * e + pair + 1)
                if e or pair:
                    A.e.wait_ge(S["ctx_hidden"], 2 * e + pair)
                for k in range(4):
                    m = mm(ps[:, 6, k * 2 * CAP_C:(k + 1) * 2 * CAP_C], m_.GUC[:, k * P:(k + 1) * P], PAIR,
                           start=True, stop=True)
                m.then_inc(A.mark("ctx_turned"), 1)

        def turned_parts(bank, cap):
            x = ps[:, bank, 0:8 * cap].rearrange("p (k u s) -> p k u s", k=4, u=2)
            return x[:, :, 0, :], x[:, :, 1, :]

        def act_moe_d(A, m_, i):
            YE = m_.side(0)[6]

            def copy(e, pair):
                A.e.wait_ge(S["psum_full"], 2 * e + pair + 1)
                if e or pair:
                    A.e.wait_ge(S["turned"], 2 * e + pair)
                act(m_.GU, ps[:, pair, :], ACT.Copy).then_inc(A.mark("act_out"), 1)

            def silu(e, pair):
                A.e.wait_ge(S["turned"], 2 * e + pair + 1)
                if e and pair == 0:
                    A.e.wait_ge(S["o_full"], e)
                act(m_.AT[:, 4 * pair:4 * pair + 4, :], turned_parts(2 + pair, CAP_L)[0], ACT.Silu)\
                    .then_inc(A.mark("b_ready"), 1)
                if m_.layer == 0:
                    A.e.wait_ge(S["ctx_turned"], 2 * e + pair + 1)
                    if e and pair == 0:
                        A.e.wait_ge(S["ctx_o_full"], e)
                    act(m_.ATC[:, 4 * pair:4 * pair + 4, :], turned_parts(6, CAP_C)[0], ACT.Silu)\
                        .then_inc(A.mark("ctx_silu"), 1)

            for e in range(EB):
                copy(e, 0)
                silu(e, 0)
                copy(e, 1)
                silu(e, 1)
                A.e.wait_ge(S["o_full"], e + 1)
                r = 64 * (e % 2)
                for dh in range(2):
                    dst = YE[r:r + 64, bass.ds(i * (EB // 2) + e // 2, 1), dh * 512:(dh + 1) * 512]
                    act(dst.rearrange("p o n -> p (o n)"), ps[64 * dh:64 * dh + 64, 7, :], ACT.Copy)\
                        .then_inc(A.mark("e_ready" if dh else None), 1)
            end_phase(A)

        def dve_moe_d(A, m_, i):
            def tokens(e):
                if e >= 2:
                    A.e.wait_ge(S["psum_full"], 2 * (e - 1))
                    if m_.layer == 0:
                        A.e.wait_ge(S["ctx_full"], 2 * (e - 1))
                src = m_.XE[:, :, bass.ds(i * EB + e, 1), :].rearrange("p k o s -> p k (o s)")
                nc.vector.tensor_copy(m_.XS[e % 2], src).then_inc(A.mark("a_ready"), 1)

            def copy(e, pair):
                A.e.wait_ge(S["ctx_full"], 2 * e + pair + 1)
                if e or pair:
                    A.e.wait_ge(S["ctx_turned"], 2 * e + pair)
                nc.vector.tensor_copy(m_.GUC, ps[:, 4 + pair, :]).then_inc(A.mark("ctx_out"), 1)

            def product(e, pair):
                A.e.wait_ge(S["b_ready"], 2 * e + pair + 1)
                x = m_.AT[:, 4 * pair:4 * pair + 4, :]
                tt(x, x, turned_parts(2 + pair, CAP_L)[1], ALU.mult).then_inc(A.mark("c_ready"), 1)
                if m_.layer == 0:
                    A.e.wait_ge(S["ctx_silu"], 2 * e + pair + 1)
                    x = m_.ATC[:, 4 * pair:4 * pair + 4, :]
                    tt(x, x, turned_parts(6, CAP_C)[1], ALU.mult).then_inc(A.mark("ctx_hidden"), 1)

            tokens(0)
            for e in range(EB):
                for pair in range(2):
                    if m_.layer == 0:
                        copy(e, pair)
                    product(e, pair)
                    if pair == 0 and e + 1 < EB:
                        tokens(e + 1)
                if m_.layer == 0:
                    YC = m_.side(1)[6]
                    r = 32 * (e % 4)
                    A.e.wait_ge(S["ctx_o_full"], e + 1)
                    dst = [YC[r:r + 32, bass.ds(i * (EB // 4) + e // 4, 1), dh * 512:(dh + 1) * 512].rearrange("p o n -> p (o n)")
                           for dh in range(2)]
                    for dh in range(2):
                        nc.vector.tensor_copy(dst[dh], ps[64 * dh:64 * dh + 32, 5, :]).then_inc(A.mark(), 1)
                    A.e.wait_ge(*A.last)
                    for dh in range(2):
                        tt(dst[dh], ps[64 * dh + 32:64 * dh + 64, 5, :], dst[dh], ALU.add)\
                            .then_inc(A.mark("ctx_o_out" if dh else None), 1)
            end_phase(A)

        def pe_moe_e(A, m_):
            j = 0
            for n in m_.sides:
                L, cap, _, _, _, G, YE = m_.side(n)
                npair = 16 * cap // P
                for k in range(KD):
                    if j >= 4:
                        A.e.wait_ge(S["dve_out"], j - 3)
                    for p_ in range(npair):
                        m = mm(ps[:, j % 4, 0:L], YE[:, p_, k * P:(k + 1) * P], G[:, p_, :],
                               start=(p_ == 0), stop=(p_ == npair - 1))
                    m.then_inc(A.mark("psum_full"), 1)
                    j += 1
            end_phase(A)

        def dve_moe_e(A, m_):
            j = 0
            for n in m_.sides:
                L, X, _ = side(n)
                for k in range(KD):
                    A.e.wait_ge(S["psum_full"], j + 1)
                    stt(X[:, k, :], ps[:, j % 4, 0:L], mod(m_.layer, 5, k, n), X[:, k, :], ALU.mult, ALU.add).then_inc(A.mark("dve_out"), 1)
                    j += 1
            end_phase(A)

        wm = Map(AR_)
        QS_, K2_, VS_, PT_, PP_, OS_ = (wm.take(4096), wm.take(4 * 768), wm.take(6 * 256), wm.take(2 * 2560),
                                        wm.take(4 * 640), wm.take(4096))
        AX_, AP_, MK_, RT2_ = wm.take(1024), wm.take(P), wm.take(512), wm.take(1024)
        assert wm.at <= AR_END
        QS, K2, VS = v(QS_, 8, 512), v(K2_, 4, 768), v(VS_, 6, 256)
        PT = [v(PT_ + i * 2560, 5, 4, P) for i in range(2)]
        PW = [v(PP_ + i * 640, 640) for i in range(4)]
        OS = v(OS_, 8, 512)
        AXT, APM = v(AX_, 2, 512), v(AP_, P)
        WMASK = half_words(MK_, 4 * P).rearrange("p (a b) -> p a b", b=P)
        SQW = lambda L: v(PT_, KD, L)
        SWT = [("q", 0, t) for t in range(8)] + [("k", n, t) for n in (0, 1) for t in range(2)] + \
              [("v", 0, t) for t in range(4)] + [("v", 1, t) for t in range(2)]

        def act_sw_a(A):
            e = A.e
            for dst, src in ((v(AX_, 1024), a["k_axial"][:, 0:1024]), (APM, a["k_axial"][:, 1024:1152]),
                             (v(OS_, 512), a["k_masks"])):
                e.dma_start(dst, src).then_inc(S["const_in"], 16)
            for n in (0, 1):
                L = side(n)[0]
                if n:
                    A.e.wait_ge(S["stat"], n)
                act_mod_norm(A, n, SQW(L), v(RT2_ + 512 * n, L), 1, 0, n + 1, bank=7 - n)
            for j, (w, n, t) in enumerate(SWT):
                if j % 2:
                    continue
                A.e.wait_ge(S["psum_full"], j + 1)
                for i, (dst, src, sc) in enumerate(sw_dests(j)):
                    last = i == len(sw_dests(j)) - 1
                    act(dst, src, ACT.Copy, scale=sc).then_inc(A.mark("act_out" if last else None), 1)
            A.e.wait_ge(S["const_in"], 48)
            end_phase(A)

        def sw_dests(j):
            w, n, t = SWT[j]
            L = (T, TC)[n]
            b = ps[:, j % 4, :]
            if w == "q":
                return [(QS[:, t, :], b, 0.125)]
            if w == "v":
                return [(VS[:, (2 + t) if n == 0 else t, :], b[:, 0:256], 1.0)]
            lo = TC if n == 0 else 0
            return [(K2[r:r + 64, 2 * t + s, lo:lo + L], ps[64 * s:64 * s + 64, j % 4, 0:L], 1.0)
                    for s in range(2) for r in (0, 64)]

        def pe_sw_a(A, st):
            pe_norm(A, SQW(T), T, 7, 1)
            for j, (w, n, t) in enumerate(SWT):
                L, _, H = side(n)
                if j in (0, 4, 8):
                    s = st.get()
                if j >= 4:
                    A.e.wait_ge(S["act_out" if j % 2 == 0 else "dve_out"], (j - 4) // 2 + 1)
                if n == 1:
                    A.e.wait_ge(S["h_ready"], 2 * KD)
                for k in range(KD):
                    if j == 0:
                        A.e.wait_ge(S["h_ready"], k + 1)
                    if w == "v":
                        m = mm(ps[:, j % 4, 0:256], H[:, k, t * P:(t + 1) * P], Wc[s][:, k, 256:512],
                               start=(k == 0), stop=(k == KD - 1))
                    else:
                        c = t % 4
                        m = mm(ps[:, j % 4, 0:L], Wc[s][:, k, c * P:(c + 1) * P], H[:, k, :],
                               start=(k == 0), stop=(k == KD - 1))
                    if k == 0 and j in (4, 8):
                        m.then_inc(S["w_used"], 2)
                m.then_inc(A.mark("psum_full"), 1)
                if j == 1:
                    pe_norm(A, SQW(TC), TC, 6, 2)
                for x in roped(j):
                    pe_sw_rope(A, x)
                if j in (3, 7):
                    st.next()
            st.done(A)
            end_phase(A)

        def dve_sw_a(A):
            for n in (0, 1):
                L = side(n)[0]
                if n:
                    A.e.wait_ge(S["stat"], n)
                dve_mod_norm(A, n, SQW(L), v(RT2_ + 512 * n, L), 1, 0, "norm1", n + 1)
            A.e.wait_ge(S["const_in"], 48)
            nc.vector.tensor_copy(half_words(MK_, 4 * P), v(OS_, 512)).then_inc(A.mark(), 1)
            ts(MISC[:, 80:96], gv("sink", 0, 16), -1.0, None, ALU.mult).then_inc(A.mark(), 1)
            for j in range(len(SWT)):
                if j % 2:
                    A.e.wait_ge(S["psum_full"], j + 1)
                    for i, (dst, src, sc) in enumerate(sw_dests(j)):
                        last = i == len(sw_dests(j)) - 1
                        ts(dst, src, sc, None, ALU.mult).then_inc(A.mark("dve_out" if last else None), 1)
                for x in roped(j):
                    dve_sw_rope(A, x)
            end_phase(A)

        SW_ROPE = [QS[:, t, :] for t in range(8)] + [K2[:, g, TC:TC + T] for g in range(4)]

        def pe_sw_rope(A, r):
            src = r if r < 8 else 8 + (r - 8) // 2
            if r == 0:
                A.e.wait_ge(S["const_in"], 48)
            if r >= 2:
                A.e.wait_ge(S["g_ready"], r - 1)
            A.e.wait_ge(S["act_out" if src % 2 == 0 else "dve_out"], src // 2 + 1)
            mm(ps[:, 4 + r % 2, :], APM, SW_ROPE[r], start=True, stop=True).then_inc(A.mark("e_ready"), 1)

        def dve_sw_rope(A, r):
            x = SW_ROPE[r]
            r2 = v(RT2_ + 512 * (r % 2), 512)
            A.e.wait_ge(S["e_ready"], r + 1)
            tt(r2, ps[:, 4 + r % 2, :], AXT[:, 1, :], ALU.mult).then_inc(A.mark("g_ready"), 1)
            tt(x, x, AXT[:, 0, :], ALU.mult).then_inc(A.mark(), 1)
            A.e.wait_ge(*A.last)
            A.e.wait_ge(S["g_ready"], r + 1)
            tt(x, x, r2, ALU.add).then_inc(A.mark(), 1)

        def roped(j):
            return [j - 3] if 3 <= j <= 10 else [j - 4] if 12 <= j <= 15 else []

        SU = [(g, i, r) for g in range(4) for i in range(NQ) for r in range(4)]

        def window(i):
            return list(range(max(0, i - 1), min(NQ, i + 2)))

        def pe_sw_c(A):
            for s in range(len(SU) + LAG):
                if s < len(SU):
                    g, i, r = SU[s]
                    if s >= 2:
                        A.e.wait_ge(S["probs"], s - 1)
                    hd, rr = g * 4 + r, 64 * (r % 2)
                    q = QS[rr:rr + 64, hd // 2, i * P:(i + 1) * P]
                    w = window(i)
                    b = 2 * (s % 2)
                    lo = TC + w[0] * P
                    mm(ps[:, b, 0:TC], q, K2[rr:rr + 64, g, 0:TC], start=True, stop=True)
                    m = mm(ps[:, b, TC:512], q, K2[rr:rr + 64, g, lo:lo + 256], start=True, stop=False)
                    if len(w) == 3:
                        mm(ps[:, b + 1, 0:P], q, K2[rr:rr + 64, g, lo + 256:lo + 384], start=True, stop=False)
                    masked = [(x, 3 if kb < i else 2) for x, kb in enumerate(w) if kb != i]
                    for x, msk in masked:
                        bb, cc = (b, TC + x * P) if x < 2 else (b + 1, 0)
                        m = mm(ps[:, bb, cc:cc + P], IDB, WMASK[:, msk, :], start=False, stop=True)
                    m.then_inc(A.mark("scores"), 1)
                if s >= LAG:
                    u = s - LAG
                    g, i, r = SU[u]
                    nk = 2 + len(window(i))
                    if u >= 2:
                        A.e.wait_ge(S["turned_out"], u - 1)
                    if u:
                        A.e.wait_ge(S["i_ready"], u)
                    A.e.wait_ge(S["weights"], u + 1)
                    for j in range(nk):
                        o = ps[:, 4 + u % 2, j * P:(j + 1) * P] if j < 4 else ps[:, 6, 0:P]
                        m = tr(o, PW[u % 4][:, j * P:(j + 1) * P], IDENT)
                    m.then_inc(A.mark("turned"), 1)
                    if r == 0 and u:
                        pe_sw_pv(A, u // 4 - 1)
            pe_sw_pv(A, len(SU) // 4 - 1)
            end_phase(A)

        def pe_sw_pv(A, gi):
            g, i, _ = SU[4 * gi]
            w = window(i)
            A.e.wait_ge(S["turned_out"], 4 * (gi + 1))
            A.e.wait_ge(S["i_ready"], 4 * (gi + 1))
            if gi >= 2:
                A.e.wait_ge(S["o_out"], gi - 1)
            h = 64 * (gi % 2)
            blocks = [0, 1] + [2 + kb for kb in w]
            for j, kb in enumerate(blocks):
                m = mm(ps[h:h + 64, 7, :], VS[:, kb, g * 64:(g + 1) * 64], PT[gi % 2][:, j, :, :],
                       start=(j == 0), stop=(j == len(blocks) - 1))
            m.then_inc(A.mark("o_full"), 1)

        def act_sw_c(A):
            for s in range(len(SU) + LAG + 1):
                if s < len(SU):
                    g, i, r = SU[s]
                    hd = g * 4 + r
                    wd = (2 + len(window(i))) * P
                    b = 2 * (s % 2)
                    A.e.wait_ge(S["maxima"], s + 1)
                    if s >= 4:
                        A.e.wait_ge(S["turned"], s - 3)
                    nm = MISC[:, 32 + s % 4:33 + s % 4]
                    act(PW[s % 4][:, 0:wd], ps[:, b:b + 2, :].rearrange("p a n -> p (a n)")[:, 0:wd], ACT.Exp,
                               bias=nm, accum_out=MISC[:, 36 + s % 4:37 + s % 4]).then_inc(A.mark(), 1)
                    act(MISC[:, 48 + s % 4:49 + s % 4], gv("sink", hd), ACT.Exp, bias=nm).then_inc(A.mark("probs"), 1)
                if LAG <= s < len(SU) + LAG:
                    u = s - LAG
                    g, i, r = SU[u]
                    gi = u // 4
                    A.e.wait_ge(S["turned"], u + 1)
                    if r == 0 and gi >= 2:
                        A.e.wait_ge(S["o_full"], gi - 1)
                    act(PT[gi % 2][:, 0:4, r, :], ps[:, 4 + u % 2, :].rearrange("p (j q) -> p j q", q=P),
                               ACT.Copy).then_inc(A.mark("turned_out"), 1)
            end_phase(A)

        def dve_sw_c(A):
            def evac_o(gi):
                g, i, _ = SU[4 * gi]
                A.e.wait_ge(S["o_full"], gi + 1)
                h = 64 * (gi % 2)
                src = ps[h:h + 64, 7, :].rearrange("p (a b q) -> p a b q", a=2, b=2)
                for rp in range(2):
                    nc.vector.tensor_copy(OS[64 * rp:64 * rp + 64, 2 * g:2 * g + 2, i * P:(i + 1) * P],
                                                 src[:, :, rp, :]).then_inc(A.mark("o_out" if rp else None), 1)

            for s in range(len(SU) + LAG + 2):
                if s < len(SU):
                    g, i, r = SU[s]
                    wd = (2 + len(window(i))) * P
                    b = 2 * (s % 2)
                    nm = MISC[:, 32 + s % 4:33 + s % 4]
                    A.e.wait_ge(S["scores"], s + 1)
                    nc.vector.tensor_reduce(nm, ps[:, b:b + 2, :].rearrange("p a n -> p (a n)")[:, 0:wd], AX_X,
                                                   ALU.max, negate=True).then_inc(A.mark(), 1)
                    A.e.wait_ge(*A.last)
                    tt(nm, nm, MISC[:, 80 + g * 4 + r:81 + g * 4 + r], ALU.min).then_inc(A.mark("maxima"), 1)
                if 1 <= s <= len(SU):
                    u = s - 1
                    wd = (2 + len(window(SU[u][1]))) * P
                    A.e.wait_ge(S["probs"], u + 1)
                    sm, es = MISC[:, 36 + u % 4:37 + u % 4], MISC[:, 48 + u % 4:49 + u % 4]
                    tt(sm, sm, es, ALU.add).then_inc(A.mark(), 1)
                    A.e.wait_ge(*A.last)
                    nc.vector.reciprocal(sm, sm).then_inc(A.mark(), 1)
                    A.e.wait_ge(*A.last)
                    ts(PW[u % 4][:, 0:wd], PW[u % 4][:, 0:wd], sm, None, ALU.mult).then_inc(A.mark("weights"), 1)
                if LAG <= s < len(SU) + LAG:
                    u = s - LAG
                    g, i, r = SU[u]
                    gi = u // 4
                    A.e.wait_ge(S["turned"], u + 1)
                    if r == 0 and gi >= 2:
                        A.e.wait_ge(S["o_full"], gi - 1)
                    if len(window(i)) == 3:
                        ins = nc.vector.tensor_copy(PT[gi % 2][:, 4, r, :], ps[:, 6, 0:P])
                    else:
                        ins = nc.vector.memset(MISC[:, 5:6], 0.0)
                    ins.then_inc(A.mark("i_ready"), 1)
                if s >= LAG + 4 and (s - LAG) % 4 == 1 and (s - LAG) // 4 - 1 < len(SU) // 4 - 1:
                    evac_o((s - LAG) // 4 - 1)
            evac_o(len(SU) // 4 - 1)
            end_phase(A)

        def act_final(A):
            act_norm(A, XT, v(AR_, KD, T), v(AR_ + 4096, T), T, 7, 1)
            for k in range(0, KD, 2):
                A.e.wait_ge(S["a_ready"], k + 2)
                A.e.dma_start(out[:, k:k + 2, :], HTL[:, k:k + 2, :]).then_inc(S["stored"], 16)
            A.e.wait_ge(S["stored"], 16 * KD // 2)

        def dve_final(A):
            dve_squares(A, XT, v(AR_, KD, T))
            dve_recip(A, v(AR_ + 4096, T), 1)
            for k in range(KD):
                stt(HTL[:, k, :], XT[:, k, :], gv("final", k), v(AR_ + 4096, T), ALU.mult, ALU.mult)\
                    .then_inc(A.mark("a_ready"), 1)

        HYENAS = [Hy(0), Hy(1)]
        MOES = [Moe(0), Moe(1)]
        H_PHASES = 3
        TURNS = N_EXP // EB

        @block.sync
        def _(sp):
            st = Stream(sp)

            def experts(layer):
                with sp.Fori(0, TURNS) as i:
                    st.enter(i, 12 * EB)
                    for e in range(EB):
                        g, u, dn = (a[n][layer][bass.ds(i * EB + e, 1)].rearrange("o r n -> (o r) n")
                                    for n in ("moe_w_gate_2", "moe_w_up_2", "moe_w_down_2"))
                        for x, y in ((cols(g, 0), cols(u, 0)), (cols(g, 1), cols(u, 1)), (cols(dn, 0), cols(dn, 1))):
                            for k in (0, 4):
                                st.load_half(Wh, x[:, k:k + 4, :])
                                st.load_half(Wh, y[:, k:k + 4, :])
                st.leave(TURNS)

            with sp.Fori(0, DEPTH) as l:
                st.enter(l, N_HYB)
                wi = a["w_in"][bass.ds(l, 1)].rearrange("o r n -> (o r) n")
                wo = a["w_out"][bass.ds(l, 1)].rearrange("o r n -> (o r) n")
                wa = a["ada_w_2"][bass.ds(l, 1)].rearrange("o r n -> (o r) n")
                for c in range(12):
                    st.load(cols(wi, c))
                    st.load(cols(wa, c))
                for c in range(3):
                    src = wo[c * 512:(c + 1) * 512, :].rearrange("(k p) n -> p k n", p=P)
                    st.load_half(Wr2, src[:, 0:2, :])
                    st.load_half(Wr2, src[:, 2:4, :])
            st.leave(DEPTH)
            for _y in HYENAS:
                for c in range(6):
                    st.load(cols(a["hy_w_in_2"], c))
                for c in range(2):
                    st.load(cols(a["hy_w_out_2"], c))
            experts(0)
            for c in range(3):
                st.load(cols(a["sw_w_in_2"], c))
            for c in range(2):
                st.load(cols(a["sw_w_out_2"], c))
            experts(1)

        @block.tensor
        def _(e):
            A = Engine(e, "pe", S)
            st = Stream(e)
            e.sem_inc(S["w_used"], WSLOTS)

            def moe(m_):
                pe_moe_a(A, m_)
                pe_moe_b(A, m_)
                pe_moe_c(A, m_)
                with e.Fori(0, TURNS) as i:
                    A.loop = (i, 1)
                    st.enter(i, 12 * EB)
                    pe_moe_d(A, m_, st)
                A.leave(TURNS)
                st.leave(TURNS)
                pe_moe_e(A, m_)

            A.e.wait_ge(S["a_ready"], 2)
            pe_next_stat(A, 0)
            end_phase(A)
            with e.Fori(0, DEPTH) as l:
                A.loop = (l, H_PHASES)
                st.enter(l, N_HYB)
                pe_hyb_proj(A, st)
                pe_attn(A)
                pe_hyb_out(A, st)
            A.leave(DEPTH)
            st.leave(DEPTH)
            end_phase(A)
            for y in HYENAS:
                pe_hy_a(A, y, st)
                for c in range(2):
                    for o in range(2):
                        pe_hy_b(A, y, c, o)
                pe_proj_out(A, st, y.U3, y.L)
            moe(MOES[0])
            pe_sw_a(A, st)
            pe_sw_c(A)
            pe_proj_out(A, st, OS, T)
            moe(MOES[1])
            pe_norm(A, v(AR_, KD, T), T, 7, 1)

        @block.scalar
        def _(e):
            A = Engine(e, "act", S)

            def moe(m_):
                act_moe_a(A, m_)
                act_moe_b(A, m_)
                act_moe_c(A, m_)
                with e.Fori(0, TURNS) as i:
                    A.loop = (i, 1)
                    act_moe_d(A, m_, i)
                A.leave(TURNS)
                end_phase(A)

            act_setup(A)
            with e.Fori(0, DEPTH) as l:
                A.loop = (l, H_PHASES)
                act_hyb_proj(A, l)
                act_attn(A)
                act_hyb_out(A)
            A.leave(DEPTH)
            e.dma_start(CT, a["ctx"]).then_inc(S["const_in"], 16)
            e.wait_ge(S["const_in"], 16)
            end_phase(A)
            for y in HYENAS:
                act_hy_a(A, y)
                for c in range(2):
                    for o in range(2):
                        act_hy_b(A, y, c, o)
                end_phase(A)
            moe(MOES[0])
            act_sw_a(A)
            act_sw_c(A)
            end_phase(A)
            moe(MOES[1])
            act_final(A)

        @block.vector
        def _(e):
            A = Engine(e, "dve", S)

            def moe(m_):
                dve_moe_a(A, m_)
                dve_moe_b(A, m_)
                dve_moe_c(A, m_)
                with e.Fori(0, TURNS) as i:
                    A.loop = (i, 1)
                    dve_moe_d(A, m_, i)
                A.leave(TURNS)
                dve_moe_e(A, m_)

            dve_setup(A)
            with e.Fori(0, DEPTH) as l:
                A.loop = (l, H_PHASES)
                dve_hyb_proj(A, l)
                dve_attn(A)
                dve_hyb_out(A)
            A.leave(DEPTH)
            end_phase(A)
            for y in HYENAS:
                dve_hy_a(A, y)
                for c in range(2):
                    for o in range(2):
                        dve_hy_b(A, y, c, o)
                dve_proj_out(A, y.n, v(T_, y.L), 0, "hy_b_out")
            moe(MOES[0])
            dve_sw_a(A)
            dve_sw_c(A)
            dve_proj_out(A, 0, None, 1, None)
            moe(MOES[1])
            dve_final(A)

        @block.gpsimd
        def _(e):
            A = Engine(e, "pool", S)
            open_next_phase(A)
            with e.Fori(0, DEPTH) as l:
                for _p in range(H_PHASES):
                    open_next_phase(A)
            for _p in range(1 + 2 * (1 + 4 + 1)):
                open_next_phase(A)
            for layer in range(2):
                for _p in range(3):
                    open_next_phase(A)
                with e.Fori(0, TURNS) as i:
                    open_next_phase(A)
                open_next_phase(A)
                if layer == 0:
                    for _p in range(3):
                        open_next_phase(A)


def pack_vectors(inp):
    f = lambda x: np.asarray(x, np.float32)
    col = lambda x: f(x).reshape(-1, P).T

    def short(x):
        x = f(x)
        o = np.zeros((P, x.shape[-1]), np.float32)
        o[:x.shape[0]] = x
        return o

    lvs = []
    for l in range(DEPTH):
        li = 0.8 - 0.6 * math.exp(-0.3 * l)
        parts = {
            "g_pre": col(inp["pre_norm"][l]), "g_post": col(inp["post_norm"][l]), "subln": col(inp["diff_subln"][l]),
            "lam_vec": short(f(inp["diff_lambda"][l]).T), "f_bias": short(f(inp["forget_bias"][l])[:, None]),
            "lam_init": np.full((P, 1), li, np.float32), "one_minus": np.full((P, 1), 1.0 - li, np.float32),
            "ada_b": col(inp["ada_b_2"][l]),
        }
        lvs.append(np.concatenate([parts[n] for n in LAYER_COLS], axis=1))
    cc = np.stack([col(inp["c_2"][0]), col(inp["c_ctx_2"])], axis=2).reshape(P, -1)
    pick = np.zeros((P, 2), np.float32)
    for side in range(2):
        pick[side::32, side] = 1
    one0 = np.zeros((P, 1), np.float32)
    one0[0] = 1
    dft = lambda L: np.concatenate([np.where(one0 > 0, 1.0, 2.0) / (2 * L), np.full((P, 1), 2.0) / (2 * L)], axis=1)
    g = {
        "c": cc, "pick": pick,
        "norm1": np.concatenate([col(inp["norm1_w_2"][l]) for l in range(2)], axis=1),
        "norm2": np.concatenate([col(inp["norm2_w_2"][l]) for l in range(2)], axis=1),
        "final": col(inp["final_norm_w_2"]), "hy_b_in": col(inp["hy_b_in_2"]),
        "hy_sw": np.concatenate([col(inp["hy_short_w_2"][i]) for i in range(3)], axis=1),
        "hy_sb": col(inp["hy_short_b_2"]), "hy_b_out": col(inp["hy_b_out_2"]),
        "ffn_b1": short(f(inp["hy_ffn_b1_2"])[:, None]), "ffn_b2": short(f(inp["hy_ffn_b2_2"])[:, None]),
        "freq": short(f(inp["hy_sin_freq_2"]).T), "sink": np.broadcast_to(f(inp["sw_sink_2"])[None], (P, 16)),
        "not0": 1 - one0, "is0": one0, "dft_l": dft(T), "dft_c": dft(TC),
    }
    gvec = np.concatenate([g[n] for n in GLOBAL_COLS], axis=1)
    return (np.ascontiguousarray(gvec, dtype=np.float32),
            np.ascontiguousarray(np.concatenate(lvs, axis=1), dtype=np.float32))


WEIGHTS = ["w_in", "w_out", "ada_w_2", "hy_w_in_2", "hy_ffn_w1_2", "hy_ffn_w2_2", "hy_ffn_w3_2", "hy_filter_bias_2",
           "hy_w_out_2", "sw_w_in_2", "sw_w_out_2", "moe_router_2", "moe_w_gate_2", "moe_w_up_2", "moe_w_down_2"]


def transposed(x):
    return np.ascontiguousarray(np.asarray(x, np.float32).T.reshape(KD, P, -1).transpose(1, 0, 2))


def prepare(inputs):
    gvec, lvec = pack_vectors(inputs)
    arrays = {n: np.ascontiguousarray(np.asarray(inputs[n])) for n in WEIGHTS}
    arrays["w_out"] = np.ascontiguousarray(np.roll(arrays["w_out"], -512, axis=1))
    arrays["x"] = transposed(inputs["x"][0])
    arrays["ctx"] = transposed(inputs["ctx_2"][0])
    arrays["k_gvec"], arrays["k_lvec"] = gvec, lvec
    for n, x in shape_constants().items():
        arrays["k_" + n] = np.ascontiguousarray(x)
    return arrays


def kernel(**inputs):
    import concourse.bacc as bacc
    from concourse.bass_utils import run_bass_kernel_spmd

    arrays = prepare(inputs)
    nc = bacc.Bacc("TRN2", target_bir_lowering=False, num_devices=1)
    aps = {n: nc.dram_tensor("in_" + n, x.shape, F32, kind="ExternalInput").ap() for n, x in arrays.items()}
    out = nc.dram_tensor("out_x", (P, KD, T), F32, kind="ExternalOutput").ap()
    build(nc, aps, out)
    r = run_bass_kernel_spmd(nc, [{"in_" + n: x for n, x in arrays.items()}], core_ids=[0])
    o = np.asarray(r.results[0]["out_x"])
    return np.ascontiguousarray(o.transpose(2, 1, 0).reshape(1, T, D))
```
